# Optimizing a Trainium2 kernel written in Bass

```python
import math
import jax, jax.numpy as jnp
from jax import lax
import numpy as np

D_MODEL = 1024
BATCH = 1
SEQ = 256
DEPTH = 2

RMS_EPS = 1e-6
Q_BLOCK = 128

MLA_HEADS = 4
MLA_NOPE = 64
MLA_ROPE = 32
MLA_V = 64
MLA_Q_LORA = 256
MLA_KV_LORA = 128
MLA_WIDTH = MLA_HEADS * MLA_V
ROPE_THETA = 10000.0

GDN_HEADS = 4
GDN_DK = 128
GDN_DV = 128
GDN_CONV = 4
GDN_CHUNK = 64
GDN_WIDTH = GDN_HEADS * GDN_DV

MOBA_HEADS = 4
MOBA_DH = 64
MOBA_BLOCK = 256
MOBA_TOPK = 3
MOBA_WIDTH = MOBA_HEADS * MOBA_DH

T5_BUCKETS = 32
T5_MAX_DIST = 2048

MIX_WIDTH = MLA_WIDTH + GDN_WIDTH + MOBA_WIDTH

IN_SIZES = (
    MLA_Q_LORA, MLA_KV_LORA, MLA_ROPE, MLA_WIDTH,
    GDN_HEADS * GDN_DK, GDN_HEADS * GDN_DK, GDN_WIDTH, GDN_WIDTH,
    GDN_HEADS, GDN_HEADS,
    MOBA_WIDTH, MOBA_WIDTH, MOBA_WIDTH, MOBA_WIDTH,
)
IN_COLS = sum(IN_SIZES)


def rmsnorm(x, w):
    xf = x.astype(jnp.float32)
    y = xf * lax.rsqrt(jnp.mean(xf * xf, axis=-1, keepdims=True) + RMS_EPS)
    return (y * w.astype(jnp.float32)).astype(x.dtype)

def l2norm(x):
    xf = x.astype(jnp.float32)
    return xf * lax.rsqrt(jnp.sum(xf * xf, axis=-1, keepdims=True) + 1e-6)

def rope_tables(seq, dim):
    inv = 1.0 / (ROPE_THETA ** (jnp.arange(0, dim, 2, dtype=jnp.float32) / dim))
    ang = jnp.arange(seq, dtype=jnp.float32)[:, None] * inv[None, :]
    return jnp.cos(ang), jnp.sin(ang)

def apply_rope(x, cos, sin):
    half = x.shape[-1] // 2
    xf = x.astype(jnp.float32)
    x1, x2 = xf[..., :half], xf[..., half:]
    c, s = cos[None, :, None, :], sin[None, :, None, :]
    return jnp.concatenate([x1 * c - x2 * s, x1 * s + x2 * c], axis=-1).astype(x.dtype)

def t5_bucket(rel):
    n = jnp.maximum(rel, 0)
    max_exact = T5_BUCKETS // 2
    nf = jnp.maximum(n, 1).astype(jnp.float32)
    large = max_exact + (jnp.log(nf / max_exact) / math.log(T5_MAX_DIST / max_exact)
                         * (T5_BUCKETS - max_exact)).astype(jnp.int32)
    large = jnp.minimum(large, T5_BUCKETS - 1)
    return jnp.where(n < max_exact, n, large)

def causal_block_attention(q, k, v, scale):
    B, S, H, Dk = q.shape
    Dv = v.shape[-1]
    nqb = S // Q_BLOCK
    qb = q.reshape(B, nqb, Q_BLOCK, H, Dk).transpose(1, 0, 2, 3, 4)
    kpos = jnp.arange(S)

    def one(args):
        i, qi = args
        logits = jnp.einsum('bqhd,bkhd->bhqk', qi, k, preferred_element_type=jnp.float32) * scale
        qpos = i * Q_BLOCK + jnp.arange(Q_BLOCK)
        logits = jnp.where(kpos[None, :] <= qpos[:, None], logits, -jnp.inf)
        p = jax.nn.softmax(logits, axis=-1).astype(v.dtype)
        return jnp.einsum('bhqk,bkhd->bqhd', p, v)

    out = lax.map(one, (jnp.arange(nqb), qb))
    return out.transpose(1, 0, 2, 3, 4).reshape(B, S, H, Dv)

def mla_mixer(c_q, c_kv, k_rope, q_norm_w, w_uq, kv_norm_w, w_ukv, cos, sin):
    B, S, _ = c_q.shape
    q = (rmsnorm(c_q, q_norm_w) @ w_uq).reshape(B, S, MLA_HEADS, MLA_NOPE + MLA_ROPE)
    q_nope, q_pe = q[..., :MLA_NOPE], q[..., MLA_NOPE:]
    q_pe = apply_rope(q_pe, cos, sin)
    kv = (rmsnorm(c_kv, kv_norm_w) @ w_ukv).reshape(B, S, MLA_HEADS, MLA_NOPE + MLA_V)
    k_nope, v = kv[..., :MLA_NOPE], kv[..., MLA_NOPE:]
    k_pe = apply_rope(k_rope[:, :, None, :], cos, sin)
    k = jnp.concatenate([k_nope, jnp.broadcast_to(k_pe, (B, S, MLA_HEADS, MLA_ROPE))], axis=-1)
    qh = jnp.concatenate([q_nope, q_pe], axis=-1)
    o = causal_block_attention(qh, k, v, (MLA_NOPE + MLA_ROPE) ** -0.5)
    return o.reshape(B, S, MLA_WIDTH)

def causal_conv(x, w):
    K = w.shape[0]
    S = x.shape[1]
    xp = jnp.pad(x, ((0, 0), (K - 1, 0), (0, 0)))
    return sum(xp[:, j:j + S] * w[j] for j in range(K))

def chunk_gated_delta_rule(q, k, v, beta, g):
    B, S, H, DK = q.shape
    DV = v.shape[-1]
    C = GDN_CHUNK
    N = S // C

    def chunks(t):
        return t.reshape(B, N, C, H, t.shape[-1]).transpose(0, 3, 1, 2, 4)

    qc, kc, vc = chunks(q), chunks(k), chunks(v)
    bc = beta.reshape(B, N, C, H).transpose(0, 3, 1, 2)
    gc = jnp.cumsum(g.reshape(B, N, C, H).transpose(0, 3, 1, 2), axis=-1)

    idx = jnp.arange(C)
    strict = idx[:, None] > idx[None, :]
    incl = idx[:, None] >= idx[None, :]
    diff = gc[..., :, None] - gc[..., None, :]
    decay = jnp.exp(jnp.where(incl, diff, -jnp.inf))

    kk = jnp.einsum('bhntd,bhnjd->bhntj', kc, kc)
    L = jnp.where(strict, bc[..., :, None] * kk * decay, 0.0)
    rhs = jnp.concatenate([kc * (bc * jnp.exp(gc))[..., None], vc * bc[..., None]], axis=-1)
    sol = lax.linalg.triangular_solve(L + jnp.eye(C, dtype=L.dtype), rhs,
                                      left_side=True, lower=True, unit_diagonal=True)
    W, U0 = sol[..., :DK], sol[..., DK:]
    A_qk = jnp.einsum('bhntd,bhnjd->bhntj', qc, kc) * decay
    q_g = qc * jnp.exp(gc)[..., None]
    k_end = kc * jnp.exp(gc[..., -1:] - gc)[..., None]
    g_end = jnp.exp(gc[..., -1])

    def step(state, xs):
        W_n, U0_n, A_n, qg_n, ke_n, ge_n = xs
        U = U0_n - jnp.einsum('bhcd,bhde->bhce', W_n, state)
        o = jnp.einsum('bhcd,bhde->bhce', qg_n, state) + jnp.einsum('bhtj,bhje->bhte', A_n, U)
        new_state = ge_n[..., None, None] * state + jnp.einsum('bhcd,bhce->bhde', ke_n, U)
        return new_state, o

    xs = tuple(jnp.moveaxis(t, 2, 0) for t in (W, U0, A_qk, q_g, k_end, g_end))
    s0 = jnp.zeros((B, H, DK, DV), jnp.float32)
    _, o = lax.scan(step, s0, xs)
    return o.transpose(1, 0, 3, 2, 4).reshape(B, S, H, DV)

def gdn_mixer(q, k, v, z, b, a, conv_w, A_log, dt_bias, norm_w):
    B, S, _ = q.shape
    qkv = jax.nn.silu(causal_conv(jnp.concatenate([q, k, v], axis=-1), conv_w))
    nk = GDN_HEADS * GDN_DK
    q, k, v = qkv[..., :nk], qkv[..., nk:2 * nk], qkv[..., 2 * nk:]
    q = l2norm(q.reshape(B, S, GDN_HEADS, GDN_DK)) * (GDN_DK ** -0.5)
    k = l2norm(k.reshape(B, S, GDN_HEADS, GDN_DK))
    v = v.reshape(B, S, GDN_HEADS, GDN_DV).astype(jnp.float32)
    beta = jax.nn.sigmoid(b.astype(jnp.float32))
    g = -jnp.exp(A_log.astype(jnp.float32)) * jax.nn.softplus(
        a.astype(jnp.float32) + dt_bias.astype(jnp.float32))
    o = chunk_gated_delta_rule(q, k, v, beta, g).astype(z.dtype)
    o = rmsnorm(o, norm_w) * jax.nn.silu(z.reshape(B, S, GDN_HEADS, GDN_DV))
    return o.reshape(B, S, GDN_WIDTH)

def moba_mixer(q, k, v, t5_table):
    B, S, _ = q.shape
    H, Dh, BS = MOBA_HEADS, MOBA_DH, MOBA_BLOCK
    q = q.reshape(B, S, H, Dh).transpose(0, 2, 1, 3)
    k = k.reshape(B, S, H, Dh).transpose(0, 2, 1, 3)
    v = v.reshape(B, S, H, Dh).transpose(0, 2, 1, 3)
    NB = -(-S // BS)
    pad = NB * BS - S
    kp = jnp.pad(k, ((0, 0), (0, 0), (0, pad), (0, 0)))
    vp = jnp.pad(v, ((0, 0), (0, 0), (0, pad), (0, 0)))
    kblk = kp.reshape(B, H, NB, BS, Dh)
    vblk = vp.reshape(B, H, NB, BS, Dh)
    kmean = jnp.mean(kblk.astype(jnp.float32), axis=3).astype(k.dtype)
    topk = min(MOBA_TOPK, NB)
    scale = Dh ** -0.5
    nqb = S // Q_BLOCK
    qb = jnp.moveaxis(q.reshape(B, H, nqb, Q_BLOCK, Dh), 2, 0)
    bi = jnp.arange(B)[:, None, None, None]
    hi = jnp.arange(H)[None, :, None, None]
    hi5 = jnp.arange(H)[None, :, None, None, None]
    blk_iota = jnp.arange(BS)

    def one(args):
        i, qi = args
        qpos = i * Q_BLOCK + jnp.arange(Q_BLOCK)
        own = (i * Q_BLOCK) // BS
        gate = jnp.einsum('bhqd,bhnd->bhqn', qi, kmean, preferred_element_type=jnp.float32)
        gate = jnp.where(jnp.arange(NB) < own, gate, -jnp.inf)
        _, sel = lax.top_k(gate, topk)
        valid = sel < own
        ksel = kblk[bi, hi, sel]
        vsel = vblk[bi, hi, sel]
        kpos_sel = sel[..., None] * BS + blk_iota
        bias_sel = t5_table[t5_bucket(qpos[None, None, :, None, None] - kpos_sel), hi5]
        l_sel = jnp.einsum('bhqd,bhqnkd->bhqnk', qi, ksel, preferred_element_type=jnp.float32) * scale
        l_sel = jnp.where(valid[..., None], l_sel + bias_sel.astype(jnp.float32), -jnp.inf)
        kown = lax.dynamic_slice_in_dim(kp, own * BS, BS, axis=2)
        vown = lax.dynamic_slice_in_dim(vp, own * BS, BS, axis=2)
        kpos_own = own * BS + blk_iota
        rel_own = qpos[:, None] - kpos_own[None, :]
        bias_own = t5_table[t5_bucket(rel_own)].transpose(2, 0, 1)[None]
        l_own = jnp.einsum('bhqd,bhkd->bhqk', qi, kown, preferred_element_type=jnp.float32) * scale
        l_own = jnp.where(rel_own[None, None] >= 0, l_own + bias_own.astype(jnp.float32), -jnp.inf)
        logits = jnp.concatenate([l_sel.reshape(B, H, Q_BLOCK, topk * BS), l_own], axis=-1)
        p = jax.nn.softmax(logits, axis=-1).astype(v.dtype)
        p_sel = p[..., :topk * BS].reshape(B, H, Q_BLOCK, topk, BS)
        p_own = p[..., topk * BS:]
        return (jnp.einsum('bhqnk,bhqnkd->bhqd', p_sel, vsel)
                + jnp.einsum('bhqk,bhkd->bhqd', p_own, vown))

    out = lax.map(one, (jnp.arange(nqb), qb))
    out = out.transpose(1, 2, 0, 3, 4).reshape(B, H, S, Dh)
    return out.transpose(0, 2, 1, 3).reshape(B, S, MOBA_WIDTH)

def hybrid_layer(x, norm_w, w_in, mla_q_norm, mla_w_uq, mla_kv_norm, mla_w_ukv,
                 gdn_conv_w, gdn_A_log, gdn_dt_bias, gdn_norm_w, w_out, t5_table, cos, sin):
    h = rmsnorm(x, norm_w)
    proj = h @ w_in
    split_points = np.cumsum(IN_SIZES)[:-1].tolist()
    (m_cq, m_ckv, m_kr, m_gate, g_q, g_k, g_v, g_z, g_b, g_a,
     c_q, c_k, c_v, c_gate) = jnp.split(proj, split_points, axis=-1)
    y_mla = mla_mixer(m_cq, m_ckv, m_kr, mla_q_norm, mla_w_uq, mla_kv_norm, mla_w_ukv,
                      cos, sin) * jax.nn.silu(m_gate)
    y_gdn = gdn_mixer(g_q, g_k, g_v, g_z, g_b, g_a, gdn_conv_w, gdn_A_log, gdn_dt_bias, gdn_norm_w)
    y_moba = moba_mixer(c_q, c_k, c_v, t5_table) * jax.nn.silu(c_gate)
    y = jnp.concatenate([y_mla, y_gdn, y_moba], axis=-1)
    return x + y @ w_out

def first_inputs(seed: int = 0) -> dict:
    key = jax.random.key(seed)
    ks = jax.random.split(key, 20)
    nrm = jax.random.normal
    f32 = jnp.float32
    dt = jnp.exp(jax.random.uniform(ks[10], (DEPTH, GDN_HEADS), f32, math.log(1e-3), math.log(1e-1)))
    return {
        "x": nrm(ks[0], (BATCH, SEQ, D_MODEL), f32),
        "norm_w": 1.0 + 0.02 * nrm(ks[1], (DEPTH, D_MODEL), f32),
        "w_in": nrm(ks[2], (DEPTH, D_MODEL, IN_COLS), f32) * D_MODEL ** -0.5,
        "mla_q_norm": 1.0 + 0.02 * nrm(ks[3], (DEPTH, MLA_Q_LORA), f32),
        "mla_w_uq": nrm(ks[4], (DEPTH, MLA_Q_LORA, MLA_HEADS * (MLA_NOPE + MLA_ROPE)), f32) * MLA_Q_LORA ** -0.5,
        "mla_kv_norm": 1.0 + 0.02 * nrm(ks[5], (DEPTH, MLA_KV_LORA), f32),
        "mla_w_ukv": nrm(ks[6], (DEPTH, MLA_KV_LORA, MLA_HEADS * (MLA_NOPE + MLA_V)), f32) * MLA_KV_LORA ** -0.5,
        "gdn_conv_w": nrm(ks[7], (DEPTH, GDN_CONV, 2 * GDN_HEADS * GDN_DK + GDN_WIDTH), f32) * GDN_CONV ** -0.5,
        "gdn_A_log": jnp.log(jax.random.uniform(ks[8], (DEPTH, GDN_HEADS), f32, 1.0, 16.0)),
        "gdn_dt_bias": jnp.log(jnp.expm1(dt)),
        "gdn_norm_w": 1.0 + 0.02 * nrm(ks[9], (DEPTH, GDN_DV), f32),
        "w_out": nrm(ks[11], (DEPTH, MIX_WIDTH, D_MODEL), f32) * (MIX_WIDTH * 2 * DEPTH) ** -0.5,
        "t5_table": 0.5 * nrm(ks[12], (T5_BUCKETS, MOBA_HEADS), f32),
        "final_norm_w": 1.0 + 0.02 * nrm(ks[13], (D_MODEL,), f32),
    }

def first_block(x, norm_w, w_in, mla_q_norm, mla_w_uq, mla_kv_norm, mla_w_ukv,
              gdn_conv_w, gdn_A_log, gdn_dt_bias, gdn_norm_w, w_out, t5_table, final_norm_w):
    S = x.shape[1]
    cos, sin = rope_tables(S, MLA_ROPE)
    for l in range(DEPTH):
        x = hybrid_layer(x, norm_w[l], w_in[l], mla_q_norm[l], mla_w_uq[l], mla_kv_norm[l],
                         mla_w_ukv[l], gdn_conv_w[l], gdn_A_log[l], gdn_dt_bias[l],
                         gdn_norm_w[l], w_out[l], t5_table, cos, sin)
    return rmsnorm(x, final_norm_w)


DEPTH_2 = 4

N_MIXERS = 3
PLE_DIM = 256
D_FF = 2816
EPS = 1e-6
HG_HEADS = 8
HG_DK = D_MODEL // HG_HEADS
HG_DV = D_MODEL // HG_HEADS
HG_CHUNK = 64
ML_HEADS = 4
ML_DQK = D_MODEL // 2 // ML_HEADS
ML_DV = D_MODEL // ML_HEADS
ML_CHUNK = 64
ML_GATE_CAP = 15.0
SW_HEADS = 16
SW_KV_HEADS = 4
SW_GROUP = SW_HEADS // SW_KV_HEADS
SW_HD = 64
WINDOW = 128
SW_BLOCK = 128
N_A = (DEPTH_2 + 2) // 3
N_B = (DEPTH_2 + 1) // 3
N_C = DEPTH_2 // 3


def rmsnorm_2(x, gain):
    xf = x.astype(jnp.float32)
    y = xf * lax.rsqrt(jnp.mean(xf * xf, axis=-1, keepdims=True) + EPS)
    return (y * gain.astype(jnp.float32)).astype(x.dtype)

def swiglu(x, w_gu, w_down):
    g, u = jnp.split(x @ w_gu, 2, axis=-1)
    return (jax.nn.silu(g) * u) @ w_down

def to_chunks(t, L):
    B, T, H, d = t.shape
    return t.reshape(B, T // L, L, H, d).transpose(1, 0, 3, 2, 4)

def from_chunks(t):
    N, B, H, L, d = t.shape
    return t.transpose(1, 0, 3, 2, 4).reshape(B, N * L, H, d)

def gate_chunks(t, L):
    B, T, H = t.shape
    return t.reshape(B, T // L, L, H).transpose(1, 0, 3, 2)

def alibi_slopes(n_heads):
    return jnp.asarray([2.0 ** (-8.0 * (h + 1) / n_heads) for h in range(n_heads)], jnp.float32)

def hgrn2_mixer(x, lb, w_in, g_norm, w_out):
    B, T, _ = x.shape
    q, f, i, og = jnp.split(x @ w_in, 4, axis=-1)
    q = jax.nn.silu(q).astype(jnp.float32)
    f = f.astype(jnp.float32)
    lb = lb.astype(jnp.float32)
    log_f = jnp.logaddexp(jnp.log(lb), jnp.log1p(-lb) + jax.nn.log_sigmoid(f))
    k = (1.0 - lb) * jax.nn.sigmoid(-f)
    L = HG_CHUNK
    qc = to_chunks(q.reshape(B, T, HG_HEADS, HG_DK), L)
    kc = to_chunks(k.reshape(B, T, HG_HEADS, HG_DK), L)
    gc = to_chunks(log_f.reshape(B, T, HG_HEADS, HG_DK), L)
    vc = to_chunks(i.astype(jnp.float32).reshape(B, T, HG_HEADS, HG_DV), L)
    causal = jnp.tril(jnp.ones((L, L), bool))

    def step(S, inp):
        q_, k_, v_, g_ = inp
        b = jnp.cumsum(g_, axis=2)
        o_inter = jnp.einsum('bhtk,bhkv->bhtv', q_ * jnp.exp(b), S)
        diff = b[:, :, :, None, :] - b[:, :, None, :, :]
        decay = jnp.exp(jnp.where(causal[:, :, None], diff, -jnp.inf))
        A = jnp.einsum('bhtk,bhsk,bhtsk->bhts', q_, k_, decay)
        o_intra = jnp.einsum('bhts,bhsv->bhtv', A, v_)
        b_last = b[:, :, -1:, :]
        S_new = jnp.exp(b_last[:, :, 0, :])[..., None] * S + jnp.einsum(
            'bhsk,bhsv->bhkv', k_ * jnp.exp(b_last - b), v_)
        return S_new, o_inter + o_intra

    S0 = jnp.zeros((B, HG_HEADS, HG_DK, HG_DV), jnp.float32)
    _, o = lax.scan(step, S0, (qc, kc, vc, gc))
    o = rmsnorm_2(from_chunks(o), g_norm)
    o = o.reshape(B, T, D_MODEL).astype(x.dtype) * jax.nn.silu(og)
    return o @ w_out

def mlstm_mixer(x, w_qkvo, w_if, b_if, norm_g, w_out):
    B, T, _ = x.shape
    dqk_all = ML_HEADS * ML_DQK
    q, k, v, og = jnp.split(x @ w_qkvo, [dqk_all, 2 * dqk_all, 2 * dqk_all + D_MODEL], axis=-1)
    gates = (x @ w_if).astype(jnp.float32) + b_if.astype(jnp.float32)
    gates = ML_GATE_CAP * jnp.tanh(gates / ML_GATE_CAP)
    ig, fg = jnp.split(gates, 2, axis=-1)
    lf = jax.nn.log_sigmoid(fg)
    L = ML_CHUNK
    qc = to_chunks(q.astype(jnp.float32).reshape(B, T, ML_HEADS, ML_DQK), L)
    kc = to_chunks(k.astype(jnp.float32).reshape(B, T, ML_HEADS, ML_DQK), L) * (ML_DQK ** -0.5)
    vc = to_chunks(v.astype(jnp.float32).reshape(B, T, ML_HEADS, ML_DV), L)
    ic = gate_chunks(ig, L)
    fc = gate_chunks(lf, L)
    causal = jnp.tril(jnp.ones((L, L), bool))

    def step(carry, inp):
        C, n, m = carry
        q_, k_, v_, i_, f_ = inp
        b = jnp.cumsum(f_, axis=-1)
        log_intra = jnp.where(causal, b[..., :, None] - b[..., None, :] + i_[..., None, :], -jnp.inf)
        log_inter = b + m[..., None]
        m_t = jnp.maximum(jnp.max(log_intra, axis=-1), log_inter)
        w_intra = jnp.exp(log_intra - m_t[..., None])
        w_inter = jnp.exp(log_inter - m_t)
        scores = jnp.einsum('bhtk,bhsk->bhts', q_, k_) * w_intra
        num = w_inter[..., None] * jnp.einsum('bhtk,bhkv->bhtv', q_, C) + jnp.einsum('bhts,bhsv->bhtv', scores, v_)
        den = w_inter * jnp.einsum('bhtk,bhk->bht', q_, n) + jnp.sum(scores, axis=-1)
        h = num / jnp.maximum(jnp.abs(den), jnp.exp(-m_t))[..., None]
        b_L = b[..., -1]
        log_state = b_L + m
        log_src = b_L[..., None] - b + i_
        m_new = jnp.maximum(log_state, jnp.max(log_src, axis=-1))
        w_src = jnp.exp(log_src - m_new[..., None])
        decay = jnp.exp(log_state - m_new)
        C_new = decay[..., None, None] * C + jnp.einsum('bhsk,bhsv->bhkv', k_ * w_src[..., None], v_)
        n_new = decay[..., None] * n + jnp.einsum('bhs,bhsk->bhk', w_src, k_)
        return (C_new, n_new, m_new), h

    carry0 = (jnp.zeros((B, ML_HEADS, ML_DQK, ML_DV), jnp.float32),
              jnp.zeros((B, ML_HEADS, ML_DQK), jnp.float32),
              jnp.zeros((B, ML_HEADS), jnp.float32))
    _, h = lax.scan(step, carry0, (qc, kc, vc, ic, fc))
    h = rmsnorm_2(from_chunks(h), norm_g.reshape(ML_HEADS, ML_DV))
    h = h.reshape(B, T, D_MODEL).astype(x.dtype) * jax.nn.sigmoid(og)
    return h @ w_out

def swa_mixer(x, w_qkv, q_gain, k_gain, sinks, w_o):
    B, T, _ = x.shape
    nq = SW_HEADS * SW_HD
    nk = SW_KV_HEADS * SW_HD
    q, k, v = jnp.split(x @ w_qkv, [nq, nq + nk], axis=-1)
    q = rmsnorm_2(q.reshape(B, T, SW_HEADS, SW_HD), q_gain)
    k = rmsnorm_2(k.reshape(B, T, SW_KV_HEADS, SW_HD), k_gain)
    v = v.reshape(B, T, SW_KV_HEADS, SW_HD)
    nb = T // SW_BLOCK
    qb = q.reshape(B, nb, SW_BLOCK, SW_KV_HEADS, SW_GROUP, SW_HD)

    def band(t):
        tb = t.reshape(B, nb, SW_BLOCK, SW_KV_HEADS, SW_HD)
        prev = jnp.pad(tb, ((0, 0), (1, 0), (0, 0), (0, 0), (0, 0)))[:, :-1]
        return jnp.concatenate([prev, tb], axis=2)

    kk, vv = band(k), band(v)
    s = jnp.einsum('bnqkgd,bnskd->bnkgqs', qb, kk).astype(jnp.float32) * (SW_HD ** -0.5)
    qpos = jnp.arange(SW_BLOCK)
    kpos = jnp.arange(2 * SW_BLOCK) - SW_BLOCK
    dist = (qpos[:, None] - kpos[None, :]).astype(jnp.float32)
    blk_start = jnp.arange(nb) * SW_BLOCK
    valid = (dist >= 0) & (dist < WINDOW) & ((blk_start[:, None, None] + kpos[None, None, :]) >= 0)
    slopes = alibi_slopes(SW_HEADS).reshape(SW_KV_HEADS, SW_GROUP)
    s = s - slopes[:, :, None, None] * dist
    s = jnp.where(valid[None, :, None, None], s, -jnp.inf)
    sink = jnp.broadcast_to(sinks.astype(jnp.float32).reshape(SW_KV_HEADS, SW_GROUP)[:, :, None, None],
                            s.shape[:-1] + (1,))
    probs = jax.nn.softmax(jnp.concatenate([s, sink], axis=-1), axis=-1)[..., :-1]
    o = jnp.einsum('bnkgqs,bnskd->bnqkgd', probs.astype(vv.dtype), vv).reshape(B, T, nq)
    return o @ w_o

def second_inputs(seed: int = 0) -> dict:
    key = jax.random.key(seed)
    ks = jax.random.split(key, 24)
    f32 = jnp.float32

    def nrm(k, shape, fan_in):
        return jax.random.normal(k, shape, f32) * (fan_in ** -0.5)

    D = D_MODEL
    b_if = jnp.concatenate([
        0.1 * jax.random.normal(ks[11], (N_B, ML_HEADS), f32),
        jnp.linspace(3.0, 6.0, ML_HEADS, dtype=f32)[None, :] + 0.1 * jax.random.normal(ks[12], (N_B, ML_HEADS), f32),
    ], axis=-1)
    return {
        "x": jax.random.normal(ks[0], (BATCH, SEQ, D), f32),
        "p": jax.random.normal(ks[1], (DEPTH_2, BATCH, SEQ, PLE_DIM), f32),
        "norm_gains": 1.0 + 0.02 * jax.random.normal(ks[2], (DEPTH_2, 4, D), f32),
        "w_ffn_gu": nrm(ks[3], (DEPTH_2, 2, D, 2 * D_FF), D),
        "w_ffn_down": nrm(ks[4], (DEPTH_2, 2, D_FF, D), D_FF),
        "w_ple_gate": nrm(ks[5], (DEPTH_2, D, D), D),
        "w_ple_proj": nrm(ks[6], (DEPTH_2, PLE_DIM, D), PLE_DIM),
        "hg_lower_bounds": 0.5 * jax.random.normal(ks[7], (DEPTH_2, D), f32),
        "hg_w_in": nrm(ks[8], (N_A, D, 4 * D), D),
        "hg_g_norm": 1.0 + 0.02 * jax.random.normal(ks[9], (N_A, HG_DV), f32),
        "hg_w_out": nrm(ks[10], (N_A, D, D), D),
        "ml_w_qkvo": nrm(ks[13], (N_B, D, 2 * ML_HEADS * ML_DQK + 2 * D), D),
        "ml_w_if": nrm(ks[14], (N_B, D, 2 * ML_HEADS), D),
        "ml_b_if": b_if,
        "ml_norm": 1.0 + 0.02 * jax.random.normal(ks[15], (N_B, D), f32),
        "ml_w_out": nrm(ks[16], (N_B, D, D), D),
        "sw_w_qkv": nrm(ks[17], (N_C, D, (SW_HEADS + 2 * SW_KV_HEADS) * SW_HD), D),
        "sw_q_norm": 1.0 + 0.02 * jax.random.normal(ks[18], (N_C, SW_HD), f32),
        "sw_k_norm": 1.0 + 0.02 * jax.random.normal(ks[19], (N_C, SW_HD), f32),
        "sw_sinks": 0.5 * jax.random.normal(ks[20], (N_C, SW_HEADS), f32),
        "sw_w_o": nrm(ks[21], (N_C, SW_HEADS * SW_HD, D), SW_HEADS * SW_HD),
    }

def second_block(x, p, norm_gains, w_ffn_gu, w_ffn_down, w_ple_gate, w_ple_proj,
              hg_lower_bounds, hg_w_in, hg_g_norm, hg_w_out,
              ml_w_qkvo, ml_w_if, ml_b_if, ml_norm, ml_w_out,
              sw_w_qkv, sw_q_norm, sw_k_norm, sw_sinks, sw_w_o):
    lbs = jnp.cumsum(jax.nn.softmax(hg_lower_bounds.astype(jnp.float32), axis=0), axis=0)
    lbs = lbs - lbs[0:1]
    for layer in range(DEPTH_2):
        g = norm_gains[layer]
        h = x + 0.5 * swiglu(rmsnorm_2(x, g[0]), w_ffn_gu[layer, 0], w_ffn_down[layer, 0])
        xn = rmsnorm_2(h, g[1])
        kind = layer % N_MIXERS
        j = layer // N_MIXERS
        if kind == 0:
            mix = hgrn2_mixer(xn, lbs[layer], hg_w_in[j], hg_g_norm[j], hg_w_out[j])
        elif kind == 1:
            mix = mlstm_mixer(xn, ml_w_qkvo[j], ml_w_if[j], ml_b_if[j], ml_norm[j], ml_w_out[j])
        else:
            mix = swa_mixer(xn, sw_w_qkv[j], sw_q_norm[j], sw_k_norm[j], sw_sinks[j], sw_w_o[j])
        h = h + mix
        h = h + 0.5 * swiglu(rmsnorm_2(h, g[2]), w_ffn_gu[layer, 1], w_ffn_down[layer, 1])
        gate = jax.nn.sigmoid(rmsnorm_2(h, g[3]) @ w_ple_gate[layer])
        x = h + gate * (p[layer] @ w_ple_proj[layer])
    return x


def setup_inputs(seed=0):
    out = dict(first_inputs(seed))
    for name, value in second_inputs(seed + 1).items():
        if name != "x":
            out[name + "_2"] = value
    return out


def reference(
    x, norm_w, w_in, mla_q_norm, mla_w_uq, mla_kv_norm, mla_w_ukv, gdn_conv_w, gdn_A_log,
    gdn_dt_bias, gdn_norm_w, w_out, t5_table, final_norm_w, p_2, norm_gains_2, w_ffn_gu_2,
    w_ffn_down_2, w_ple_gate_2, w_ple_proj_2, hg_lower_bounds_2, hg_w_in_2, hg_g_norm_2,
    hg_w_out_2, ml_w_qkvo_2, ml_w_if_2, ml_b_if_2, ml_norm_2, ml_w_out_2, sw_w_qkv_2,
    sw_q_norm_2, sw_k_norm_2, sw_sinks_2, sw_w_o_2,
):
    x = first_block(
        x, norm_w, w_in, mla_q_norm, mla_w_uq, mla_kv_norm, mla_w_ukv, gdn_conv_w, gdn_A_log,
        gdn_dt_bias, gdn_norm_w, w_out, t5_table, final_norm_w,
    )
    return second_block(
        x, p_2, norm_gains_2, w_ffn_gu_2, w_ffn_down_2, w_ple_gate_2, w_ple_proj_2,
        hg_lower_bounds_2, hg_w_in_2, hg_g_norm_2, hg_w_out_2, ml_w_qkvo_2, ml_w_if_2,
        ml_b_if_2, ml_norm_2, ml_w_out_2, sw_w_qkv_2, sw_q_norm_2, sw_k_norm_2, sw_sinks_2,
        sw_w_o_2,
    )


_drawn_inputs = setup_inputs


def setup_inputs(seed=0):
    import zlib

    import numpy as np

    out = dict(_drawn_inputs(seed))
    spreads = {}
    factors = {'norm_w': 3.719,
     'mla_q_norm': 8.0,
     'mla_kv_norm': 8.0,
     'gdn_norm_w': 6.54,
     'hg_lower_bounds_2': 2.766,
     'hg_g_norm_2': 4.325,
     'ml_norm_2': 7.71,
     'sw_q_norm_2': 8.0,
     'sw_k_norm_2': 8.0,
     'sw_sinks_2': 178.112}
    for name, (base, spread) in spreads.items():
        noise = np.random.default_rng([zlib.crc32(name.encode()), seed]).standard_normal(out[name].shape)
        drawn = base * np.exp(spread * noise) if base else spread * noise
        out[name] = __import__('jax').numpy.asarray(drawn.astype(out[name].dtype))
    for name, factor in factors.items():
        out[name] = (out[name] * factor).astype(out[name].dtype)
    return out
```

```python
import numpy as np
from contextlib import ExitStack

import concourse.bass as bass
from concourse import mybir

F32 = mybir.dt.float32
F32R = mybir.dt.float32r
ALU = mybir.AluOpType
ACT = mybir.ActivationFunctionType
AX = mybir.AxisListType

P = 128
S = 256
TT = S // P
D = 1024
KD = D // P
FF = 2816
FT = FF // P
CH = 1024
NS = 6
AHEAD = NS - 1
EPS = 1e-6
ARENA = 17900


class Signal:

    def __init__(self, k, name):
        self.sem = k.ctx.enter_context(k.nc.semaphore(name))
        self.n = 0

    def up(self):
        self.n += 1
        return self.sem, 1

    def up_dma(self):
        self.n += 16
        return self.sem, 16

    def made(self, back=0):
        return self.sem, max(self.n - back, 0)

    def at(self, value):
        return self.sem, value


class Kernel:

    def __init__(self, nc, ctx, n_chunks):
        self.nc, self.ctx = nc, ctx
        self.n_chunks = n_chunks
        self.used = 0
        self.hi_split = 0
        self.lo_split = 0
        self.signals = {}

    def sb(self, name, shape, dt=F32):
        return self.ctx.enter_context(self.nc.sbuf_tensor(name, shape, dt))

    def __call__(self, name):
        if name not in self.signals:
            self.signals[name] = Signal(self, name)
        return self.signals[name]

    def load(self, sp, c, i=0):
        s = c % NS
        if c >= NS:
            sp.wait_ge(self.w_lo_ready.sem, c - NS + 1 + i * NS)
        sp.dma_start(self.w_raw[:, s, :], self.w_dram[c + i * NS, :, :]).then_inc(self.w_loaded[s].sem, 16)

    def hi(self, act, c, i=0):
        if c >= self.n_chunks:
            return
        s = c % NS
        act.wait_ge(self.w_loaded[s].sem, 16 * (c // NS + 1) + i * 16)
        if c >= NS:
            act.wait_ge(self.chunk_done.sem, c - NS + 1 + i * NS)
        act.activation(self.w_hi[:, s, :], self.w_raw[:, s, :], ACT.Copy).then_inc(self.w_hi_ready.sem, 1)

    def lo(self, dve, c, i=0):
        if c >= self.n_chunks:
            return
        s = c % NS
        dve.wait_ge(self.w_hi_ready.sem, c + 1 + i * NS)
        dve.tensor_tensor(self.w_lo[:, s, :], self.w_raw[:, s, :], self.w_hi[:, s, :], ALU.subtract)\
           .then_inc(self.w_lo_ready.sem, 1)

    def hi_for(self, act, c):
        self.hi(act, c + AHEAD)

    def lo_for(self, dve, c):
        self.lo(dve, c + AHEAD)

    def wait_chunk(self, pe, c, i=0):
        pe.wait_ge(self.w_lo_ready.sem, c + 1 + i * NS)

    def products(self, pe, out, s, j0, width, rhs_hi, rhs_lo, first, last, start=None):
        w_hi, w_lo = self.w_hi[:, s, j0:j0 + width], self.w_lo[:, s, j0:j0 + width]
        start = first if start is None else start
        pe.matmul(out, w_hi, rhs_hi, start=start, stop=False, skip_group_check=True)
        pe.matmul(out, w_hi, rhs_lo, start=False, stop=False, skip_group_check=True)
        return pe.matmul(out, w_lo, rhs_hi, start=False, stop=last, skip_group_check=True)

    def rows(self, pe, out, s, j0, width, lhs_hi, lhs_lo, first, last, start=None):
        w_hi, w_lo = self.w_hi[:, s, j0:j0 + width], self.w_lo[:, s, j0:j0 + width]
        start = first if start is None else start
        pe.matmul(out, lhs_hi, w_hi, start=start, stop=False, skip_group_check=True)
        pe.matmul(out, lhs_hi, w_lo, start=False, stop=False, skip_group_check=True)
        return pe.matmul(out, lhs_lo, w_hi, start=False, stop=last, skip_group_check=True)


class Arena:

    def __init__(self, buf, size):
        self.buf, self.size = buf, size
        self.clear()

    def clear(self):
        self.at, self.parts = 0, {}

    def __call__(self, name, width):
        if name not in self.parts:
            assert self.at + width <= self.size, (name, self.at + width)
            self.parts[name] = self.buf[:, self.at:self.at + width]
            self.at += width
        return self.parts[name]


def norm(k, gain, to_x=False):
    block = k.block
    xr, sq, ssq, ready = k("x_ready"), k("square_ready"), k("sum_sq_ready"), k("xn_ready")
    xh, xl, rstd_ready = k("xn_hi_ready"), k("xn_lo_ready"), k("rstd_ready")
    x0 = xr.n - KD // 2
    x, xn = k.x, k.xn
    s0, r0, h0 = sq.n, ready.n, xh.n

    @block.scalar
    def _(act):
        act.wait_ge(*xl.made())
        for j in range(KD // 2):
            act.wait_ge(*xr.at(x0 + j + 1))
            act.activation(xn[:, 2 * j:2 * j + 2, :], x[:, 2 * j:2 * j + 2, :], ACT.Square).then_inc(*sq.up())

    @block.tensor
    def _(pe):
        pe.wait_ge(*k("misc_free").made())
        for j in range(KD // 2):
            pe.wait_ge(*sq.at(s0 + j + 1))
            for m in (2 * j, 2 * j + 1):
                mm = pe.matmul(k.ps_sum[:, 0:S], k.ones[:, :], xn[:, m, :], start=(m == 0), stop=(m == KD - 1))
        mm.then_inc(*ssq.up())

    @block.vector
    def _(dve):
        dve.wait_ge(*ssq.made())
        dve.tensor_scalar(k.rstd[:, :], k.ps_sum[:, 0:S], 1.0 / D, EPS, ALU.mult, ALU.add).then_inc(*rstd_ready.up())
        dve.wait_ge(*rstd_ready.made())
        dve.reciprocal(k.rstd[:, :], k.rstd[:, :]).then_inc(*rstd_ready.up())

    @block.scalar
    def _(act):
        act.wait_ge(*rstd_ready.made())
        act.activation(k.rstd[:, :], k.rstd[:, :], ACT.Sqrt).then_inc(*rstd_ready.up())

    if to_x:
        @block.vector
        def _(dve):
            dve.wait_ge(*rstd_ready.made())
            for m in range(KD):
                ins = dve.scalar_tensor_tensor(out=x[:, m, :], in0=x[:, m, :], scalar=gain[:, m:m + 1],
                                               in1=k.rstd[:, :], op0=ALU.mult, op1=ALU.mult)
                if m % 2:
                    ins.then_inc(*xr.up())
        return

    @block.vector
    def _(dve):
        dve.wait_ge(*rstd_ready.made())
        for m in range(KD):
            ins = dve.scalar_tensor_tensor(out=xn[:, m, :], in0=x[:, m, :], scalar=gain[:, m:m + 1],
                                           in1=k.rstd[:, :], op0=ALU.mult, op1=ALU.mult)
            if m % 2:
                ins.then_inc(*ready.up())

    @block.scalar
    def _(act):
        act.wait_ge(*k.chunk_done.at(k.used))
        for j in range(KD // 2):
            act.wait_ge(*ready.at(r0 + j + 1))
            act.activation(k.xn_hi[:, 2 * j:2 * j + 2, :], xn[:, 2 * j:2 * j + 2, :], ACT.Copy).then_inc(*xh.up())

    @block.gpsimd
    def _(pool):
        for j in range(KD // 2):
            pool.wait_ge(*xh.at(h0 + j + 1))
            pool.tensor_tensor(k.xn_lo[:, 2 * j:2 * j + 2, :], xn[:, 2 * j:2 * j + 2, :],
                               k.xn_hi[:, 2 * j:2 * j + 2, :], ALU.subtract).then_inc(*xl.up())


def ffn(k):
    block = k.block
    c0 = k.used
    silu, hr, hh, hl = k("silu_ready"), k("h_ready"), k("h_hi_ready"), k("h_lo_ready")
    b0 = silu.n
    xl0 = k("xn_lo_ready").n - KD // 2
    LOOPS = (FT - 4) // 2

    def at_g(t):
        return c0 if t == 0 else c0 + 3 * t - 1

    def tiles(eng, tile, last):
        for t in range(3):
            tile(t, 0)
        with eng.Fori(0, LOOPS) as i:
            tile(3, i)
            tile(4, i)
        tile(FT - 1, 0)
        last()

    def part(a, b, t):
        return a[:, t % 2, :]

    @block.tensor
    def _(pe):
        def down(t, c, i):
            pe.wait_ge(*hl.at(b0 + t + 1 + 2 * i))
            k.wait_chunk(pe, c, i)
            for m in range(KD):
                mm = k.products(pe, k.ps_acc[:, m // 2, (m % 2) * S:(m % 2 + 1) * S], c % NS, m * P, P,
                                k.h_hi[:, t % 2, :], k.h_lo[:, t % 2, :], False, t == FT - 1,
                                start=(t == 0 and m % 2 == 0))
            mm.then_inc(k.chunk_done.sem, 1)

        def tile(t, i):
            if t >= 2:
                pe.wait_ge(*hr.at(b0 + t - 1 + 2 * i))
            for n, c in enumerate((at_g(t), at_g(t) + 1)):
                k.wait_chunk(pe, c, i)
                for j in range(KD):
                    if t == 0 and n == 0 and j % 2 == 0:
                        pe.wait_ge(*k("xn_lo_ready").at(xl0 + j // 2 + 1))
                    mm = k.products(pe, k.ps_gu[t % 2][:, n * S:(n + 1) * S], c % NS, j * P, P,
                                    k.xn_hi[:, j, :], k.xn_lo[:, j, :], False, j == KD - 1,
                                    start=(n == 0 and j == 0))
                mm.then_inc(k.chunk_done.sem, 1)
            if t >= 1:
                down(t - 1, at_g(t) + 2, i)

        tiles(pe, tile, lambda: down(FT - 1, c0 + 3 * FT - 1, 0))

    @block.scalar
    def _(act):
        def tile(t, i):
            g = at_g(t)
            k.hi(act, g + AHEAD, i)
            k.hi(act, g + 1 + AHEAD, i)
            act.wait_ge(k.chunk_done.sem, g + 2 + i * NS)
            if t >= 2:
                act.wait_ge(*hr.at(b0 + t - 1 + 2 * i))
            act.activation(k.s[:, t % 2, :], k.ps_gu[t % 2][:, 0:S], ACT.Silu).then_inc(silu.sem, 1)
            if t >= 1:
                k.hi(act, g + 2 + AHEAD, i)
            act.wait_ge(*hr.at(b0 + t + 1 + 2 * i))
            act.activation(k.h_hi[:, t % 2, :], k.h[:, t % 2, :], ACT.Copy).then_inc(hh.sem, 1)

        tiles(act, tile, lambda: k.hi(act, c0 + 3 * FT - 1 + AHEAD))

    @block.vector
    def _(dve):
        def tile(t, i):
            g = at_g(t)
            k.lo(dve, g + AHEAD, i)
            k.lo(dve, g + 1 + AHEAD, i)
            dve.wait_ge(*silu.at(b0 + t + 1 + 2 * i))
            if t >= 2:
                dve.wait_ge(*hl.at(b0 + t - 1 + 2 * i))
            dve.tensor_tensor(k.h[:, t % 2, :], k.s[:, t % 2, :], k.ps_gu[t % 2][:, S:2 * S], ALU.mult)\
               .then_inc(hr.sem, 1)
            if t >= 1:
                k.lo(dve, g + 2 + AHEAD, i)
            dve.wait_ge(*hh.at(b0 + t + 1 + 2 * i))
            dve.tensor_tensor(k.h_lo[:, t % 2, :], k.h[:, t % 2, :], k.h_hi[:, t % 2, :], ALU.subtract)\
               .then_inc(hl.sem, 1)

        tiles(dve, tile, lambda: k.lo(dve, c0 + 3 * FT - 1 + AHEAD))

    for s in (silu, hr, hh, hl):
        s.n += FT
    k.used += 3 * FT
    residual(k, 0.5)


def residual(k, scale):
    xr = k("x_ready")

    @k.block.vector
    def _(dve):
        dve.wait_ge(*k.chunk_done.at(k.used))
        dve.wait_ge(*k("xn_ready").made())
        for j in range(KD // 2):
            dve.scalar_tensor_tensor(out=k.x[:, 2 * j:2 * j + 2, :], in0=k.ps_acc[:, j, :].rearrange("p (m t) -> p m t", m=2),
                                     scalar=scale, in1=k.x[:, 2 * j:2 * j + 2, :],
                                     op0=ALU.mult, op1=ALU.add).then_inc(*xr.up())


def ple(k, layer):
    block = k.block
    c0 = k.used
    xr, ph, pl = k("x_ready"), k("p_hi_ready"), k("p_lo_ready")
    gate, prod = k("ple_gate_ready"), k("ple_gated")
    g0, r0 = gate.n, prod.n

    xl0 = k("xn_lo_ready").n - KD // 2
    p_hi, p_lo = k.h_hi[:, 0:2, :], k.h_lo[:, 0:2, :]

    @block.gpsimd
    def _(pool):
        pool.wait_ge(*k("p_loaded").made())
        pool.wait_ge(*k.chunk_done.at(c0))
        pool.tensor_copy(p_hi[:, :, :], k.p_all[:, layer, :, :]).then_inc(*ph.up())
        pool.wait_ge(*ph.made())
        pool.tensor_tensor(p_lo[:, :, :], k.p_all[:, layer, :, :], p_hi[:, :, :], ALU.subtract).then_inc(*pl.up())

    @block.tensor
    def _(pe):
        pe.wait_ge(*pl.made())
        pe.wait_ge(*xr.made())
        for j in range(2):
            k.wait_chunk(pe, c0 + j)
            for m in range(KD):
                mm = k.products(pe, k.ps_acc[:, m // 2, (m % 2) * S:(m % 2 + 1) * S], (c0 + j) % NS, m * P, P,
                                p_hi[:, j, :], p_lo[:, j, :], False, j == 1, start=(j == 0 and m % 2 == 0))
            mm.then_inc(k.chunk_done.sem, 1)
        for m in range(KD):
            c = c0 + 2 + m
            k.wait_chunk(pe, c)
            if m < 2:
                pe.wait_ge(*prod.at(r0))
            else:
                pe.wait_ge(*gate.at(g0 + m - 1))
            for j in range(KD):
                if m == 0 and j % 2 == 0:
                    pe.wait_ge(*k("xn_lo_ready").at(xl0 + j // 2 + 1))
                mm = k.products(pe, k.ps_gu[m % 2][:, 0:S], c % NS, j * P, P,
                                k.xn_hi[:, j, :], k.xn_lo[:, j, :], j == 0, j == KD - 1)
            mm.then_inc(k.chunk_done.sem, 1)

    @block.scalar
    def _(act):
        for j in range(2):
            k.hi(act, c0 + j + AHEAD)
        for m in range(KD):
            c = c0 + 2 + m
            k.hi(act, c + AHEAD)
            act.wait_ge(k.chunk_done.sem, c + 1)
            if m >= 2:
                act.wait_ge(*prod.at(r0 + m - 1))
            act.activation(k.s[:, m % 2, :], k.ps_gu[m % 2][:, 0:S], ACT.Sigmoid).then_inc(*gate.up())

    @block.vector
    def _(dve):
        for j in range(2):
            k.lo(dve, c0 + j + AHEAD)
        for m in range(KD):
            k.lo(dve, c0 + 2 + m + AHEAD)
            dve.wait_ge(*gate.at(g0 + m + 1))
            dve.wait_ge(*k("h_hi_ready").made())
            dve.tensor_tensor(k.h[:, m % 2, :], k.s[:, m % 2, :],
                              k.ps_acc[:, m // 2, (m % 2) * S:(m % 2 + 1) * S], ALU.mult).then_inc(*prod.up())
            dve.wait_ge(*prod.made())
            ins = dve.tensor_tensor(k.x[:, m, :], k.x[:, m, :], k.h[:, m % 2, :], ALU.add)
            if m % 2:
                ins.then_inc(*xr.up())
    k.used += 2 + KD


def load_p(k, io):
    @k.block.scalar
    def _(act):
        act.wait_ge(*k("logits_ready").made())
        act.dma_start(k.p_all[:, :, :, :], io["p"]).then_inc(*k("p_loaded").up_dma())


def setup(nc, ctx, io, n_chunks, n_vec, n_const=1):
    k = Kernel(nc, ctx, n_chunks)
    k.w_dram = io["w"]
    k.w_raw = k.sb("w_raw", [P, NS, CH])
    k.w_hi = k.sb("w_hi", [P, NS, CH], F32R)
    k.w_lo = k.sb("w_lo", [P, NS, CH], F32R)
    k.x = k.sb("x_res", [P, KD, S])
    k.xn = k.sb("xn", [P, KD, S])
    k.xn_hi = k.sb("xn_hi", [P, KD, S], F32R)
    k.xn_lo = k.sb("xn_lo", [P, KD, S], F32R)
    k.rstd = k.sb("rstd", [P, S])
    k.s = k.sb("silu", [P, 2, S])
    k.h = k.sb("h", [P, 2, S])
    k.h_hi = k.sb("h_hi", [P, 3, S], F32R)
    k.h_lo = k.sb("h_lo", [P, 3, S], F32R)
    k.lat_hi, k.lat_lo = k.h_hi, k.h_lo
    k.vec = k.sb("vec", [P, n_vec])
    k.ones = k.sb("ones", [P, P])
    k.p_all = k.sb("p_all", [P, 4, 2, S])
    k.t5b = k.p_all[:, :, :, :].rearrange("p a b t -> p (a b) t").rearrange("p (q h) t -> p q h t", q=2)
    k.const = k.sb("const", [P, n_const])
    k.t5 = k.sb("t5", [33, 4])
    k.ba = k.sb("ba", [P, 16])
    k.tiny = k.sb("tiny", [P, 16])
    k.lbw = k.sb("bounds", [P, 8 * KD])
    k.arena = Arena(k.sb("arena", [P, ARENA]), ARENA)
    k.bank = 0
    ps = [ctx.enter_context(nc.psum_tensor(f"ps_gu{i}", [P, 2 * S], F32)) for i in range(2)]
    k.ps_gu = ps
    k.ps_acc = ctx.enter_context(nc.psum_tensor("ps_acc", [P, 4, 2 * S], F32))
    k.ps_sum = ctx.enter_context(nc.psum_tensor("ps_sum", [P, 2 * S], F32))
    k.ps_misc = ctx.enter_context(nc.psum_tensor("ps_misc", [P, 2 * S], F32))
    k.w_loaded = [k(f"w_loaded{s}") for s in range(NS)]
    k.w_hi_ready, k.w_lo_ready, k.chunk_done = k("w_hi_ready"), k("w_lo_ready"), k("chunk_done")
    k.gu_read = [k("product_read_act").made()] * 2
    k.block = ctx.enter_context(nc.Block())
    return k


def start(k, io):
    block = k.block
    n = k.n_chunks

    @block.sync
    def _(sp):
        for c in range(NS):
            k.load(sp, c)
        with sp.Fori(0, n // NS - 1) as i:
            for c in range(NS, 2 * NS):
                k.load(sp, c, i)
        for c in range(n // NS * NS, n):
            k.load(sp, c)

    ins = k("inputs_loaded")

    @block.scalar
    def _(act):
        act.dma_start(k.x[:, :, :], io["x"]).then_inc(*ins.up_dma())
        act.dma_start(k.vec[:, :], io["vec"]).then_inc(*ins.up_dma())
        act.dma_start(k.const[:, :], io["const"]).then_inc(*ins.up_dma())
        act.dma_start(k.t5[0:32, :], io["t5"]).then_inc(*ins.up_dma())

    @block.gpsimd
    def _(pool):
        pool.memset(k.ones[:, :], 1.0).then_inc(*k("constants_ready").up())

    @block.vector
    def _(dve):
        dve.wait_ge(*ins.made())
        dve.wait_ge(*k("constants_ready").made())
        dve.memset(k.t5[32:33, :], 1.0).then_inc(*k("constants_ready").up())
        for j in range(KD // 2):
            dve.tensor_copy(k.rstd[:, j:j + 1], k.x[:, 2 * j, 0:1]).then_inc(*k("x_ready").up())

    @block.scalar
    def _(act):
        act.wait_ge(*ins.made())
        for c in range(AHEAD):
            k.hi(act, c)

    @block.vector
    def _(dve):
        for c in range(AHEAD):
            k.lo(dve, c)

    @block.tensor
    def _(pe):
        pe.wait_ge(*k("constants_ready").made())


CONSTS = {}
_parts = []


def _const(name, a):
    a = np.asarray(a, np.float32)
    if a.shape[0] < P:
        a = np.concatenate([a, np.zeros((P - a.shape[0], a.shape[1]), np.float32)])
    at = sum(p.shape[1] for p in _parts)
    CONSTS[name] = (at, at + a.shape[1])
    _parts.append(a)


_r = np.arange(P)
LEVELS = 7
_const("ident", np.eye(P))
_const("upper", _r[:, None] <= _r[None, :])
_const("levels", np.concatenate([(_r[:, None] // (2 * s) == _r[None, :] // (2 * s)) & (_r[:, None] // s % 2 == 0)
                                 & (_r[None, :] // s % 2 == 1) for s in (1 << n for n in range(LEVELS))], 1))
OFF = -1e30
_const("causal", np.concatenate([np.zeros((P, P)), np.where(_r[None, :] <= _r[:, None], 0.0, OFF)], 1))


def _rope():
    inv = (1.0 / (np.float32(10000.0) ** (np.arange(0, 32, 2, dtype=np.float32) / np.float32(32)))).astype(np.float32)
    ang = (np.arange(S, dtype=np.float32)[:, None] * inv[None, :]).astype(np.float32)
    cos, sin = np.cos(ang).T, np.sin(ang).T
    t = np.zeros((P, S), np.float32)
    t[64:96] = np.concatenate([cos, cos])
    t[96:128] = np.concatenate([-sin, sin])
    return t


_const("rope", _rope())


def _t5():
    rel = np.maximum(255 - np.arange(2 * S), 0)
    f = np.float32
    large = 16 + (np.log(np.maximum(rel, 1).astype(f) / f(16)) / f(np.log(2048 / 16)) * f(16)).astype(np.int32)
    bucket = np.where(rel < 16, rel, np.minimum(large, 31))
    hot = np.zeros((33, 2 * S), np.float32)
    hot[bucket, np.arange(2 * S)] = 255 - np.arange(2 * S) >= 0
    hot[32] = np.where(255 - np.arange(2 * S) >= 0, 0.0, OFF)
    return hot


_const("t5_hot", _t5())
_const("halves", _r[:, None] // 64 == _r[None, :] // 64)
_d = _r[:, None] - _r[None, :]
_const("distance", np.concatenate([np.where(_d + P < P, _d + P, -OFF), np.where(_d >= 0, _d, -OFF)], 1))
N_CONST_1 = sum(p.shape[1] for p in _parts)


def constants():
    return np.ascontiguousarray(np.concatenate(_parts, 1))


def con(k, name, a=0, b=None):
    lo, hi = CONSTS[name]
    return k.const[:, lo + a:hi if b is None else lo + b]


def tools(k):
    return k.block, (lambda name: k(name).made()), (lambda name: k(name).up())


def project(k, tiles, x_hi, x_lo, kt=KD, first=None):
    block, made, up = tools(k)
    c0 = k.used
    read = {}

    def out(t):
        return k.ps_gu[(k.bank + t) % 2]

    def reads(engine, eng, split):
        for t, (who, rows, width, work) in enumerate(tiles):
            split(eng, c0 + t)
            if who == engine:
                eng.wait_ge(*k.chunk_done.at(c0 + t + 1))
                work(eng, out(t)).then_inc(*up("product_read_" + engine))
                read[t] = k("product_read_" + engine).made()

    @block.scalar
    def _(act):
        reads("act", act, k.hi_for)

    @block.vector
    def _(dve):
        reads("dve", dve, k.lo_for)

    @block.tensor
    def _(pe):
        for t, (who, rows, width, work) in enumerate(tiles):
            c = c0 + t
            k.wait_chunk(pe, c)
            pe.wait_ge(*(read[t - 2] if t >= 2 else k.gu_read[(k.bank + t) % 2]))
            for j in range(kt):
                if t == 0 and first is not None and j in first:
                    pe.wait_ge(*first[j])
                if rows:
                    for tt in range(2):
                        mm = k.rows(pe, out(t)[:, tt * P:tt * P + width], c % NS, j * P, width,
                                    x_hi[:, j, tt * P:(tt + 1) * P], x_lo[:, j, tt * P:(tt + 1) * P],
                                    False, j == kt - 1, start=(j == 0 and tt == 0))
                else:
                    mm = k.products(pe, out(t)[:, 0:S], c % NS, j * P, width, x_hi[:, j, :], x_lo[:, j, :],
                                    j == 0, j == kt - 1)
            mm.then_inc(k.chunk_done.sem, 1)
    n = len(tiles)
    for t in range(max(n - 2, 0), n):
        k.gu_read[(k.bank + t) % 2] = read[t]
    k.bank = (k.bank + n) % 2
    k.used += n


def xn_parts(k):
    xl = k("xn_lo_ready")
    return {2 * j: xl.at(xl.n - KD // 2 + j + 1) for j in range(KD // 2)}


def split_y(k):
    block, made, up = tools(k)
    xh, xl = k("xn_hi_ready"), k("xn_lo_ready")
    h0 = xh.n

    @block.scalar
    def _(act):
        act.wait_ge(*k.chunk_done.at(k.used))
        act.wait_ge(*made("y_ready"))
        for j in range(KD // 2):
            act.activation(k.xn_hi[:, 2 * j:2 * j + 2, :], k.xn[:, 2 * j:2 * j + 2, :], ACT.Copy).then_inc(*xh.up())

    @block.gpsimd
    def _(pool):
        for j in range(KD // 2):
            pool.wait_ge(*xh.at(h0 + j + 1))
            pool.tensor_tensor(k.xn_lo[:, 2 * j:2 * j + 2, :], k.xn[:, 2 * j:2 * j + 2, :],
                               k.xn_hi[:, 2 * j:2 * j + 2, :], ALU.subtract).then_inc(*xl.up())


def project_out(k):
    block, made, up = tools(k)
    split_y(k)

    def add(m):
        return lambda dve, ps: dve.tensor_tensor(k.x[:, m, :], k.x[:, m, :], ps[:, 0:S], ALU.add)

    project(k, [("dve", False, P, add(m)) for m in range(KD)], k.xn_hi, k.xn_lo, first=xn_parts(k))

    @block.vector
    def _(dve):
        dve.wait_ge(*made("product_read_dve"))
        for j in range(KD // 2):
            dve.tensor_copy(k.tiny[:, j:j + 1], k.x[:, 2 * j, 0:1]).then_inc(*up("x_ready"))


def attention(k, q, kk, v, rows, scale, bias, gate, y0, slopes=None, sink=None):
    block, made, up = tools(k)
    H = 4
    A = k.arena
    logit = A("logit", H * S).rearrange("p (h t) -> p h t", h=H)
    pt0 = A("pt0", H * S).rearrange("p (h t) -> p h t", h=H)
    pt1 = A("pt1", H * P).rearrange("p (h t) -> p h t", h=H)
    ps = k.ps_acc[:, :, :].rearrange("p (q j) (h t) -> p q (j h) t", q=2, h=2)
    mx, es = k.tiny[:, 8:8 + H], k.tiny[:, 4:4 + H]
    for tq in range(2):
        K = P * (tq + 1)
        L = logit[:, :, 0:K]

        @block.tensor
        def _(pe):
            if tq == 0:
                pe.wait_ge(*made("att_operands"))
                pe.wait_ge(*made("x_ready"))
                pe.wait_ge(*made("acc_read"))
                pe.wait_ge(*made("logits_ready"))
            for h in range(H):
                mm = pe.matmul(ps[:, tq, h, 0:K], q(h, tq), kk(h, K), start=(h % 2 == 0), stop=True,
                               skip_group_check=True)
            mm.then_inc(*up("scores_ready"))
    for tq in range(2):
        K = P * (tq + 1)
        L = logit[:, :, 0:K]

        @block.vector
        def _(dve):
            dve.wait_ge(*k("scores_ready").made(1 - tq))
            dve.wait_ge(*made("transposed"))
            if slopes is None:
                dve.scalar_tensor_tensor(out=L, in0=ps[:, tq, :, 0:K], scalar=scale, in1=bias(tq),
                                         op0=ALU.mult, op1=ALU.add).then_inc(*up("logits_ready"))
            else:
                for h in range(H):
                    ins = dve.scalar_tensor_tensor(out=L[:, h, :], in0=bias(tq), scalar=slopes[h],
                                                   in1=ps[:, tq, h, 0:K], op0=ALU.mult, op1=ALU.add)
                ins.then_inc(*up("logits_ready"))
            dve.wait_ge(*made("logits_ready"))
            dve.tensor_reduce(mx, L, AX.X, ALU.max).then_inc(*up("row_max_ready"))
            dve.wait_ge(*made("row_max_ready"))
            if sink is not None:
                dve.tensor_tensor(mx, mx, sink, ALU.max).then_inc(*up("row_max_ready"))
                dve.wait_ge(*made("row_max_ready"))
                dve.tensor_tensor(es, sink, mx, ALU.subtract)
            dve.tensor_tensor(L, L, mx.unsqueeze(2).to_broadcast([P, H, K]), ALU.subtract)\
               .then_inc(*up("logits_ready"))

        @block.scalar
        def _(act):
            act.wait_ge(*made("logits_ready"))
            if sink is not None:
                act.activation(es, es, ACT.Exp)
            act.activation(L, L, ACT.Exp).then_inc(*up("exp_ready"))

        @block.vector
        def _(dve):
            dve.wait_ge(*made("exp_ready"))
            dve.tensor_reduce(k.tiny[:, 12:12 + H], L, AX.X, ALU.add).then_inc(*up("row_sum_ready"))
            dve.wait_ge(*made("row_sum_ready"))
            if sink is not None:
                dve.tensor_tensor(k.tiny[:, 12:12 + H], k.tiny[:, 12:12 + H], es, ALU.add).then_inc(*up("row_sum_ready"))
                dve.wait_ge(*made("row_sum_ready"))
            dve.reciprocal(k.tiny[:, 12:12 + H], k.tiny[:, 12:12 + H]).then_inc(*up("row_sum_ready"))
            dve.wait_ge(*made("row_sum_ready"))
            dve.tensor_tensor(L, L, k.tiny[:, 12:12 + H].unsqueeze(2).to_broadcast([P, H, K]), ALU.mult)\
               .then_inc(*up("probs_ready"))

        @block.tensor
        def _(pe):
            if tq == 0:
                pe.wait_ge(*k.gu_read[0])
                pe.wait_ge(*k.gu_read[1])
                pe.wait_ge(*made("misc_free"))
            pe.wait_ge(*made("probs_ready"))
            for h in range(H):
                for kt in range(tq + 1):
                    out = (k.ps_gu[h // 2][:, (h % 2) * S + tq * P:(h % 2) * S + (tq + 1) * P] if kt == 0
                           else k.ps_misc[:, h * P:(h + 1) * P])
                    mm = pe.transpose(out, logit[:, h, kt * P:(kt + 1) * P], con(k, "ident"))
            mm.then_inc(*up("transposed"))

    @block.scalar
    def _(act):
        act.wait_ge(*made("transposed"))
        for j in range(2):
            act.activation(pt0[:, 2 * j:2 * j + 2, :], k.ps_gu[j][:, :].rearrange("p (h t) -> p h t", h=2), ACT.Copy)\
               .then_inc(*up("pt_ready"))
            k.gu_read[j] = made("pt_ready")

    @block.vector
    def _(dve):
        dve.wait_ge(*made("transposed"))
        dve.tensor_copy(pt1, k.ps_misc[:, :].rearrange("p (h t) -> p h t", h=H)).then_inc(*up("misc_free"))

    @block.tensor
    def _(pe):
        pe.wait_ge(*made("pt_ready"))
        pe.wait_ge(*made("misc_free"))
        for h in range(H):
            b = 64 * (h % 2)
            out = k.ps_sum[b:b + 64, (h // 2) * S:(h // 2 + 1) * S]
            pe.matmul(out, v(0, h), pt0[:, h, :], start=(h < 2), stop=True, skip_group_check=True)
            mm = pe.matmul(out[:, P:S], v(1, h), pt1[:, h, :], start=False, stop=True, skip_group_check=True)
        mm.then_inc(*up("heads_ready"))

    @block.vector
    def _(dve):
        dve.wait_ge(*made("heads_ready"))
        heads = k.ps_sum[:, :].rearrange("p (m t) -> p m t", m=2)
        if gate is None:
            dve.tensor_copy(k.xn[:, y0:y0 + 2, :], heads).then_inc(*up("y_ready"))
        else:
            dve.tensor_tensor(k.xn[:, y0:y0 + 2, :], heads, gate, ALU.mult).then_inc(*up("y_ready"))


def mla(k, vec):
    block, made, up = tools(k)
    A = k.arena
    H = 4
    cq = A("cq", 3 * S).rearrange("p (m t) -> p m t", m=3)
    sq = A("sq", 3 * S).rearrange("p (m t) -> p m t", m=3)
    rs = A("rs", 2 * S)
    kh = A("kh", H * S).rearrange("p (h t) -> p h t", h=H)
    qh = A("qh", H * S).rearrange("p (h t) -> p h t", h=H)
    t1 = A("t1", H * S).rearrange("p (h t) -> p h t", h=H)
    v = A("v", 2 * S).rearrange("p (k c) -> p k c", k=2)
    gate = A("gate", 2 * S).rearrange("p (m t) -> p m t", m=2)
    cos, sin = con(k, "rope")[64:96, :], con(k, "rope")[96:128, :]

    def copy(dst):
        return lambda eng, ps: (eng.tensor_copy(dst, ps[:, 0:S]))

    def act_copy(dst, rows=slice(0, P)):
        return lambda eng, ps: eng.activation(dst, ps[rows, 0:S], ACT.Copy)

    def act_silu(dst):
        return lambda eng, ps: eng.activation(dst, ps[:, 0:S], ACT.Silu)

    project(k, [("act", False, P, act_copy(cq[:, 0, :])), ("act", False, P, act_copy(cq[:, 1, :])),
                ("act", False, P, act_copy(cq[:, 2, :]))], k.xn_hi, k.xn_lo, first=xn_parts(k))
    c0 = k.used

    @block.tensor
    def _(pe):
        s = c0 % NS
        k.wait_chunk(pe, c0)
        pe.wait_ge(*made("acc_read"))
        pe.wait_ge(*made("x_ready"))
        for j in range(KD):
            k.products(pe, k.ps_acc[:, 0, 0:S], s, j * P, P, k.xn_hi[:, j, :], k.xn_lo[:, j, :], j == 0, j == KD - 1)
        for j in range(KD):
            for tt in range(2):
                mm = k.rows(pe, k.ps_acc[:, 1, tt * 8:tt * 8 + 8], s, j * P, 8, k.xn_hi[:, j, tt * P:(tt + 1) * P],
                            k.xn_lo[:, j, tt * P:(tt + 1) * P], False, j == KD - 1, start=(j == 0 and tt == 0))
        mm.then_inc(k.chunk_done.sem, 1)
    k.used += 1

    @block.scalar
    def _(act):
        k.hi_for(act, c0)
        act.wait_ge(*made("product_read_act"))
        act.activation(sq, cq, ACT.Square).then_inc(*up("square_ready"))

    @block.vector
    def _(dve):
        k.lo_for(dve, c0)
        dve.wait_ge(*k.chunk_done.at(c0 + 1))
        dve.tensor_tensor(t1[64:96, 0, :], k.ps_acc[64:96, 0, 0:S], cos, ALU.mult)
        dve.tensor_copy(k.ba[:, :], k.ps_acc[:, 1, 0:16]).then_inc(*up("ba_ready"))
        dve.tensor_tensor(t1[64:96, 1, :], k.ps_acc[96:128, 0, 0:S], sin, ALU.mult).then_inc(*up("acc_read"))
        dve.wait_ge(*made("acc_read"))
        for h in range(H):
            ins = dve.tensor_tensor(kh[64:96, h, :], t1[64:96, 0, :], t1[64:96, 1, :], ALU.add)
        ins.then_inc(*up("rope_keys"))

    @block.tensor
    def _(pe):
        pe.wait_ge(*made("square_ready"))
        pe.wait_ge(*made("misc_free"))
        pe.wait_ge(*made("sum_read"))
        for m in range(3):
            mm = pe.matmul(k.ps_sum[:, (m // 2) * S:(m // 2 + 1) * S], k.ones[:, :], sq[:, m, :],
                           start=(m == 0), stop=(m >= 1), skip_group_check=True)
        mm.then_inc(*up("sum_sq_ready"))

    @block.vector
    def _(dve):
        dve.wait_ge(*made("sum_sq_ready"))
        dve.tensor_scalar(rs[:, 0:S], k.ps_sum[:, 0:S], 1.0 / 256, EPS, ALU.mult, ALU.add)
        dve.tensor_scalar(rs[:, S:2 * S], k.ps_sum[:, S:2 * S], 1.0 / 128, EPS, ALU.mult, ALU.add)\
           .then_inc(*up("sum_read"))
        dve.wait_ge(*made("sum_read"))
        dve.reciprocal(rs, rs).then_inc(*up("rstd_ready"))

    @block.scalar
    def _(act):
        act.wait_ge(*made("rstd_ready"))
        act.activation(rs, rs, ACT.Sqrt).then_inc(*up("rstd_ready"))

    @block.vector
    def _(dve):
        dve.wait_ge(*made("rstd_ready"))
        for m in range(3):
            ins = dve.scalar_tensor_tensor(out=sq[:, m, :], in0=cq[:, m, :], scalar=vec[:, m:m + 1],
                                           in1=rs[:, (m // 2) * S:(m // 2 + 1) * S], op0=ALU.mult, op1=ALU.mult)
        ins.then_inc(*up("latent_ready"))

    @block.scalar
    def _(act):
        act.wait_ge(*made("latent_ready"))
        act.activation(k.lat_hi[:, :, :], sq, ACT.Copy).then_inc(*up("latent_hi_ready"))

    @block.vector
    def _(dve):
        dve.wait_ge(*made("latent_hi_ready"))
        dve.tensor_tensor(k.lat_lo[:, :, :], sq, k.lat_hi[:, :, :], ALU.subtract).then_inc(*up("latent_lo_ready"))

    c1 = k.used
    psq = k.ps_acc[:, 0:2, :].rearrange("p j (h t) -> p (j h) t", h=2)
    psk = k.ps_acc[:, 2:4, :].rearrange("p j (h t) -> p (j h) t", h=2)

    @block.tensor
    def _(pe):
        pe.wait_ge(*made("latent_lo_ready"))
        pe.wait_ge(*made("acc_read"))
        k.wait_chunk(pe, c1)
        for h in range(H):
            for j in range(2):
                mm = k.products(pe, psq[:, h, :], c1 % NS, j * 512 + h * P, P, k.lat_hi[:, j, :], k.lat_lo[:, j, :],
                                False, j == 1, start=(j == 0 and h % 2 == 0))
        mm.then_inc(k.chunk_done.sem, 1)
        k.wait_chunk(pe, c1 + 1)
        pe.wait_ge(*k.gu_read[0])
        for h in range(H):
            k.products(pe, psk[:, h, :], (c1 + 1) % NS, h * P, P, k.lat_hi[:, 2, :], k.lat_lo[:, 2, :],
                       False, True, start=(h % 2 == 0))
        s = (c1 + 1) % NS
        for tt in range(2):
            out = k.ps_gu[0][:, tt * S:(tt + 1) * S].rearrange("p (h c) -> p h c", h=H)
            wh, wl = (w[:, s, 0:512].rearrange("p (h c) -> p h c", h=H)[:, :, 64:128] for w in (k.w_hi, k.w_lo))
            lh, ll = (x[:, 2, tt * P:(tt + 1) * P] for x in (k.lat_hi, k.lat_lo))
            pe.matmul(out, lh, wh, start=(tt == 0), stop=False, skip_group_check=True)
            pe.matmul(out, lh, wl, start=False, stop=False, skip_group_check=True)
            mm = pe.matmul(out, ll, wh, start=False, stop=True, skip_group_check=True)
        mm.then_inc(k.chunk_done.sem, 1)
    k.used += 2

    @block.scalar
    def _(act):
        k.hi_for(act, c1)
        k.hi_for(act, c1 + 1)
        act.wait_ge(*k.chunk_done.at(c1 + 2))
        act.activation(kh[0:64, :, :], psk[0:64, :, :], ACT.Copy)
        act.activation(v, k.ps_gu[0][:, :].rearrange("p (k c) -> p k c", k=2), ACT.Copy).then_inc(*up("keys_ready"))
        k.gu_read[0] = made("keys_ready")

    @block.vector
    def _(dve):
        k.lo_for(dve, c1)
        k.lo_for(dve, c1 + 1)
        dve.wait_ge(*k.chunk_done.at(c1 + 1))
        dve.wait_ge(*made("rope_keys"))
        dve.tensor_copy(qh[0:64, :, :], psq[0:64, :, :])
        dve.tensor_tensor(qh[64:96, :, :], psq[64:96, :, :], cos.unsqueeze(1).to_broadcast([32, H, S]), ALU.mult)
        dve.tensor_tensor(t1[64:96, :, :], psq[96:128, :, :], sin.unsqueeze(1).to_broadcast([32, H, S]), ALU.mult)\
           .then_inc(*up("acc_read"))
        dve.wait_ge(*made("acc_read"))
        dve.tensor_tensor(qh[64:96, :, :], qh[64:96, :, :], t1[64:96, :, :], ALU.add).then_inc(*up("att_operands"))

    @block.tensor
    def _(pe):
        pe.wait_ge(*made("keys_ready"))
    project(k, [("act", False, P, act_silu(gate[:, 0, :])), ("act", False, P, act_silu(gate[:, 1, :]))],
            k.xn_hi, k.xn_lo)
    attention(k, lambda h, tq: qh[0:96, h, tq * P:(tq + 1) * P], lambda h, K: kh[0:96, h, 0:K],
              lambda kt, h: v[:, kt, h * 64:(h + 1) * 64], 96, 96.0 ** -0.5,
              lambda tq: con(k, "causal", P if tq == 0 else 0).unsqueeze(1).to_broadcast([P, H, P * (tq + 1)]),
              gate, 0)


def t5_bias(k, io):
    block, made, up = tools(k)
    rep = k.arena("t5_rep", 4 * P).rearrange("p (h c) -> p h c", h=4)
    row = k.arena("t5_row", 4 * 2 * S).rearrange("p (h c) -> p h c", h=4)
    scratch = io["scratch"]

    @block.vector
    def _(dve):
        dve.wait_ge(*made("constants_ready"))
        dve.tensor_copy(rep[0:33, :, :], k.t5[0:33, :].unsqueeze(2).to_broadcast([33, 4, P])).then_inc(*up("t5_rep"))

    @block.tensor
    def _(pe):
        pe.wait_ge(*made("t5_rep"))
        for h in range(4):
            mm = pe.matmul(k.ps_acc[:, h, :], rep[0:33, h, :], con(k, "t5_hot")[0:33, :], start=True, stop=True)
        mm.then_inc(*up("t5_rows"))

    @block.vector
    def _(dve):
        dve.wait_ge(*made("t5_rows"))
        dve.tensor_copy(row, k.ps_acc[:, :, :]).then_inc(*up("acc_read"))

    @block.scalar
    def _(act):
        act.wait_ge(*made("acc_read"))
        act.dma_start(scratch.rearrange("h p c -> p h c"), row).then_inc(*k("t5_stored").up_dma())
        act.wait_ge(*made("t5_stored"))
        for tq in range(2):
            src = bass.AP(scratch.tensor, (S - 1) - P * tq, [[2 * S - 1, P], [2 * S * P, 4], [1, S]])
            act.dma_start(k.t5b[:, tq, :, :], src).then_inc(*k("t5_loaded").up_dma())


def moba(k):
    block, made, up = tools(k)
    A = k.arena
    H = 4
    q = A("q", 2 * S).rearrange("p (m t) -> p m t", m=2)
    kz = A("kz", H * S).rearrange("p (h t) -> p h t", h=H)
    v = A("v", 2 * S).rearrange("p (k c) -> p k c", k=2)
    gate = A("gate", 2 * S).rearrange("p (m t) -> p m t", m=2)

    @block.gpsimd
    def _(pool):
        pool.wait_ge(*made("heads_ready"))
        pool.wait_ge(*made("y_ready"))
        pool.memset(kz, 0.0).then_inc(*up("kz_zero"))

    def keys(m):
        def work(act, ps):
            act.activation(kz[0:64, 2 * m, :], ps[0:64, 0:S], ACT.Copy)
            return act.activation(kz[64:128, 2 * m + 1, :], ps[64:128, 0:S], ACT.Copy)
        return work

    @block.scalar
    def _(act):
        act.wait_ge(*made("y_ready"))
        act.wait_ge(*made("kz_zero"))
    project(k, [("act", False, P, lambda act, ps: act.activation(q[:, 0, :], ps[:, 0:S], ACT.Copy)),
                ("act", False, P, lambda act, ps: act.activation(q[:, 1, :], ps[:, 0:S], ACT.Copy)),
                ("act", False, P, keys(0)), ("act", False, P, keys(1)),
                ("act", True, P, lambda act, ps: act.activation(v[:, :, 0:P], ps[:, 0:S].rearrange("p (k c) -> p k c", k=2), ACT.Copy)),
                ("act", True, P, lambda act, ps: act.activation(v[:, :, P:S], ps[:, 0:S].rearrange("p (k c) -> p k c", k=2), ACT.Copy)),
                ("act", False, P, lambda act, ps: act.activation(gate[:, 0, :], ps[:, 0:S], ACT.Silu)),
                ("act", False, P, lambda act, ps: act.activation(gate[:, 1, :], ps[:, 0:S], ACT.Silu))],
            k.xn_hi, k.xn_lo)

    @block.tensor
    def _(pe):
        pe.wait_ge(*made("product_read_act"))

    @block.vector
    def _(dve):
        dve.wait_ge(*made("t5_loaded"))
    attention(k, lambda h, tq: q[:, h // 2, tq * P:(tq + 1) * P], lambda h, K: kz[:, h, 0:K],
              lambda kt, h: v[:, kt, h * 64:(h + 1) * 64], 128, 64.0 ** -0.5,
              lambda tq: k.t5b[:, tq, :, 0:P * (tq + 1)], gate, 6)


def gdn(k, vec):
    block, made, up = tools(k)
    A = k.arena
    H, TAPS, G = 4, 4, 8
    qkv = A("qkv", 12 * S).rearrange("p (m t) -> p m t", m=12)
    z = A("z", H * S).rearrange("p (m t) -> p m t", m=H)
    raw = A("raw", 2 * (S + 4)).rearrange("p (b t) -> p b t", b=2)
    acc = A("acc", 2 * S).rearrange("p (b t) -> p b t", b=2)
    sq = A("sq", 8 * S)
    rs = A("rs", 8 * S)
    acc_flat = A("acc", 2 * S)
    conv_w, gain, a_log, dt_bias = vec[:, 0:48], vec[:, 48:49], vec[:, 49:53], vec[:, 53:57]
    c0 = k.used
    b0 = k.bank
    cr, cd, cs = k("conv_raw_ready"), k("conv_ready"), k("conv_silu_ready")
    cs0, cd0, cr0 = cs.n, cd.n, cr.n

    @block.gpsimd
    def _(pool):
        pool.wait_ge(*made("y_ready"))
        pool.wait_ge(*made("heads_ready"))
        pool.memset(raw[:, :, 0:3], 0.0).then_inc(*up("conv_pad_ready"))

    @block.scalar
    def _(act):
        act.wait_ge(*made("conv_pad_ready"))
        def finish(t):
            act.wait_ge(*cd.at(cd0 + TAPS * (t + 1)))
            act.activation(qkv[:, t, :], acc[:, t % 2, :], ACT.Silu).then_inc(*cs.up())
        for t in range(12):
            k.hi_for(act, c0 + t)
            act.wait_ge(*k.chunk_done.at(c0 + t + 1))
            act.activation(raw[:, t % 2, 3:3 + S], k.ps_gu[(b0 + t) % 2][:, 0:S], ACT.Copy).then_inc(*cr.up())
            if t >= 1:
                finish(t - 1)
        finish(11)

    @block.vector
    def _(dve):
        for t in range(12):
            k.lo_for(dve, c0 + t)
            dve.wait_ge(*cr.at(cr0 + t + 1))
            if t >= 2:
                dve.wait_ge(*cs.at(cs0 + t - 1))
            w = lambda j: conv_w[:, 4 * t + j:4 * t + j + 1]
            dst, src = acc[:, t % 2, :], raw[:, t % 2, :]
            dve.tensor_scalar(dst, src[:, 0:S], w(0), None, ALU.mult).then_inc(*cd.up())
            for j in range(1, TAPS):
                dve.wait_ge(*cd.made())
                dve.scalar_tensor_tensor(out=dst, in0=src[:, j:j + S], scalar=w(j), in1=dst,
                                         op0=ALU.mult, op1=ALU.add).then_inc(*cd.up())

    @block.tensor
    def _(pe):
        for t in range(12):
            c = c0 + t
            k.wait_chunk(pe, c)
            pe.wait_ge(*(cr.at(cr0 + t - 1) if t >= 2 else k.gu_read[(b0 + t) % 2]))
            for j in range(KD):
                mm = k.products(pe, k.ps_gu[(b0 + t) % 2][:, 0:S], c % NS, j * P, P, k.xn_hi[:, j, :],
                                k.xn_lo[:, j, :], j == 0, j == KD - 1)
            mm.then_inc(k.chunk_done.sem, 1)
    k.used += 12
    for t in (10, 11):
        k.gu_read[(b0 + t) % 2] = cr.at(cr0 + t + 1)
    project(k, [("act", False, P, (lambda m: lambda act, ps: act.activation(z[:, m, :], ps[:, 0:S], ACT.Silu))(m))
                for m in range(H)], k.xn_hi, k.xn_lo)

    g8 = A("g8", 96).rearrange("p (n c) -> p n c", n=12)
    (beta, aa, low, g, gc, kb_s, ke_s, ew) = (g8[:, n, :] for n in range(8))
    view = lambda t: t.rearrange("p (t h) -> p t h", t=2)
    ba = k.ba[:, :].rearrange("p (t c) -> p t c", t=2)

    @block.vector
    def _(dve):
        dve.wait_ge(*made("ba_ready"))
        dve.tensor_tensor(view(aa), ba[:, :, 4:8], dt_bias.unsqueeze(1).to_broadcast([P, 2, 4]), ALU.add)\
           .then_inc(*up("gate_step"))
        dve.wait_ge(*made("gate_step"))
        dve.tensor_scalar(low, aa, -1.0, None, ALU.mult).then_inc(*up("gate_step"))
        dve.wait_ge(*made("gate_step"))
        dve.tensor_tensor(low, aa, low, ALU.min).then_inc(*up("gate_step"))

    @block.scalar
    def _(act):
        act.wait_ge(*made("gate_step"))
        act.activation(view(beta), ba[:, :, 0:4], ACT.Sigmoid)
        act.activation(low, low, ACT.Exp).then_inc(*up("gate_exp"))
        act.activation(g8[:, 8, 0:4], a_log, ACT.Exp)
        act.wait_ge(*made("gate_exp"))
        act.activation(low, low, ACT.Ln, bias=1.0).then_inc(*up("gate_exp"))

    @block.vector
    def _(dve):
        dve.wait_ge(*made("gate_exp"))
        dve.scalar_tensor_tensor(out=g, in0=aa, scalar=0.0, in1=low, op0=ALU.max, op1=ALU.add).then_inc(*up("gate_step"))
        dve.wait_ge(*made("gate_step"))
        dve.scalar_tensor_tensor(out=view(g), in0=view(g), scalar=-1.0, in1=g8[:, 8, 0:4].unsqueeze(1).to_broadcast([P, 2, 4]),
                                 op0=ALU.mult, op1=ALU.mult).then_inc(*up("gate_step"))

    big = lambda name: A(name, G * P)
    four = lambda ap: ap.rearrange("p (n c) -> p n c", n=G)
    ET, LT, AT, T, U, Y = (big(n) for n in ("ET", "LT", "AT", "T", "U", "Y"))
    Lm = [big("Lm0"), big("Lm1")]
    grow = k.ps_acc[:, 0:2, :].rearrange("p j c -> p (j c)")
    brow = k.ps_acc[:, 2:4, :].rearrange("p j c -> p (j c)")
    bank = lambda ps0, n: ps0[:, n // 4, (n % 4) * P:(n % 4 + 1) * P]
    acc01, acc23 = k.ps_acc[:, 0:2, :], k.ps_acc[:, 2:4, :]
    grep, brep = Y, Lm[0]

    @block.vector
    def _(dve):
        dve.wait_ge(*made("gate_step"))
        dve.tensor_copy(four(grep), g.unsqueeze(2).to_broadcast([P, G, P]))
        dve.tensor_copy(four(brep), beta.unsqueeze(2).to_broadcast([P, G, P])).then_inc(*up("gates_spread"))

    @block.tensor
    def _(pe):
        pe.wait_ge(*made("gates_spread"))
        pe.wait_ge(*made("acc_read"))
        pe.wait_ge(*made("misc_free"))
        for n in range(G):
            pe.matmul(bank(acc01, n), four(grep)[:, n, :], con(k, "upper"), start=(n % 4 == 0), stop=True, skip_group_check=True)
        for n in range(G):
            pe.matmul(bank(acc23, n), four(brep)[:, n, :], con(k, "ident"), start=(n % 4 == 0), stop=True, skip_group_check=True)
        pe.matmul(k.ps_misc[:, 0:G], con(k, "upper"), g, start=True, stop=True).then_inc(*up("gate_rows_ready"))

    @block.scalar
    def _(act):
        act.wait_ge(*made("conv_silu_ready"))
        act.activation(sq, qkv[:, 0:8, :].rearrange("p m t -> p (m t)"), ACT.Square).then_inc(*up("square_ready"))

    @block.vector
    def _(dve):
        dve.wait_ge(*made("gate_rows_ready"))
        dve.tensor_copy(gc, k.ps_misc[:, 0:G]).then_inc(*up("misc_free"))
        dve.wait_ge(*made("misc_free"))
        for n in range(G):
            ins = dve.tensor_scalar(four(ET)[:, n, :], bank(acc01, n), gc[:, n:n + 1], 0.0, ALU.subtract, ALU.min)
        dve.tensor_tensor(ke_s, grow.rearrange("p (n c) -> p n c", c=P)[:, :, P - 1], gc, ALU.subtract)
        dve.tensor_copy(acc_flat, grow[:, 4 * P:8 * P]).then_inc(*up("decay_args"))

    @block.scalar
    def _(act):
        act.wait_ge(*made("decay_args"))
        act.activation(ET, ET, ACT.Exp)
        act.activation(ke_s, ke_s, ACT.Exp)
        act.activation(kb_s, gc, ACT.Exp)
        act.activation(acc_flat, acc_flat, ACT.Exp).then_inc(*up("decay_exp"))

    @block.vector
    def _(dve):
        dve.wait_ge(*made("decay_exp"))
        dve.tensor_tensor(four(ET), four(ET), con(k, "upper").unsqueeze(1).to_broadcast([P, G, P]), ALU.mult)
        dve.tensor_tensor(kb_s, kb_s, beta, ALU.mult).then_inc(*up("decay_ready"))
        dve.tensor_copy(LT, brow).then_inc(*up("acc_read"))

    for half in range(2):
        @block.tensor
        def _(pe):
            pe.wait_ge(*made("square_ready"))
            pe.wait_ge(*made("acc_read"))
            for m in range(4 * half, 4 * half + 4):
                mm = pe.matmul(k.ps_acc[:, m // 2, (m % 2) * S:(m % 2 + 1) * S], k.ones[:, :], sq[:, m * S:(m + 1) * S],
                               start=(m % 2 == 0), stop=True, skip_group_check=True)
            mm.then_inc(*up("sum_sq_ready"))

    @block.vector
    def _(dve):
        dve.wait_ge(*made("sum_sq_ready"))
        dve.tensor_scalar(rs, k.ps_acc[:, :, :].rearrange("p j c -> p (j c)"), 1e-6, None, ALU.add).then_inc(*up("acc_read"))

    @block.scalar
    def _(act):
        act.wait_ge(*made("acc_read"))
        act.activation(rs, rs, ACT.Ln).then_inc(*up("rs_step"))
        act.wait_ge(*made("rs_step"))
        act.activation(rs, rs, ACT.Exp, scale=-0.5).then_inc(*up("rs_step"))

    @block.vector
    def _(dve):
        dve.wait_ge(*made("rs_step"))
        rows = lambda m: qkv[:, m:m + 4, :].rearrange("p m t -> p (m t)")
        dve.tensor_tensor(rows(4), rows(4), rs[:, 4 * S:8 * S], ALU.mult).then_inc(*up("k_ready"))
        dve.scalar_tensor_tensor(out=rows(0), in0=rows(0), scalar=128.0 ** -0.5, in1=rs[:, 0:4 * S],
                                 op0=ALU.mult, op1=ALU.mult).then_inc(*up("q_ready"))

    tile = lambda m, n: qkv[:, m + n % 4, (n // 4) * P:(n // 4 + 1) * P]
    gu = [k.ps_gu[0][:, :], k.ps_gu[1][:, :]]
    gub = lambda n: gu[n // 4][:, (n % 4) * P:(n % 4 + 1) * P]

    @block.tensor
    def _(pe):
        pe.wait_ge(*made("k_ready"))
        pe.wait_ge(*made("acc_read"))
        for n in range(G):
            mm = pe.matmul(bank(acc01, n), tile(4, n), tile(4, n), start=(n % 4 == 0), stop=True, skip_group_check=True)
        mm.then_inc(*up("kk_ready"))
        pe.wait_ge(*made("q_ready"))
        for n in range(G):
            mm = pe.matmul(bank(acc23, n), tile(4, n), tile(0, n), start=(n % 4 == 0), stop=True, skip_group_check=True)
        mm.then_inc(*up("qk_ready"))
        pe.wait_ge(*k.gu_read[0])
        pe.wait_ge(*k.gu_read[1])
        for n in range(G):
            mm = pe.transpose(gub(n), tile(4, n), con(k, "ident"))
        mm.then_inc(*up("k_turned"))

    kN, vN = sq[:, 0:G * P], sq[:, G * P:2 * G * P]
    Kb, ke, Vb = rs[:, 0:H * P], rs[:, H * P:2 * H * P], rs[:, 2 * H * P:4 * H * P]

    @block.vector
    def _(dve):
        dve.wait_ge(*made("decay_ready"))
        dve.wait_ge(*made("kk_ready"))
        dve.tensor_tensor(LT, LT, ET, ALU.mult).then_inc(*up("L_step"))
        dve.wait_ge(*made("L_step"))
        dve.tensor_tensor(LT, LT, acc01.rearrange("p j c -> p (j c)"), ALU.mult).then_inc(*up("L_ready"))
        dve.wait_ge(*made("qk_ready"))
        dve.tensor_tensor(AT, ET, acc23.rearrange("p j c -> p (j c)"), ALU.mult).then_inc(*up("A_ready"))

    @block.scalar
    def _(act):
        act.wait_ge(*made("k_turned"))
        for j in range(2):
            act.activation(kN[:, j * 4 * P:(j + 1) * 4 * P], gu[j], ACT.Copy).then_inc(*up("kN_ready"))

    @block.tensor
    def _(pe):
        pe.wait_ge(*made("kN_ready"))
        for n in range(G):
            mm = pe.transpose(gub(n), tile(8, n), con(k, "ident"))
        mm.then_inc(*up("v_turned"))

    @block.scalar
    def _(act):
        act.wait_ge(*made("v_turned"))
        for j in range(2):
            act.activation(vN[:, j * 4 * P:(j + 1) * 4 * P], gu[j], ACT.Copy).then_inc(*up("vN_ready"))
            k.gu_read[j] = made("vN_ready")

    @block.gpsimd
    def _(pool):
        pool.wait_ge(*made("L_ready"))
        pool.wait_ge(*made("gate_rows_ready"))
        ident = con(k, "ident").unsqueeze(1).to_broadcast([P, G, P])
        pool.tensor_copy(four(T), ident)
        pool.tensor_copy(four(U), ident).then_inc(*up("inv_start"))

    lm, yr, ys, ty, tr = k("Lm_ready"), k("Y_ready"), k("Y_copied"), k("TY_ready"), k("T_ready")
    yr0, lm0 = yr.n, lm.n
    lm_eng = block.gpsimd
    for lv in range(LEVELS):
        last = lv == LEVELS - 1

        @block.gpsimd
        def _(pool):
            if lv >= 2:
                pool.wait_ge(*yr.at(yr0 + lv - 1))
            m = con(k, "levels", lv * P, (lv + 1) * P).unsqueeze(1).to_broadcast([P, G, P])
            pool.tensor_tensor(four(Lm[lv % 2]), four(LT), m, ALU.mult).then_inc(*lm.up())

        @block.tensor
        def _(pe):
            if lv == 0:
                pe.wait_ge(*made("inv_start"))
                pe.wait_ge(*made("A_ready"))
            else:
                pe.wait_ge(*tr.made())
            pe.wait_ge(*lm.at(lm0 + lv + 1))
            for n in range(G):
                mm = pe.matmul(bank(acc01, n), four(Lm[lv % 2])[:, n, :], four(T)[:, n, :],
                               start=(n % 4 == 0), stop=True, skip_group_check=True)
            mm.then_inc(*yr.up())

        @block.scalar
        def _(act):
            act.wait_ge(*yr.made())
            act.activation(Y, acc01.rearrange("p j c -> p (j c)"), ACT.Copy).then_inc(*ys.up())

        @block.tensor
        def _(pe):
            pe.wait_ge(*ys.made())
            if lv == 0:
                pe.wait_ge(*made("vN_ready"))
            for n in range(G):
                mm = pe.matmul(bank(acc23, n), four(Y)[:, n, :], four(U)[:, n, :],
                               start=(n % 4 == 0), stop=True, skip_group_check=True)
            mm.then_inc(*ty.up())
            if not last:
                for n in range(G):
                    mm = pe.matmul(gub(n), four(U)[:, n, :], four(Y)[:, n, :],
                                   start=(n % 4 == 0), stop=True, skip_group_check=True)
                mm.then_inc(*ty.up())

        @block.vector
        def _(dve):
            if not last:
                dve.wait_ge(*ty.made())
                for j in range(2):
                    part = T[:, j * 4 * P:(j + 1) * 4 * P]
                    dve.tensor_tensor(part, part, gu[j], ALU.subtract)
            dve.wait_ge(*ty.made())
            dve.tensor_tensor(U, U, acc23.rearrange("p j c -> p (j c)"), ALU.subtract).then_inc(*tr.up())
    k.gu_read = [made("T_ready")] * 2

    cols = lambda s, w: s.unsqueeze(2).to_broadcast([P, w, P])

    @block.vector
    def _(dve):
        dve.wait_ge(*made("vN_ready"))
        dve.wait_ge(*made("decay_ready"))
        dve.tensor_tensor(four(Vb), four(vN), cols(beta, G), ALU.mult)
        dve.tensor_tensor(Kb.rearrange("p (h c) -> p h c", h=H), four(kN)[:, 4:8, :], cols(kb_s[:, 4:8], H), ALU.mult)
        dve.tensor_tensor(ke.rearrange("p (h c) -> p h c", h=H), four(kN)[:, 0:4, :], cols(ke_s[:, 0:4], H), ALU.mult)
        dve.tensor_tensor(acc_flat.rearrange("p (h c) -> p h c", h=H), acc_flat.rearrange("p (h c) -> p h c", h=H),
                          qkv[:, 0:4, P:S], ALU.mult).then_inc(*up("rhs_ready"))
    qg = acc_flat
    U0, WT, ST = T, Lm[0][:, 0:H * P], Lm[0][:, H * P:2 * H * P]
    UN = Lm[1][:, 0:H * P]
    h4 = lambda t, h: t[:, h * P:(h + 1) * P]

    @block.tensor
    def _(pe):
        pe.wait_ge(*made("T_ready"))
        pe.wait_ge(*made("rhs_ready"))
        for n in range(G):
            mm = pe.matmul(gub(n), four(U)[:, n, :], four(Vb)[:, n, :], start=(n % 4 == 0), stop=True, skip_group_check=True)
        mm.then_inc(*up("U0_ready"))
        for h in range(H):
            mm = pe.matmul(bank(acc01, h), h4(Kb, h), four(U)[:, 4 + h, :], start=(h == 0), stop=True, skip_group_check=True)
        mm.then_inc(*up("W_ready"))

    @block.scalar
    def _(act):
        act.wait_ge(*made("U0_ready"))
        for j in range(2):
            act.activation(U0[:, j * 4 * P:(j + 1) * 4 * P], gu[j], ACT.Copy).then_inc(*up("U0_copied"))
        k.gu_read = [made("U0_copied")] * 2

    @block.vector
    def _(dve):
        dve.wait_ge(*made("W_ready"))
        dve.tensor_copy(WT, acc01[:, 0, :]).then_inc(*up("W_copied"))

    @block.tensor
    def _(pe):
        pe.wait_ge(*made("U0_copied"))
        for h in range(H):
            mm = pe.matmul(bank(acc01, 4 + h), h4(ke, h), four(U0)[:, h, :], start=(h == 0), stop=True, skip_group_check=True)
        mm.then_inc(*up("S_ready"))

    @block.scalar
    def _(act):
        act.wait_ge(*made("S_ready"))
        act.activation(ST, acc01[:, 1, :], ACT.Copy).then_inc(*up("S_copied"))

    @block.tensor
    def _(pe):
        pe.wait_ge(*made("S_copied"))
        pe.wait_ge(*made("W_copied"))
        for h in range(H):
            mm = pe.matmul(bank(acc01, h), h4(WT, h), h4(ST, h), start=(h == 0), stop=True, skip_group_check=True)
        mm.then_inc(*up("WS_ready"))

    @block.vector
    def _(dve):
        dve.wait_ge(*made("WS_ready"))
        dve.tensor_tensor(UN, U0[:, 4 * P:8 * P], acc01[:, 0, :], ALU.subtract).then_inc(*up("U_ready"))

    @block.tensor
    def _(pe):
        for h in range(H):
            out = acc23[:, h // 2, (h % 2) * S:(h % 2 + 1) * S]
            pe.matmul(out[:, 0:P], four(U0)[:, h, :], four(AT)[:, h, :], start=(h % 2 == 0), stop=True, skip_group_check=True)
            pe.matmul(out[:, P:S], h4(ST, h), h4(qg, h), start=False, stop=False, skip_group_check=True)
        pe.wait_ge(*made("U_ready"))
        for h in range(H):
            out = acc23[:, h // 2, (h % 2) * S:(h % 2 + 1) * S]
            mm = pe.matmul(out[:, P:S], h4(UN, h), four(AT)[:, 4 + h, :], start=False, stop=True, skip_group_check=True)
        mm.then_inc(*up("heads_ready"))
    out = acc23.rearrange("p j c -> p (j c)")
    head_norm(k, out, [acc01[:, 0, :], acc01[:, 1, :]], Y, Lm[1], gain, z.rearrange("p m t -> p (m t)"), 2, H, P)

    @block.vector
    def _(dve):
        dve.wait_ge(*made("y_ready"))
        dve.tensor_copy(k.tiny[:, 0:1], k.xn[:, 2, 0:1]).then_inc(*up("acc_read"))


def head_norm(k, out, sums, sq, rs, gain, gate, y0, tiles, width):
    block, made, up = tools(k)
    half = lambda t, j: t[:, j * 2 * S:(j + 1) * 2 * S]

    @block.scalar
    def _(act):
        act.wait_ge(*made("heads_ready"))
        act.activation(sq, out, ACT.Square).then_inc(*up("square_ready"))

    @block.tensor
    def _(pe):
        pe.wait_ge(*made("square_ready"))
        pe.wait_ge(*made("head_sums_read"))
        for m in range(tiles):
            mm = pe.matmul(sums[m // 2][:, (m % 2) * S:(m % 2 + 1) * S], k.ones[:, :], sq[:, m * S:(m + 1) * S],
                           start=(m % 2 == 0), stop=True, skip_group_check=True)
        mm.then_inc(*up("sum_sq_ready"))

    @block.vector
    def _(dve):
        dve.wait_ge(*made("sum_sq_ready"))
        for j in range(2):
            dve.tensor_scalar(half(rs, j), sums[j], 1.0 / width, EPS, ALU.mult, ALU.add).then_inc(*up("head_sums_read"))

    @block.scalar
    def _(act):
        act.wait_ge(*made("head_sums_read"))
        act.activation(rs, rs, ACT.Ln).then_inc(*up("rs_step"))
        act.wait_ge(*made("rs_step"))
        act.activation(rs, rs, ACT.Exp, scale=-0.5).then_inc(*up("rs_step"))

    @block.vector
    def _(dve):
        dve.wait_ge(*made("rs_step"))
        dve.tensor_tensor(rs, rs, out, ALU.mult).then_inc(*up("norm_step"))
        dve.wait_ge(*made("norm_step"))
        dve.scalar_tensor_tensor(out=k.xn[:, y0:y0 + tiles, :].rearrange("p m t -> p (m t)"), in0=rs, scalar=gain,
                                 in1=gate, op0=ALU.mult, op1=ALU.mult).then_inc(*up("y_ready"))


def widths(w, *parts):
    return np.concatenate([w[:, a:b] for a, b in parts], 1)


def as_columns(w):
    K, N = w.shape
    return w.reshape(K // P, P, N // P, P).transpose(2, 1, 0, 3).reshape(N // P, P, -1)


def as_rows(w):
    return w.reshape(-1, P, w.shape[1])


def filled(chunks):
    n, p, c = chunks.shape
    return chunks if c == CH else np.concatenate([chunks, np.zeros((n, p, CH - c), chunks.dtype)], 2)


def first_chunks(w_in, w_uq, w_ukv, w_out):
    at = np.cumsum([0, 256, 128, 32, 256, 512, 512, 512, 512, 4, 4, 256, 256, 256, 256])
    part = lambda n: w_in[:, at[n]:at[n + 1]]
    kr = part(2)
    misc = np.concatenate([part(8), part(9), np.zeros((D, 56), w_in.dtype), kr, kr[:, 16:], kr[:, :16]], 1)
    q = w_uq.reshape(256, 4, 96)
    uq = np.concatenate([q, q[:, :, 80:96], q[:, :, 64:80]], 2).reshape(256, 512)
    uq = uq.reshape(2, P, 512).transpose(1, 0, 2).reshape(1, P, CH)
    return [as_columns(part(0)), as_columns(part(1)), as_columns(misc), uq, filled(w_ukv.reshape(1, P, 512)),
            as_columns(part(3)),
            as_columns(w_in[:, at[4]:at[8]]),
            as_columns(w_in[:, at[10]:at[14]]),
            as_columns(w_out)]


def first_layer(k, v):
    norm(k, v[:, 0:8])
    k.arena.clear()
    mla(k, v[:, 8:11])
    k.arena.clear()
    gdn(k, v[:, 11:68])
    k.arena.clear()
    moba(k)
    project_out(k)


def columns(v):
    return v.reshape(-1, P).T


def spread(v):
    return np.broadcast_to(v.reshape(1, -1), (P, v.size))


def first_vectors(norm_w, q_norm, kv_norm, conv_w, a_log, dt_bias, gdn_norm):
    conv = conv_w.reshape(4, 12, P).transpose(2, 1, 0).reshape(P, 48)
    return [columns(norm_w), columns(q_norm), columns(kv_norm), conv, columns(gdn_norm), spread(a_log), spread(dt_bias)]


I32 = mybir.dt.int32


def lower_bounds(k, raw):
    block, made, up = tools(k)
    L = k.lbw
    part = lambda n: L[:, n * KD:(n + 1) * KD]
    layer = lambda n: raw[:, n * KD:(n + 1) * KD]
    e4 = L[:, 0:4 * KD]

    @block.vector
    def _(dve):
        dve.tensor_reduce(part(4), raw.rearrange("p (l m) -> p m l", l=4), AX.X, ALU.max).then_inc(*up("bounds_step"))
        dve.wait_ge(*made("bounds_step"))
        dve.tensor_tensor(e4.rearrange("p (l m) -> p l m", l=4), raw.rearrange("p (l m) -> p l m", l=4),
                          part(4).unsqueeze(1).to_broadcast([P, 4, KD]), ALU.subtract).then_inc(*up("bounds_step"))

    @block.scalar
    def _(act):
        act.wait_ge(*made("bounds_step"))
        act.activation(e4, e4, ACT.Exp).then_inc(*up("bounds_exp"))

    @block.vector
    def _(dve):
        dve.wait_ge(*made("bounds_exp"))
        dve.tensor_reduce(part(5), e4.rearrange("p (l m) -> p m l", l=4), AX.X, ALU.add)
        dve.tensor_tensor(part(6), part(1), part(2), ALU.add).then_inc(*up("bounds_step"))
        dve.wait_ge(*made("bounds_step"))
        dve.tensor_tensor(part(6), part(6), part(3), ALU.add)
        dve.reciprocal(part(5), part(5)).then_inc(*up("bounds_step"))
        dve.wait_ge(*made("bounds_step"))
        dve.tensor_tensor(part(6), part(6), part(5), ALU.mult)
        dve.tensor_tensor(part(7), part(0), part(5), ALU.mult).then_inc(*up("bounds_ready"))
    k.lb = (part(6), part(7))


def hgrn(k, g_norm, lb):
    block, made, up = tools(k)
    A = k.arena
    H = 8
    q, kk, f = A("q", H * S), A("k", H * S), A("f", H * S)
    f2 = A("f2", H * S)
    v = A("v", 2 * H * P).rearrange("p (k c) -> p k c", k=2)
    gate = A("gate", H * S)
    at0 = A("at0", H * S).rearrange("p (h t) -> p h t", h=H)
    at1 = A("at1", H * P).rearrange("p (h t) -> p h t", h=H)
    m = lambda t, h: t[:, h * S:(h + 1) * S]
    sil = lambda h: lambda act, ps: act.activation(m(q, h), ps[:, 0:S], ACT.Silu)

    def forget(h):
        def work(act, ps):
            act.activation(m(f, h), ps[:, 0:S], ACT.Sigmoid)
            return act.activation(m(kk, h), ps[:, 0:S], ACT.Sigmoid, scale=-1.0)
        return work

    @block.scalar
    def _(act):
        act.wait_ge(*made("y_ready"))
        act.wait_ge(*made("acc_read"))
    project(k, [("act", False, P, sil(h)) for h in range(H)], k.xn_hi, k.xn_lo, first=xn_parts(k))
    project(k, [("act", False, P, forget(h)) for h in range(H)], k.xn_hi, k.xn_lo)

    @block.vector
    def _(dve):
        dve.wait_ge(*made("product_read_act"))
        if lb is not None:
            for h in range(H):
                dve.tensor_scalar(m(f, h), m(f, h), lb[1][:, h:h + 1], lb[0][:, h:h + 1], ALU.mult, ALU.add)
                ins = dve.tensor_scalar(m(kk, h), m(kk, h), lb[1][:, h:h + 1], None, ALU.mult)
            ins.then_inc(*up("forget_ready"))
    project(k, [("act", True, P, (lambda h: lambda act, ps: act.activation(
        v[:, :, h * P:(h + 1) * P], ps[:, 0:S].rearrange("p (k c) -> p k c", k=2), ACT.Copy))(h)) for h in range(H)],
        k.xn_hi, k.xn_lo)
    project(k, [("act", False, P, (lambda h: lambda act, ps: act.activation(m(gate, h), ps[:, 0:S], ACT.Silu))(h))
                for h in range(H)], k.xn_hi, k.xn_lo)

    sc, cp, dq, dk = k("level_scores"), k("level_copied"), k("q_decayed"), k("k_decayed")
    HG = 4
    copied, q_done, k_done = ([None, None] for _ in range(3))
    ident = con(k, "ident").unsqueeze(1).to_broadcast([P, HG, P])
    tot = [(f, 0)]
    at = 0
    for s in (2 << n for n in range(LEVELS)):
        tot.append((f2, at))
        at += H * S // s
    for lv in range(-1, LEVELS + 1):
        s = 0 if lv < 0 else 1 << lv
        for g in range(2):
            h0 = HG * g
            bank = lambda tt: k.ps_acc[:, 2 * g + tt, :]

            @block.tensor
            def _(pe):
                if lv < 0:
                    pe.wait_ge(*made("forget_ready"))
                    pe.wait_ge(*made("product_read_act"))
                    pe.wait_ge(*made("x_ready"))
                    pe.wait_ge(*made("acc_read"))
                else:
                    pe.wait_ge(*q_done[g])
                    pe.wait_ge(*k_done[g])
                    pe.wait_ge(*copied[g])
                for h in range(HG):
                    for tt in range(2 if lv < LEVELS else 1):
                        a = (h0 + h) * S + tt * P
                        b = a if lv < LEVELS else a + P
                        mm = pe.matmul(bank(tt)[:, h * P:(h + 1) * P], kk[:, a:a + P], q[:, b:b + P],
                                       start=(h == 0), stop=True, skip_group_check=True)
                mm.then_inc(*sc.up())

            @block.vector
            def _(dve):
                dve.wait_ge(*sc.made())
                for tt in range(2):
                    src = bank(tt).rearrange("p (h t) -> p h t", h=HG)
                    dst = at0[:, h0:h0 + HG, 0:P] if tt == 0 else at1[:, h0:h0 + HG, :]
                    if lv < 0:
                        ins = dve.tensor_tensor(dst, src, ident, ALU.mult)
                    elif lv < LEVELS:
                        mask = con(k, "levels", lv * P, (lv + 1) * P).bitcast(I32).unsqueeze(1).to_broadcast([P, HG, P])
                        if tt == 0:
                            dve.wait_ge(*copied[g])
                        ins = dve.copy_predicated(dst, mask, src)
                    elif tt == 0:
                        ins = dve.tensor_copy(at0[:, h0:h0 + HG, P:S], src)
                ins.then_inc(*cp.up())
            copied[g] = cp.made()

            n = slice(h0 * S, (h0 + HG) * S)
            if lv == -1:
                @block.vector
                def _(dve):
                    dve.tensor_tensor(q[:, n], q[:, n], f[:, n], ALU.mult).then_inc(*dq.up())
                @block.gpsimd
                def _(pool):
                    pool.wait_ge(*sc.made())
                    pool.memset(k.tiny[:, g:g + 1], 0.0).then_inc(*dk.up())
            elif lv < LEVELS:
                src, a = tot[lv]
                w = H * S // s
                t2 = src[:, a + g * w // 2:a + (g + 1) * w // 2].rearrange("p (n two) -> p n two", two=2)
                blocks = lambda t: t[:, n].rearrange("p (n two s) -> p n two s", two=2, s=s)
                N = HG * S // (2 * s)
                first = t2[:, :, 0].unsqueeze(2).to_broadcast([P, N, s])
                second = t2[:, :, 1].unsqueeze(2).to_broadcast([P, N, s])

                q_before = q_done[g]

                @block.vector
                def _(dve):
                    dve.wait_ge(*q_done[g])
                    dve.tensor_tensor(blocks(q)[:, :, 1, :], blocks(q)[:, :, 1, :], first, ALU.mult)
                    dst, b = tot[lv + 1]
                    dve.tensor_tensor(dst[:, b + g * w // 4:b + (g + 1) * w // 4], t2[:, :, 0], t2[:, :, 1], ALU.mult)\
                       .then_inc(*dq.up())

                @block.gpsimd
                def _(pool):
                    pool.wait_ge(*sc.made())
                    if lv >= 1:
                        pool.wait_ge(*q_before)
                    pool.wait_ge(*k_done[g])
                    pool.tensor_tensor(blocks(kk)[:, :, 0, :], blocks(kk)[:, :, 0, :], second, ALU.mult).then_inc(*dk.up())
            q_done[g], k_done[g] = dq.made(), dk.made()

    @block.tensor
    def _(pe):
        pe.wait_ge(*cp.made())
        for h in range(H):
            out = k.ps_acc[:, h // 2, (h % 2) * S:(h % 2 + 1) * S]
            pe.matmul(out, v[:, 0, h * P:(h + 1) * P], at0[:, h, :], start=(h % 2 == 0), stop=True, skip_group_check=True)
            mm = pe.matmul(out[:, P:S], v[:, 1, h * P:(h + 1) * P], at1[:, h, :], start=False, stop=True,
                           skip_group_check=True)
        mm.then_inc(*up("heads_ready"))

    @block.tensor
    def _(pe):
        pe.wait_ge(*k.gu_read[0])
        pe.wait_ge(*k.gu_read[1])
    for g in range(2):
        out = k.ps_acc[:, 2 * g:2 * g + 2, :].rearrange("p j c -> p (j c)")
        head_norm(k, out, [k.ps_gu[0][:, :], k.ps_gu[1][:, :]], q[:, g * HG * S:(g + 1) * HG * S],
                  kk[:, g * HG * S:(g + 1) * HG * S], g_norm,
                  gate[:, g * HG * S:(g + 1) * HG * S], HG * g, HG, P)
    k.gu_read = [made("head_sums_read")] * 2
    end_mixer(k)


def end_mixer(k):
    block, made, up = tools(k)

    @block.vector
    def _(dve):
        dve.wait_ge(*made("y_ready"))
        dve.wait_ge(*made("end_of_mixer"))
        dve.tensor_copy(k.tiny[:, 15:16], k.xn[:, 7, 0:1]).then_inc(*up("end_of_mixer"))
        dve.wait_ge(*made("end_of_mixer"))
        dve.tensor_copy(k.tiny[:, 14:15], k.xn[:, 7, 0:1]).then_inc(*up("acc_read"))


def mlstm(k, b_if, norm_g):
    block, made, up = tools(k)
    A = k.arena
    H, G = 4, 8
    CAP = 15.0
    q, kt = A("q", H * S), A("k", H * S)
    v = A("v", 2 * D).rearrange("p (k c) -> p k c", k=2)
    gate = A("gate", KD * S)
    rows = A("rows", 2 * G * P)
    r, mrow, em, den = (A(n, H * S) for n in ("r", "mrow", "em", "den"))
    w0, s0 = A("w0", H * S), A("s0", H * S)
    w1, s1 = A("w1", H * P), A("s1", H * P)
    m = lambda t, h: t[:, h * S:(h + 1) * S]
    mp = lambda t, h: t[:, h * P:(h + 1) * P]
    copy = lambda t, h: lambda act, ps: act.activation(m(t, h), ps[:, 0:S], ACT.Copy)

    @block.scalar
    def _(act):
        act.wait_ge(*made("y_ready"))
        act.wait_ge(*made("acc_read"))
    gates = A("gates", 112).rearrange("p (n c) -> p n c", c=8)
    raw = gates[:, 0:2, :].rearrange("p t c -> p (t c)")
    project(k, [("dve", True, 8, lambda dve, ps: dve.tensor_copy(gates[:, 0:2, :], ps[:, 0:S].rearrange(
        "p (t c) -> p t c", t=2)[:, :, 0:8]))], k.xn_hi, k.xn_lo, first=xn_parts(k))
    project(k, [("act", False, P, copy(q, h)) for h in range(H)] + [("act", False, P, copy(kt, h)) for h in range(H)],
            k.xn_hi, k.xn_lo)

    c8 = lambda n: gates[:, n, :]
    view = lambda t: t.rearrange("p (t h) -> p t h", t=2)
    fg, low, lsm, nlf, ig, rc, nb = (c8(n) for n in range(3, 10))

    @block.vector
    def _(dve):
        dve.wait_ge(*made("product_read_dve"))
        dve.tensor_tensor(gates[:, 0:2, :], gates[:, 0:2, :], b_if.unsqueeze(1).to_broadcast([P, 2, 8]), ALU.add)\
           .then_inc(*up("gate_step"))

    @block.scalar
    def _(act):
        act.wait_ge(*made("gate_step"))
        act.activation(raw, raw, ACT.Tanh, scale=1.0 / CAP).then_inc(*up("gate_exp"))

    @block.vector
    def _(dve):
        dve.wait_ge(*made("gate_exp"))
        dve.tensor_scalar(view(ig), gates[:, 0:2, 0:4], CAP, None, ALU.mult)
        dve.tensor_scalar(view(fg), gates[:, 0:2, 4:8], CAP, None, ALU.mult)
        dve.tensor_scalar(view(low), gates[:, 0:2, 4:8], -CAP, None, ALU.mult).then_inc(*up("gate_step"))
        dve.wait_ge(*made("gate_step"))
        dve.tensor_tensor(low, fg, low, ALU.min).then_inc(*up("gate_step"))

    @block.scalar
    def _(act):
        act.wait_ge(*made("gate_step"))
        act.activation(lsm, low, ACT.Exp).then_inc(*up("gate_exp"))
        act.wait_ge(*made("gate_exp"))
        act.activation(lsm, lsm, ACT.Ln, bias=1.0).then_inc(*up("gate_exp"))

    @block.vector
    def _(dve):
        dve.wait_ge(*made("gate_exp"))
        dve.tensor_scalar(low, fg, 0.0, None, ALU.min).then_inc(*up("gate_step"))
        dve.wait_ge(*made("gate_step"))
        dve.tensor_tensor(nlf, lsm, low, ALU.subtract).then_inc(*up("gate_step"))
        dve.wait_ge(*made("gate_step"))
        four = lambda t: t.rearrange("p (n c) -> p n c", n=G)
        dve.tensor_copy(four(rows[:, 0:G * P]), ig.unsqueeze(2).to_broadcast([P, G, P]))
        dve.tensor_copy(four(rows[:, G * P:2 * G * P]), nlf.unsqueeze(2).to_broadcast([P, G, P]))\
           .then_inc(*up("gates_spread"))
    rows_i, rows_f = rows[:, 0:G * P], rows[:, G * P:2 * G * P]
    upper, ident = con(k, "upper"), con(k, "ident")

    @block.tensor
    def _(pe):
        pe.wait_ge(*made("gates_spread"))
        pe.wait_ge(*made("x_ready"))
        pe.wait_ge(*made("acc_read"))
        pe.wait_ge(*made("misc_free"))
        for h in range(H):
            for base, with_i in ((2, False), (0, True)):
                out = k.ps_acc[:, base + h // 2, (h % 2) * S:(h % 2 + 1) * S]
                pe.matmul(out[:, 0:P], mp(rows_f, h), upper, start=(h % 2 == 0), stop=True, skip_group_check=True)
                pe.matmul(out[:, P:S], mp(rows_f, 4 + h), upper, start=False, stop=True, skip_group_check=True)
                pe.matmul(out[:, P:S], mp(rows_f, h), k.ones[:, :], start=False, stop=True, skip_group_check=True)
                if with_i:
                    for tt in range(2):
                        pe.matmul(out[:, tt * P:(tt + 1) * P], mp(rows_i, 4 * tt + h), ident, start=False, stop=True,
                                  skip_group_check=True)
        pe.matmul(k.ps_misc[:, 0:8], upper, nlf, start=True, stop=True, skip_group_check=True)
        pe.matmul(k.ps_misc[:, 4:8], k.ones[:, :], nlf[:, 0:4], start=False, stop=True, skip_group_check=True)\
          .then_inc(*up("gate_rows_ready"))

    @block.scalar
    def _(act):
        act.wait_ge(*made("gate_rows_ready"))
        act.activation(r, k.ps_acc[:, 0:2, :].rearrange("p j c -> p (j c)"), ACT.Copy).then_inc(*up("r_ready"))

    @block.vector
    def _(dve):
        dve.wait_ge(*made("gate_rows_ready"))
        dve.tensor_tensor(rc, k.ps_misc[:, 0:8], ig, ALU.add).then_inc(*up("misc_free"))
        dve.wait_ge(*made("r_ready"))
        for h in range(H):
            ins = dve.tensor_tensor_scan(m(mrow, h), m(r, h), m(r, h), 0.0, ALU.max, ALU.max)
        ins.then_inc(*up("M_ready"))
        dve.wait_ge(*made("M_ready"))
        dve.wait_ge(*made("misc_free"))
        dve.tensor_tensor(em, k.ps_acc[:, 2:4, :].rearrange("p j c -> p (j c)"), mrow, ALU.subtract).then_inc(*up("acc_read"))
        for h in range(H):
            dve.tensor_scalar(m(w0, h), m(mrow, h), rc[:, h:h + 1], 0.0, ALU.subtract, ALU.max)
            ins = dve.tensor_scalar(mp(w1, h), m(mrow, h)[:, P:S], rc[:, 4 + h:5 + h], 0.0, ALU.subtract, ALU.max)
        ins.then_inc(*up("decay_args"))

    @block.scalar
    def _(act):
        act.wait_ge(*made("decay_args"))
        act.activation(w0, w0, ACT.Exp, scale=-1.0)
        act.activation(w1, w1, ACT.Exp, scale=-1.0)
        act.activation(em, em, ACT.Exp).then_inc(*up("decay_exp"))

    @block.vector
    def _(dve):
        dve.wait_ge(*made("decay_exp"))
        diag0 = w0.rearrange("p (h t) -> p h t", h=H)[:, :, 0:P]
        diag1 = w1.rearrange("p (h t) -> p h t", h=H)
        for d in (diag0, diag1):
            ins = dve.tensor_tensor(d, d, upper.unsqueeze(1).to_broadcast([P, H, P]), ALU.mult)
        ins.then_inc(*up("decay_ready"))
    project(k, [("act", True, P, (lambda h: lambda act, ps: act.activation(
        v[:, :, h * P:(h + 1) * P], ps[:, 0:S].rearrange("p (k c) -> p k c", k=2), ACT.Copy))(h)) for h in range(KD)],
        k.xn_hi, k.xn_lo)
    project(k, [("act", False, P, (lambda h: lambda act, ps: act.activation(m(gate, h), ps[:, 0:S], ACT.Sigmoid))(h))
                for h in range(KD)], k.xn_hi, k.xn_lo)

    @block.tensor
    def _(pe):
        pe.wait_ge(*made("acc_read"))
        for h in range(H):
            pe.matmul(k.ps_acc[:, h // 2, (h % 2) * S:(h % 2 + 1) * S], m(kt, h)[:, 0:P], m(q, h),
                      start=(h % 2 == 0), stop=True, skip_group_check=True)
        for h in range(H):
            mm = pe.matmul(k.ps_acc[:, 2, h * P:(h + 1) * P], m(kt, h)[:, P:S], m(q, h)[:, P:S],
                           start=(h == 0), stop=True, skip_group_check=True)
        mm.then_inc(*up("scores_ready"))

    @block.vector
    def _(dve):
        dve.wait_ge(*made("scores_ready"))
        dve.wait_ge(*made("decay_ready"))
        dve.scalar_tensor_tensor(out=s0, in0=k.ps_acc[:, 0:2, :].rearrange("p j c -> p (j c)"), scalar=128.0 ** -0.5,
                                 in1=w0, op0=ALU.mult, op1=ALU.mult)
        dve.scalar_tensor_tensor(out=s1, in0=k.ps_acc[:, 2, :], scalar=128.0 ** -0.5, in1=w1, op0=ALU.mult, op1=ALU.mult)\
           .then_inc(*up("weights_ready"))

    @block.tensor
    def _(pe):
        pe.wait_ge(*made("weights_ready"))
        pe.wait_ge(*k.gu_read[0])
        pe.wait_ge(*k.gu_read[1])
        for h in range(H):
            out = k.ps_gu[h // 2][:, (h % 2) * S:(h % 2 + 1) * S]
            pe.matmul(out, k.ones[:, :], m(s0, h), start=(h % 2 == 0), stop=True, skip_group_check=True)
            mm = pe.matmul(out[:, P:S], k.ones[:, :], mp(s1, h), start=False, stop=True, skip_group_check=True)
        mm.then_inc(*up("den_ready"))
        for j in range(KD):
            out = k.ps_acc[:, j // 2, (j % 2) * S:(j % 2 + 1) * S]
            pe.matmul(out, v[:, 0, j * P:(j + 1) * P], m(s0, j // 2), start=(j % 2 == 0), stop=True, skip_group_check=True)
            mm = pe.matmul(out[:, P:S], v[:, 1, j * P:(j + 1) * P], mp(s1, j // 2), start=False, stop=True,
                           skip_group_check=True)
        mm.then_inc(*up("heads_ready"))

    @block.scalar
    def _(act):
        act.wait_ge(*made("den_ready"))
        for j in range(2):
            act.activation(den[:, j * 2 * S:(j + 1) * 2 * S], k.ps_gu[j][:, :], ACT.Abs).then_inc(*up("den_abs"))
        act.wait_ge(*made("heads_ready"))
        act.activation(rows, k.ps_acc[:, :, :].rearrange("p j c -> p (j c)"), ACT.Square).then_inc(*up("square_ready"))

    @block.vector
    def _(dve):
        dve.wait_ge(*made("den_abs"))
        dve.tensor_tensor(den, den, em, ALU.max).then_inc(*up("den_step"))
        dve.wait_ge(*made("den_step"))
        dve.scalar_tensor_tensor(out=den, in0=den, scalar=EPS, in1=den, op0=ALU.mult, op1=ALU.mult).then_inc(*up("den_step"))

    @block.tensor
    def _(pe):
        pe.wait_ge(*made("square_ready"))
        pe.wait_ge(*made("den_abs"))
        for h in range(H):
            for j in range(2):
                mm = pe.matmul(k.ps_gu[h // 2][:, (h % 2) * S:(h % 2 + 1) * S], k.ones[:, :], m(rows, 2 * h + j),
                               start=(h % 2 == 0 and j == 0), stop=(j == 1), skip_group_check=True)
        mm.then_inc(*up("sum_sq_ready"))

    @block.vector
    def _(dve):
        dve.wait_ge(*made("sum_sq_ready"))
        dve.wait_ge(*made("den_step"))
        for j in range(2):
            dve.scalar_tensor_tensor(out=den[:, j * 2 * S:(j + 1) * 2 * S], in0=k.ps_gu[j][:, :], scalar=1.0 / 256,
                                     in1=den[:, j * 2 * S:(j + 1) * 2 * S], op0=ALU.mult, op1=ALU.add)\
               .then_inc(*up("head_sums_read"))
    k.gu_read = [made("head_sums_read")] * 2

    @block.scalar
    def _(act):
        act.wait_ge(*made("head_sums_read"))
        act.activation(den, den, ACT.Ln).then_inc(*up("rs_step"))
        act.wait_ge(*made("rs_step"))
        act.activation(den, den, ACT.Exp, scale=-0.5).then_inc(*up("rs_step"))

    @block.vector
    def _(dve):
        dve.wait_ge(*made("rs_step"))
        for j in range(KD):
            ins = dve.scalar_tensor_tensor(out=k.xn[:, j, :], in0=k.ps_acc[:, j // 2, (j % 2) * S:(j % 2 + 1) * S],
                                           scalar=norm_g[:, j:j + 1], in1=m(den, j // 2), op0=ALU.mult, op1=ALU.mult)
        ins.then_inc(*up("norm_step"))
        dve.wait_ge(*made("norm_step"))
        flat = k.xn[:, :, :].rearrange("p m t -> p (m t)")
        dve.tensor_tensor(flat, flat, gate, ALU.mult).then_inc(*up("y_ready"))
    end_mixer(k)


def swa(k, gains, sinks):
    block, made, up = tools(k)
    A = k.arena
    q = A("q", 10 * S).rearrange("p (m t) -> p m t", m=10)
    sq = A("sq", 10 * S).rearrange("p (m t) -> p m t", m=10)
    rs = A("rs", 10 * S).rearrange("p (m t) -> p m t", m=10)
    kz = A("kz", 4 * S).rearrange("p (h t) -> p h t", h=4)
    v = A("v", 2 * S).rearrange("p (k c) -> p k c", k=2)

    @block.gpsimd
    def _(pool):
        pool.wait_ge(*made("y_ready"))
        pool.wait_ge(*made("acc_read"))
        pool.memset(kz, 0.0).then_inc(*up("kz_zero"))

    @block.scalar
    def _(act):
        act.wait_ge(*made("y_ready"))
        act.wait_ge(*made("acc_read"))
    project(k, [("act", False, P, (lambda m: lambda act, ps: act.activation(q[:, m, :], ps[:, 0:S], ACT.Copy))(m))
                for m in range(10)], k.xn_hi, k.xn_lo, first=xn_parts(k))
    project(k, [("act", True, P, (lambda h: lambda act, ps: act.activation(
        v[:, :, h * P:(h + 1) * P], ps[:, 0:S].rearrange("p (k c) -> p k c", k=2), ACT.Copy))(h)) for h in range(2)],
        k.xn_hi, k.xn_lo)

    @block.scalar
    def _(act):
        act.wait_ge(*made("product_read_act"))
        act.activation(sq, q, ACT.Square).then_inc(*up("square_ready"))
    sums = lambda m: (k.ps_acc[:, m // 2, :] if m < 8 else k.ps_misc[:, :])[:, (m % 2) * S:(m % 2 + 1) * S]

    @block.tensor
    def _(pe):
        pe.wait_ge(*made("square_ready"))
        pe.wait_ge(*made("acc_read"))
        pe.wait_ge(*made("x_ready"))
        pe.wait_ge(*made("misc_free"))
        for m in range(10):
            mm = pe.matmul(sums(m), con(k, "halves"), sq[:, m, :], start=(m % 2 == 0), stop=True, skip_group_check=True)
        mm.then_inc(*up("sum_sq_ready"))

    @block.vector
    def _(dve):
        dve.wait_ge(*made("sum_sq_ready"))
        dve.tensor_scalar(rs[:, 0:8, :].rearrange("p m t -> p (m t)"), k.ps_acc[:, :, :].rearrange("p j c -> p (j c)"),
                          1.0 / 64, EPS, ALU.mult, ALU.add).then_inc(*up("acc_read"))
        dve.tensor_scalar(rs[:, 8:10, :].rearrange("p m t -> p (m t)"), k.ps_misc[:, :], 64 * EPS, None, ALU.add)\
           .then_inc(*up("misc_free"))

    @block.scalar
    def _(act):
        act.wait_ge(*made("misc_free"))
        act.activation(rs, rs, ACT.Ln).then_inc(*up("rs_step"))
        act.wait_ge(*made("rs_step"))
        act.activation(rs, rs, ACT.Exp, scale=-0.5).then_inc(*up("rs_step"))

    @block.vector
    def _(dve):
        dve.wait_ge(*made("rs_step"))
        dve.wait_ge(*made("kz_zero"))
        for h in range(4):
            b = slice(64 * (h % 2), 64 * (h % 2) + 64)
            dve.scalar_tensor_tensor(out=kz[b, h, :], in0=q[b, 8 + h // 2, :], scalar=gains[b, 1:2],
                                     in1=rs[b, 8 + h // 2, :], op0=ALU.mult, op1=ALU.mult)
        dve.scalar_tensor_tensor(out=q[:, 0:8, :], in0=q[:, 0:8, :], scalar=gains[:, 0:1], in1=rs[:, 0:8, :],
                                 op0=ALU.mult, op1=ALU.mult).then_inc(*up("att_operands"))
    for g in range(4):
        key = lambda h: 2 * (g // 2) + h % 2
        name = [HEADS_SWA[4 * g + h] for h in range(4)]
        attention(k, lambda h, tq: q[:, 2 * g + h // 2, tq * P:(tq + 1) * P], lambda h, K: kz[:, key(h), 0:K],
                  lambda kt, h: v[:, kt, key(h) * 64:(key(h) + 1) * 64], P, 1.0,
                  lambda tq: con(k, "distance", P if tq == 0 else 0), None, 2 * g,
                  slopes=[-2.0 ** (-8.0 * (n + 1) / 16) for n in name], sink=sinks[:, 4 * g:4 * g + 4])
    end_mixer(k)


HEADS_SWA = [4 * (2 * (j // 4) + half) + j % 4 for j in range(8) for half in range(2)]


def ffn_chunks(w_gu, w_down):
    g, u, d = as_columns(w_gu[:, :FF]), as_columns(w_gu[:, FF:]), as_rows(w_down)
    out = []
    for t in range(FT):
        out += [g[t], u[t]] + ([d[t - 1]] if t else [])
    return [np.stack(out + [d[FT - 1]])]


def ple_chunks(w_gate, w_proj):
    return [as_rows(w_proj), as_columns(w_gate)]


def hgrn_chunks(w_in, w_out):
    return [as_columns(w_in), as_columns(w_out)]


def mlstm_chunks(w_qkvo, w_if, w_out):
    gates = np.concatenate([w_if, np.zeros((D, P - w_if.shape[1]), w_if.dtype)], 1)
    return [as_columns(gates), as_columns(w_qkvo), as_columns(w_out)]


def swa_chunks(w_qkv, w_o):
    q = w_qkv[:, :1024].reshape(D, 16, 64)[:, HEADS_SWA, :].reshape(D, 1024)
    o = w_o.reshape(16, 64, D)[HEADS_SWA, :, :].reshape(1024, D)
    return [as_columns(np.concatenate([q, w_qkv[:, 1024:]], 1)), as_columns(o)]


def last_output(k, out):
    @k.block.sync
    def _(sp):
        sp.wait_ge(*k("x_ready").made())
        sp.dma_start(out, k.x[:, :, :]).then_inc(*k("stored").up_dma())
        sp.wait_ge(*k("stored").made())


VEC_FIRST, VEC_SECOND = 68, 4 * KD
N_VEC = 2 * VEC_FIRST + KD + 4 * VEC_SECOND + 4 * KD + 2 + (8 + KD) + (2 + 16)


def build(nc, io, out, n_chunks):
    with ExitStack() as ctx:
        k = setup(nc, ctx, io, n_chunks, N_VEC, N_CONST_1)
        start(k, io)
        t5_bias(k, io)
        at = [0]

        def vec(n):
            at[0] += n
            return k.vec[:, at[0] - n:at[0]]

        for _ in range(2):
            first_layer(k, vec(VEC_FIRST))
        norm(k, vec(KD), to_x=True)
        load_p(k, io)
        gains = [vec(VEC_SECOND) for _ in range(4)]
        bounds, hg_norm, ml, sw = vec(4 * KD), vec(2), vec(8 + KD), vec(18)
        lower_bounds(k, bounds)
        for layer in range(4):
            gain = lambda n: gains[layer][:, n * KD:(n + 1) * KD]
            norm(k, gain(0))
            ffn(k)
            norm(k, gain(1))
            k.arena.clear()
            if layer % 3 == 0:
                j = layer // 3
                hgrn(k, hg_norm[:, j:j + 1], k.lb if layer else None)
            elif layer == 1:
                mlstm(k, ml[:, 0:8], ml[:, 8:8 + KD])
            else:
                swa(k, sw[:, 0:2], sw[:, 2:18])
            project_out(k)
            norm(k, gain(2))
            ffn(k)
            norm(k, gain(3))
            ple(k, layer)
        assert k.used == n_chunks
        last_output(k, out)


def kernel(x, norm_w, w_in, mla_q_norm, mla_w_uq, mla_kv_norm, mla_w_ukv, gdn_conv_w, gdn_A_log, gdn_dt_bias,
           gdn_norm_w, w_out, t5_table, final_norm_w, p_2, norm_gains_2, w_ffn_gu_2, w_ffn_down_2, w_ple_gate_2,
           w_ple_proj_2, hg_lower_bounds_2, hg_w_in_2, hg_g_norm_2, hg_w_out_2, ml_w_qkvo_2, ml_w_if_2, ml_b_if_2,
           ml_norm_2, ml_w_out_2, sw_w_qkv_2, sw_q_norm_2, sw_k_norm_2, sw_sinks_2, sw_w_o_2):
    import concourse.bacc as _bacc
    from concourse.bass_utils import run_bass_kernel_spmd as _run

    (x, norm_w, w_in, mla_q_norm, mla_w_uq, mla_kv_norm, mla_w_ukv, gdn_conv_w, gdn_A_log, gdn_dt_bias,
     gdn_norm_w, w_out, t5_table, final_norm_w, p_2, norm_gains_2, w_ffn_gu_2, w_ffn_down_2, w_ple_gate_2,
     w_ple_proj_2, hg_lower_bounds_2, hg_w_in_2, hg_g_norm_2, hg_w_out_2, ml_w_qkvo_2, ml_w_if_2, ml_b_if_2,
     ml_norm_2, ml_w_out_2, sw_w_qkv_2, sw_q_norm_2, sw_k_norm_2, sw_sinks_2, sw_w_o_2) = (np.asarray(a) for a in (
         x, norm_w, w_in, mla_q_norm, mla_w_uq, mla_kv_norm, mla_w_ukv, gdn_conv_w, gdn_A_log, gdn_dt_bias,
         gdn_norm_w, w_out, t5_table, final_norm_w, p_2, norm_gains_2, w_ffn_gu_2, w_ffn_down_2, w_ple_gate_2,
         w_ple_proj_2, hg_lower_bounds_2, hg_w_in_2, hg_g_norm_2, hg_w_out_2, ml_w_qkvo_2, ml_w_if_2, ml_b_if_2,
         ml_norm_2, ml_w_out_2, sw_w_qkv_2, sw_q_norm_2, sw_k_norm_2, sw_sinks_2, sw_w_o_2))

    chunks, vecs = [], []
    for n in range(2):
        chunks += first_chunks(w_in[n], mla_w_uq[n], mla_w_ukv[n], w_out[n])
        vecs += first_vectors(norm_w[n], mla_q_norm[n], mla_kv_norm[n], gdn_conv_w[n], gdn_A_log[n], gdn_dt_bias[n],
                              gdn_norm_w[n])
    vecs += [columns(final_norm_w)]
    for n in range(4):
        chunks += ffn_chunks(w_ffn_gu_2[n, 0], w_ffn_down_2[n, 0])
        chunks += (hgrn_chunks(hg_w_in_2[n // 3], hg_w_out_2[n // 3]) if n % 3 == 0 else
                   mlstm_chunks(ml_w_qkvo_2[0], ml_w_if_2[0], ml_w_out_2[0]) if n == 1 else
                   swa_chunks(sw_w_qkv_2[0], sw_w_o_2[0]))
        chunks += ffn_chunks(w_ffn_gu_2[n, 1], w_ffn_down_2[n, 1])
        chunks += ple_chunks(w_ple_gate_2[n], w_ple_proj_2[n])
        vecs += [columns(norm_gains_2[n, i]) for i in range(4)]
    twice = lambda v: np.concatenate([v, v]).reshape(P, 1)
    vecs += [columns(hg_lower_bounds_2[n]) for n in range(4)] + [columns(hg_g_norm_2[n]) for n in range(2)]
    vecs += [spread(ml_b_if_2[0]), columns(ml_norm_2[0])]
    vecs += [twice(sw_q_norm_2[0]), twice(sw_k_norm_2[0]), spread(sw_sinks_2[0][HEADS_SWA])]

    arrays = {
        "w": np.concatenate(chunks),
        "x": np.ascontiguousarray(x[0].T.reshape(KD, P, S).transpose(1, 0, 2)),
        "vec": np.ascontiguousarray(np.concatenate(vecs, 1)),
        "p": np.ascontiguousarray(p_2[:, 0].transpose(0, 2, 1).reshape(4, 2, P, S).transpose(2, 0, 1, 3)),
        "const": constants(),
        "t5": np.ascontiguousarray(t5_table),
    }
    nc = _bacc.Bacc("TRN2", target_bir_lowering=False, num_devices=1)
    io = {n: nc.dram_tensor(f"in_{n}_dram", a.shape, mybir.dt.from_np(a.dtype), kind="ExternalInput").ap()
          for n, a in arrays.items()}
    io["scratch"] = nc.dram_tensor("distance_rows", [4, P, 2 * S], F32, kind="Internal").ap()
    out = nc.dram_tensor("out_0_dram", [P, KD, S], F32, kind="ExternalOutput").ap()
    build(nc, io, out, arrays["w"].shape[0])
    r = _run(nc, [{f"in_{n}_dram": a for n, a in arrays.items()}], core_ids=[0])
    y = r.results[0]["out_0_dram"]
    return np.ascontiguousarray(y.transpose(2, 1, 0)).reshape(1, S, D)
```

```python
import numpy as np
from contextlib import ExitStack

import concourse.bass as bass
from concourse import mybir

F32 = mybir.dt.float32
F32R = mybir.dt.float32r
ALU = mybir.AluOpType
ACT = mybir.ActivationFunctionType
AX = mybir.AxisListType

P = 128
S = 256
TT = S // P
D = 1024
KD = D // P
FF = 2816
FT = FF // P
CH = 1024
NS = 6
AHEAD = NS - 1
EPS = 1e-6
ARENA = 17900


class Signal:

    def __init__(self, k, name):
        self.sem = k.ctx.enter_context(k.nc.semaphore(name))
        self.n = 0

    def up(self):
        self.n += 1
        return self.sem, 1

    def up_dma(self):
        self.n += 16
        return self.sem, 16

    def made(self, back=0):
        return self.sem, max(self.n - back, 0)

    def at(self, value):
        return self.sem, value


class Kernel:

    def __init__(self, nc, ctx, n_chunks):
        self.nc, self.ctx = nc, ctx
        self.n_chunks = n_chunks
        self.used = 0
        self.hi_split = 0
        self.lo_split = 0
        self.signals = {}

    def sb(self, name, shape, dt=F32):
        return self.ctx.enter_context(self.nc.sbuf_tensor(name, shape, dt))

    def __call__(self, name):
        if name not in self.signals:
            self.signals[name] = Signal(self, name)
        return self.signals[name]

    def load(self, sp, c, i=0):
        s = c % NS
        if c >= NS:
            sp.wait_ge(self.w_lo_ready.sem, c - NS + 1 + i * NS)
        sp.dma_start(self.w_raw[:, s, :], self.w_dram[c + i * NS, :, :]).then_inc(self.w_loaded[s].sem, 16)

    def hi(self, act, c, i=0):
        if c >= self.n_chunks:
            return
        s = c % NS
        act.wait_ge(self.w_loaded[s].sem, 16 * (c // NS + 1) + i * 16)
        if c >= NS:
            act.wait_ge(self.chunk_done.sem, c - NS + 1 + i * NS)
        act.activation(self.w_hi[:, s, :], self.w_raw[:, s, :], ACT.Copy).then_inc(self.w_hi_ready.sem, 1)

    def lo(self, dve, c, i=0):
        if c >= self.n_chunks:
            return
        s = c % NS
        dve.wait_ge(self.w_hi_ready.sem, c + 1 + i * NS)
        dve.tensor_tensor(self.w_lo[:, s, :], self.w_raw[:, s, :], self.w_hi[:, s, :], ALU.subtract)\
           .then_inc(self.w_lo_ready.sem, 1)

    def hi_for(self, act, c):
        self.hi(act, c + AHEAD)

    def lo_for(self, dve, c):
        self.lo(dve, c + AHEAD)

    def wait_chunk(self, pe, c, i=0):
        pe.wait_ge(self.w_lo_ready.sem, c + 1 + i * NS)

    def products(self, pe, out, s, j0, width, rhs_hi, rhs_lo, first, last, start=None):
        w_hi, w_lo = self.w_hi[:, s, j0:j0 + width], self.w_lo[:, s, j0:j0 + width]
        start = first if start is None else start
        pe.matmul(out, w_hi, rhs_hi, start=start, stop=False, skip_group_check=True)
        pe.matmul(out, w_hi, rhs_lo, start=False, stop=False, skip_group_check=True)
        return pe.matmul(out, w_lo, rhs_hi, start=False, stop=last, skip_group_check=True)

    def rows(self, pe, out, s, j0, width, lhs_hi, lhs_lo, first, last, start=None):
        w_hi, w_lo = self.w_hi[:, s, j0:j0 + width], self.w_lo[:, s, j0:j0 + width]
        start = first if start is None else start
        pe.matmul(out, lhs_hi, w_hi, start=start, stop=False, skip_group_check=True)
        pe.matmul(out, lhs_hi, w_lo, start=False, stop=False, skip_group_check=True)
        return pe.matmul(out, lhs_lo, w_hi, start=False, stop=last, skip_group_check=True)


class Arena:

    def __init__(self, buf, size):
        self.buf, self.size = buf, size
        self.clear()

    def clear(self):
        self.at, self.parts = 0, {}

    def __call__(self, name, width):
        if name not in self.parts:
            assert self.at + width <= self.size, (name, self.at + width)
            self.parts[name] = self.buf[:, self.at:self.at + width]
            self.at += width
        return self.parts[name]


def norm_to_x(k, gain):
    norm(k, gain)
    rstd(k)
    n = k.norms

    @k.block.vector
    def _(dve):
        dve.wait_ge(*k("rstd_ready").at(n))
        dve.wait_ge(*k("xn_lo_ready").made())
        dve.wait_ge(*k("square_ready").made())
        for m in range(KD):
            dve.scalar_tensor_tensor(out=k.x[:, m, :], in0=k.x[:, m, :], scalar=gain[:, m:m + 1],
                                     in1=k.rstd[:, :], op0=ALU.mult, op1=ALU.mult).then_inc(*k("x_ready").up())
    k.x_at = [k("x_ready").made(KD - 1 - m) for m in range(KD)]


def norm(k, gain):
    block = k.block
    xh, xl, sq = k("xn_hi_ready"), k("xn_lo_ready"), k("square_ready")
    sq0 = sq.n
    h0, free, at, late = xh.n, k.xn_free, k.x_at, k.late
    hi, lo, x = k.xn_hi, k.xn_lo, k.x

    @block.scalar
    def _(act):
        act.wait_ge(*k.chunk_done.at(free or k.used))
        for m in range(KD):
            act.wait_ge(*at[m])
            act.activation(hi[:, m, :], x[:, m, :], ACT.Copy, scale=gain[:, m:m + 1]).then_inc(*xh.up())
        if late is not None:
            k.hi(act, late)

    @block.vector
    def _(dve):
        for m in range(KD):
            dve.wait_ge(*xh.at(h0 + m + 1))
            dve.scalar_tensor_tensor(out=lo[:, m, :], in0=x[:, m, :], scalar=gain[:, m:m + 1], in1=hi[:, m, :],
                                     op0=ALU.mult, op1=ALU.subtract).then_inc(*xl.up())
        if late is not None:
            k.lo(dve, late)
        dve.wait_ge(*sq.at(sq0 + KD // 2))
        dve.tensor_tensor(k.xn[:, 0:KD // 2, :], k.xn[:, 0:KD // 2, :], k.xn[:, KD // 2:KD, :], ALU.add)\
           .then_inc(k("squares_folded").sem, 1)
    k.xn_at = [xl.made(KD - 1 - m) for m in range(KD)]

    @block.gpsimd
    def _(pool):
        for j in range(KD // 2):
            pool.wait_ge(*at[2 * j])
            pool.wait_ge(*at[2 * j + 1])
            pair = x[:, 2 * j:2 * j + 2, :]
            pool.tensor_tensor(k.xn[:, 2 * j:2 * j + 2, :], pair, pair, ALU.mult).then_inc(*sq.up())
    k.norms += 1
    k.xn_free = k.late = None


def sum_squares(k, pe):
    n = k.norms
    pe.wait_ge(*k("misc_free").made())
    pe.wait_ge(*k("squares_folded").at(n))
    for m in range(KD // 2):
        for tt in range(TT):
            mm = pe.matmul(k.ps_sum[:, tt:tt + 1], k.xn[:, m, tt * P:(tt + 1) * P], k.ones[:, 0:1],
                           start=(m == 0 and tt == 0), stop=(m == KD // 2 - 1), skip_group_check=True)
    mm.then_inc(k("sum_sq_col").sem, 1)


def root_in(k, dve):
    n = k.norms
    dve.wait_ge(*k("sum_sq_col").at(n))
    dve.tensor_scalar(k.rcol[:, :], k.ps_sum[:, 0:TT], 1.0 / D, EPS, ALU.mult, ALU.add).then_inc(k("mean_sq_col").sem, 1)
    dve.wait_ge(*k("mean_sq_col").at(n))
    dve.reciprocal(k.rcol[:, :], k.rcol[:, :]).then_inc(k("root_in").sem, 1)


def root(k, act):
    n = k.norms
    act.wait_ge(*k("root_in").at(n))
    act.activation(k.rcol[:, :], k.rcol[:, :], ACT.Sqrt).then_inc(k("rstd_col").sem, 1)


def spread_root(k, dve):
    n = k.norms
    dve.wait_ge(*k("rstd_col").at(n))
    dve.tensor_copy(k.rspread[:, :, :], k.rcol[:, :].unsqueeze(2).to_broadcast([P, TT, P]))\
       .then_inc(k("rstd_spread").sem, 1)


def rstd_rows(k, pe):
    n = k.norms
    pe.wait_ge(*k("rstd_spread").at(n))
    if n == 1:
        pe.wait_ge(*k("constants_loaded").made())
    for tt in range(TT):
        mm = pe.matmul(k.ps_sum[:, tt * P:(tt + 1) * P], k.rspread[:, tt, :], k.ident, start=(tt == 0), stop=True,
                       skip_group_check=True)
    mm.then_inc(k("rstd_rows").sem, 1)


def take_rstd(k, dve):
    n = k.norms
    dve.wait_ge(*k("rstd_rows").at(n))
    dve.tensor_copy(k.rstd[:, :], k.ps_sum[:, 0:S]).then_inc(k("rstd_ready").sem, 1)


def rstd(k):
    block = k.block

    @block.tensor
    def _(pe):
        sum_squares(k, pe)

    @block.vector
    def _(dve):
        root_in(k, dve)

    @block.scalar
    def _(act):
        root(k, act)

    @block.vector
    def _(dve):
        spread_root(k, dve)

    @block.tensor
    def _(pe):
        rstd_rows(k, pe)

    @block.vector
    def _(dve):
        take_rstd(k, dve)


def ffn(k):
    block = k.block
    c0 = k.used
    silu, hr, hh, hl, sc = k("silu_ready"), k("h_ready"), k("h_hi_ready"), k("h_lo_ready"), k("gu_scaled")
    b0 = silu.n
    xn_at = k.xn_at
    LOOPS = (FT - 4) // 2

    def at_g(t):
        return c0 if t == 0 else c0 + 3 * t - 1

    def tiles(eng, tile, last):
        for t in range(3):
            tile(t, 0)
        with eng.Fori(0, LOOPS) as i:
            tile(3, i)
            tile(4, i)
        tile(FT - 1, 0)
        last()

    def part(a, b, t):
        return a[:, t % 2, :]

    @block.tensor
    def _(pe):
        def down(t, c, i):
            pe.wait_ge(*hl.at(b0 + t + 1 + 2 * i))
            k.wait_chunk(pe, c, i)
            for m in range(KD):
                mm = k.products(pe, k.ps_acc[:, m // 2, (m % 2) * S:(m % 2 + 1) * S], c % NS, m * P, P,
                                k.h_hi[:, t % 2, :], k.h_lo[:, t % 2, :], False, t == FT - 1,
                                start=(t == 0 and m % 2 == 0))
                if t == FT - 1 and m % 2 and m < KD - 1:
                    mm.then_inc(k("acc_bank_done").sem, 1)
            mm.then_inc(k.chunk_done.sem, 1)

        def tile(t, i):
            if t >= 2:
                pe.wait_ge(*hr.at(b0 + t - 1 + 2 * i))
            for n, c in enumerate((at_g(t), at_g(t) + 1)):
                k.wait_chunk(pe, c, i)
                for j in range(KD):
                    if t == 0 and n == 0:
                        pe.wait_ge(*xn_at[j])
                    mm = k.products(pe, k.ps_gu[t % 2][:, n * S:(n + 1) * S], c % NS, j * P, P,
                                    k.xn_hi[:, j, :], k.xn_lo[:, j, :], False, j == KD - 1,
                                    start=(n == 0 and j == 0))
                mm.then_inc(k.chunk_done.sem, 1)
                if t == 0 and n == 1:
                    sum_squares(k, pe)
                if t == 1 and n == 0:
                    rstd_rows(k, pe)
            if t >= 1:
                down(t - 1, at_g(t) + 2, i)

        tiles(pe, tile, lambda: down(FT - 1, c0 + 3 * FT - 1, 0))

    @block.scalar
    def _(act):
        def tile(t, i):
            g = at_g(t)
            k.hi(act, g + AHEAD, i)
            k.hi(act, g + 1 + AHEAD, i)
            if t == 0:
                root(k, act)
            act.wait_ge(*sc.at(b0 + t + 1 + 2 * i))
            if t >= 2:
                act.wait_ge(*hr.at(b0 + t - 1 + 2 * i))
            act.activation(k.s[:, t % 2, :], k.ps_gu[t % 2][:, 0:S], ACT.Silu).then_inc(silu.sem, 1)
            if t >= 1:
                k.hi(act, g + 2 + AHEAD, i)
            act.wait_ge(*hr.at(b0 + t + 1 + 2 * i))
            act.activation(k.h_hi[:, t % 2, :], k.h[:, t % 2, :], ACT.Copy).then_inc(hh.sem, 1)

        tiles(act, tile, lambda: None)

    @block.vector
    def _(dve):
        def tile(t, i):
            g = at_g(t)
            k.lo(dve, g + AHEAD, i)
            k.lo(dve, g + 1 + AHEAD, i)
            if t == 0:
                root_in(k, dve)
                spread_root(k, dve)
                take_rstd(k, dve)
                dve.wait_ge(*k("rstd_ready").at(k.norms))
            dve.wait_ge(k.chunk_done.sem, g + 2 + i * NS)
            gu = k.ps_gu[t % 2][:, :].rearrange("p (n t) -> p n t", n=2)
            dve.tensor_tensor(gu, gu, k.rstd[:, :].unsqueeze(1).to_broadcast([P, 2, S]), ALU.mult).then_inc(sc.sem, 1)
            dve.wait_ge(*silu.at(b0 + t + 1 + 2 * i))
            if t >= 2:
                dve.wait_ge(*hl.at(b0 + t - 1 + 2 * i))
            dve.tensor_tensor(k.h[:, t % 2, :], k.s[:, t % 2, :], k.ps_gu[t % 2][:, S:2 * S], ALU.mult)\
               .then_inc(hr.sem, 1)
            if t >= 1:
                k.lo(dve, g + 2 + AHEAD, i)
            dve.wait_ge(*hh.at(b0 + t + 1 + 2 * i))
            dve.tensor_tensor(k.h_lo[:, t % 2, :], k.h[:, t % 2, :], k.h_hi[:, t % 2, :], ALU.subtract)\
               .then_inc(hl.sem, 1)

        tiles(dve, tile, lambda: None)

    for s in (silu, hr, hh, hl, sc):
        s.n += FT
    k("acc_bank_done").n += KD // 2 - 1
    k.used += 3 * FT
    k.late = k.used - 1 + AHEAD
    k.xn_free = k.used - 2
    residual(k, 0.5)


def residual(k, scale):
    xr = k("x_ready")

    @k.block.vector
    def _(dve):
        for j in range(KD // 2):
            if j < KD // 2 - 1:
                dve.wait_ge(*k("acc_bank_done").made(KD // 2 - 2 - j))
            else:
                dve.wait_ge(*k.chunk_done.at(k.used))
            dve.scalar_tensor_tensor(out=k.x[:, 2 * j:2 * j + 2, :], in0=k.ps_acc[:, j, :].rearrange("p (m t) -> p m t", m=2),
                                     scalar=scale, in1=k.x[:, 2 * j:2 * j + 2, :],
                                     op0=ALU.mult, op1=ALU.add).then_inc(*xr.up())
    k.x_at = [xr.made(KD // 2 - 1 - m // 2) for m in range(KD)]


def ple(k, layer):
    block = k.block
    c0 = k.used
    xr, ph, pl = k("x_ready"), k("p_hi_ready"), k("p_lo_ready")
    gate, prod = k("ple_gate_ready"), k("ple_gated")
    g0, r0 = gate.n, prod.n

    xn_at, scaled = k.xn_at, k("ple_scaled")
    z0, x0 = scaled.n, xr.n
    gc = lambda m: c0 + m + (2 if m >= 2 else 0)
    p_hi, p_lo = k.h_hi[:, 0:2, :], k.h_lo[:, 0:2, :]

    @block.gpsimd
    def _(pool):
        pool.wait_ge(*k("p_loaded").made())
        pool.wait_ge(*k.chunk_done.at(c0))
        pool.tensor_copy(p_hi[:, :, :], k.p_all[:, layer, :, :]).then_inc(*ph.up())
        pool.wait_ge(*ph.made())
        pool.tensor_tensor(p_lo[:, :, :], k.p_all[:, layer, :, :], p_hi[:, :, :], ALU.subtract).then_inc(*pl.up())

    @block.tensor
    def _(pe):
        def gate_tile(m):
            c = gc(m)
            k.wait_chunk(pe, c)
            if m < 2:
                pe.wait_ge(*prod.at(r0))
            else:
                pe.wait_ge(*gate.at(g0 + m - 1))
            for j in range(KD):
                if m == 0:
                    pe.wait_ge(*xn_at[j])
                mm = k.products(pe, k.ps_gu[m % 2][:, 0:S], c % NS, j * P, P,
                                k.xn_hi[:, j, :], k.xn_lo[:, j, :], j == 0, j == KD - 1)
            mm.then_inc(k.chunk_done.sem, 1)

        gate_tile(0)
        sum_squares(k, pe)
        gate_tile(1)
        pe.wait_ge(*pl.made())
        pe.wait_ge(*xr.made(xr.n - x0))
        for j in range(2):
            c = c0 + 2 + j
            k.wait_chunk(pe, c)
            for m in range(KD):
                mm = k.products(pe, k.ps_acc[:, m // 2, (m % 2) * S:(m % 2 + 1) * S], c % NS, m * P, P,
                                p_hi[:, j, :], p_lo[:, j, :], False, j == 1, start=(j == 0 and m % 2 == 0))
            mm.then_inc(k.chunk_done.sem, 1)
            if j == 0:
                rstd_rows(k, pe)
        for m in range(2, KD):
            gate_tile(m)

    @block.scalar
    def _(act):
        for j in range(2):
            k.hi(act, c0 + j + AHEAD)
        root(k, act)
        for m in range(KD):
            if m >= 1:
                k.hi(act, c0 + 1 + m + AHEAD)
            act.wait_ge(*scaled.at(z0 + m + 1))
            if m >= 2:
                act.wait_ge(*prod.at(r0 + m - 1))
            act.activation(k.s[:, m % 2, :], k.ps_gu[m % 2][:, 0:S], ACT.Sigmoid).then_inc(*gate.up())

    @block.vector
    def _(dve):
        for j in range(2):
            k.lo(dve, c0 + j + AHEAD)
        root_in(k, dve)
        spread_root(k, dve)
        take_rstd(k, dve)
        dve.wait_ge(*k("h_hi_ready").made())
        dve.wait_ge(*k("rstd_ready").at(k.norms))
        for m in range(KD):
            out = k.ps_gu[m % 2][:, 0:S]
            dve.wait_ge(*k.chunk_done.at(gc(m) + 1))
            dve.tensor_tensor(out, out, k.rstd[:, :], ALU.mult).then_inc(*scaled.up())
            if m >= 1:
                k.lo(dve, c0 + 1 + m + AHEAD)
            dve.wait_ge(*gate.at(g0 + m + 1))
            if m == 0:
                dve.wait_ge(*k.chunk_done.at(c0 + 4))
            if m >= 2:
                dve.wait_ge(*xr.at(x0 + m - 1))
            dve.tensor_tensor(k.h[:, m % 2, :], k.s[:, m % 2, :],
                              k.ps_acc[:, m // 2, (m % 2) * S:(m % 2 + 1) * S], ALU.mult).then_inc(*prod.up())

    @block.gpsimd
    def _(pool):
        for m in range(KD):
            pool.wait_ge(*prod.at(r0 + m + 1))
            pool.tensor_tensor(k.x[:, m, :], k.x[:, m, :], k.h[:, m % 2, :], ALU.add).then_inc(*xr.up())
    k.x_at = [xr.made(KD - 1 - m) for m in range(KD)]
    k.used += 2 + KD
    k.late = k.used - 1 + AHEAD


def load_p(k, io):
    @k.block.scalar
    def _(act):
        act.wait_ge(*k("logits_ready").made())
        act.dma_start(k.p_all[:, :, :, :], io["p"]).then_inc(*k("p_loaded").up_dma())


def setup(nc, ctx, io, n_chunks, n_vec, n_const=1):
    k = Kernel(nc, ctx, n_chunks)
    k.w_dram = io["w"]
    k.w_raw = k.sb("w_raw", [P, NS, CH])
    k.w_hi = k.sb("w_hi", [P, NS, CH], F32R)
    k.w_lo = k.sb("w_lo", [P, NS, CH], F32R)
    k.x = k.sb("x_res", [P, KD, S])
    k.xn = k.sb("xn", [P, KD, S])
    k.xn_hi = k.sb("xn_hi", [P, KD, S], F32R)
    k.xn_lo = k.sb("xn_lo", [P, KD, S], F32R)
    k.rstd = k.sb("rstd", [P, S])
    k.rcol = k.sb("rstd_columns", [P, TT])
    k.rspread = k.sb("rstd_column_spread", [P, TT, P])
    k.norms = 0
    k.xn_free = None
    k.s = k.sb("silu", [P, 2, S])
    k.h = k.sb("h", [P, 2, S])
    k.h_hi = k.sb("h_hi", [P, 3, S], F32R)
    k.h_lo = k.sb("h_lo", [P, 3, S], F32R)
    k.lat_hi, k.lat_lo = k.h_hi, k.h_lo
    k.vec = k.sb("vec", [P, n_vec])
    k.ones = k.sb("ones", [P, P])
    k.p_all = k.sb("p_all", [P, 4, 2, S])
    k.t5b = k.p_all[:, :, :, :].rearrange("p a b t -> p (a b) t").rearrange("p (q h) t -> p q h t", q=2)
    k.const = k.sb("const", [P, n_const])
    k.t5 = k.sb("t5", [33, 4])
    k.ba = k.sb("ba", [P, 16])
    k.tiny = k.sb("tiny", [P, 16])
    k.lbw = k.sb("bounds", [P, 8 * KD])
    k.arena = Arena(k.sb("arena", [P, ARENA]), ARENA)
    k.bank = k.side_bank = 0
    k.y_at = {}
    k.late = None
    ps = [ctx.enter_context(nc.psum_tensor(f"ps_gu{i}", [P, 2 * S], F32)) for i in range(2)]
    k.ps_gu = ps
    k.ps_acc = ctx.enter_context(nc.psum_tensor("ps_acc", [P, 4, 2 * S], F32))
    k.ps_sum = ctx.enter_context(nc.psum_tensor("ps_sum", [P, 2 * S], F32))
    k.ps_misc = ctx.enter_context(nc.psum_tensor("ps_misc", [P, 2 * S], F32))
    k.w_loaded = [k(f"w_loaded{s}") for s in range(NS)]
    k.w_hi_ready, k.w_lo_ready, k.chunk_done = k("w_hi_ready"), k("w_lo_ready"), k("chunk_done")
    k.gu_read = [k("product_read_act").made()] * 2
    k.side_read = [k("product_read_dve").made()] * 2
    k.block = ctx.enter_context(nc.Block())
    return k


def start(k, io):
    block = k.block
    n = k.n_chunks

    @block.sync
    def _(sp):
        sp.dma_start(k.x[:, :, :], io["x"]).then_inc(*k("x_loaded").up_dma())
        sp.dma_start(k.vec[:, :], io["vec"]).then_inc(*k("gains_loaded").up_dma())
        for c in range(2):
            k.load(sp, c)
        sp.dma_start(k.const[:, :], io["const"]).then_inc(*k("constants_loaded").up_dma())
        sp.dma_start(k.t5[0:32, :], io["t5"]).then_inc(*k("t5_table_loaded").up_dma())
        for c in range(2, NS):
            k.load(sp, c)
        with sp.Fori(0, n // NS - 1) as i:
            for c in range(NS, 2 * NS):
                k.load(sp, c, i)
        for c in range(n // NS * NS, n):
            k.load(sp, c)

    @block.gpsimd
    def _(pool):
        pool.memset(k.ones[:, :], 1.0).then_inc(*k("ones_ready").up())

    k.x_at = [k("x_loaded").made()] * KD

    @block.scalar
    def _(act):
        act.wait_ge(*k("gains_loaded").made())


def first_splits(k):
    block = k.block

    @block.scalar
    def _(act):
        for c in range(AHEAD):
            k.hi(act, c)

    @block.vector
    def _(dve):
        for c in range(AHEAD):
            k.lo(dve, c)

    @block.tensor
    def _(pe):
        pe.wait_ge(*k("ones_ready").made())


CONSTS = {}
_parts = []


def _const(name, a):
    a = np.asarray(a, np.float32)
    if a.shape[0] < P:
        a = np.concatenate([a, np.zeros((P - a.shape[0], a.shape[1]), np.float32)])
    at = sum(p.shape[1] for p in _parts)
    CONSTS[name] = (at, at + a.shape[1])
    _parts.append(a)


_r = np.arange(P)
LEVELS = 7
_const("ident", np.eye(P))
_const("upper", _r[:, None] <= _r[None, :])
_const("levels", np.concatenate([(_r[:, None] // (2 * s) == _r[None, :] // (2 * s)) & (_r[:, None] // s % 2 == 0)
                                 & (_r[None, :] // s % 2 == 1) for s in (1 << n for n in range(LEVELS))], 1))
OFF = -1e30
_const("causal", np.concatenate([np.zeros((P, P)), np.where(_r[None, :] <= _r[:, None], 0.0, OFF)], 1))


def _rope():
    inv = (1.0 / (np.float32(10000.0) ** (np.arange(0, 32, 2, dtype=np.float32) / np.float32(32)))).astype(np.float32)
    ang = (np.arange(S, dtype=np.float32)[:, None] * inv[None, :]).astype(np.float32)
    cos, sin = np.cos(ang).T, np.sin(ang).T
    t = np.zeros((P, S), np.float32)
    t[64:96] = np.concatenate([cos, cos])
    t[96:128] = np.concatenate([-sin, sin])
    return t


_const("rope", _rope())


def _t5():
    rel = np.maximum(255 - np.arange(2 * S), 0)
    f = np.float32
    large = 16 + (np.log(np.maximum(rel, 1).astype(f) / f(16)) / f(np.log(2048 / 16)) * f(16)).astype(np.int32)
    bucket = np.where(rel < 16, rel, np.minimum(large, 31))
    hot = np.zeros((33, 2 * S), np.float32)
    hot[bucket, np.arange(2 * S)] = 255 - np.arange(2 * S) >= 0
    hot[32] = np.where(255 - np.arange(2 * S) >= 0, 0.0, OFF)
    return hot


_const("t5_hot", _t5())
_const("halves", _r[:, None] // 64 == _r[None, :] // 64)
_d = _r[:, None] - _r[None, :]
_const("distance", np.concatenate([np.where(_d + P < P, _d + P, -OFF), np.where(_d >= 0, _d, -OFF)], 1))
N_CONST_1 = sum(p.shape[1] for p in _parts)


def constants():
    return np.ascontiguousarray(np.concatenate(_parts, 1))


def con(k, name, a=0, b=None):
    lo, hi = CONSTS[name]
    return k.const[:, lo + a:hi if b is None else lo + b]


def tools(k):
    return k.block, (lambda name: k(name).made()), (lambda name: k(name).up())


def project(k, tiles, x_hi, x_lo, kt=KD, first=None, scaled=True, with_rstd=False, side=False):
    block, made, up = tools(k)
    c0 = k.used
    read = {}

    banks, bank_read = ((k.ps_sum, k.ps_misc), k.side_read) if side else (k.ps_gu, k.gu_read)
    b0 = k.side_bank if side else k.bank

    def out(t):
        return banks[(b0 + t) % 2]

    sc = k("product_scaled")
    s0 = sc.n
    order = [t for t in range(len(tiles)) if scaled and tiles[t][0] != "mul"]

    def reads(engine, eng, split):
        for t, (who, rows, width, work) in enumerate(tiles):
            early = engine == "act" or t == 0 or not scaled
            if early:
                split(eng, c0 + t)
            if t == 0 and with_rstd:
                if engine == "act":
                    root(k, eng)
                else:
                    root_in(k, eng)
                    spread_root(k, eng)
                    take_rstd(k, eng)
                    eng.wait_ge(*k("rstd_ready").at(k.norms))
            ps = out(t)
            if engine == "dve" and (scaled or who == "dve"):
                eng.wait_ge(*k.chunk_done.at(c0 + t + 1))
            if engine == "dve" and who == "mul":
                if rows:
                    for tt in range(TT):
                        ins = eng.tensor_scalar(work[:, tt, :], ps[:, tt * P:tt * P + width], k.rcol[:, tt:tt + 1],
                                                None, ALU.mult)
                else:
                    ins = eng.tensor_tensor(work, ps[:, 0:S], k.rstd[:, :], ALU.mult)
                ins.then_inc(*up("product_read_dve"))
                read[t] = k("product_read_dve").made()
            elif engine == "dve" and scaled:
                assert not rows
                eng.tensor_tensor(ps[:, 0:S], ps[:, 0:S], k.rstd[:, :], ALU.mult).then_inc(*sc.up())
            if who == engine:
                if scaled:
                    eng.wait_ge(*sc.at(s0 + order.index(t) + 1))
                else:
                    eng.wait_ge(*k.chunk_done.at(c0 + t + 1))
                work(eng, ps).then_inc(*up("product_read_" + engine))
                read[t] = k("product_read_" + engine).made()
            if not early:
                split(eng, c0 + t)

    @block.scalar
    def _(act):
        reads("act", act, k.hi_for)

    @block.vector
    def _(dve):
        reads("dve", dve, k.lo_for)

    @block.tensor
    def _(pe):
        if side:
            for name in ("misc_free", "y_ready", "sum_read"):
                if k(name).n:
                    pe.wait_ge(*made(name))
        for t, (who, rows, width, work) in enumerate(tiles):
            c = c0 + t
            k.wait_chunk(pe, c)
            pe.wait_ge(*(read[t - 2] if t >= 2 else bank_read[(b0 + t) % 2]))
            for j in range(kt):
                if t == 0 and first is not None and j in first:
                    pe.wait_ge(*first[j])
                if rows:
                    for tt in range(2):
                        mm = k.rows(pe, out(t)[:, tt * P:tt * P + width], c % NS, j * P, width,
                                    x_hi[:, j, tt * P:(tt + 1) * P], x_lo[:, j, tt * P:(tt + 1) * P],
                                    False, j == kt - 1, start=(j == 0 and tt == 0))
                else:
                    mm = k.products(pe, out(t)[:, 0:S], c % NS, j * P, width, x_hi[:, j, :], x_lo[:, j, :],
                                    j == 0, j == kt - 1)
            mm.then_inc(k.chunk_done.sem, 1)
            if with_rstd and t == 0:
                sum_squares(k, pe)
            if with_rstd and t == 1:
                rstd_rows(k, pe)
    n = len(tiles)
    for t in range(max(n - 2, 0), n):
        bank_read[(b0 + t) % 2] = read[t]
    if side:
        k.side_bank = (b0 + n) % 2
    else:
        k.gu_read, k.bank = bank_read, (b0 + n) % 2
    k.used += n
    return [read[t] for t in range(n)]


def project_rows(k, dst, cols, wide):
    block, made, up = tools(k)
    c0, per, N = k.used, CH // cols, min(cols, 2 * S)
    n = KD // per
    b = k.bank
    out = (lambda tt, h: k.ps_acc[:, 2 * tt + h, :]) if wide else (lambda tt, h: k.ps_gu[b][:, tt * S:(tt + 1) * S])

    @block.scalar
    def _(act):
        for c in range(n):
            k.hi_for(act, c0 + c)

    @block.tensor
    def _(pe):
        pe.wait_ge(*(made("acc_read") if wide else k.gu_read[b]))
        for c in range(n):
            k.wait_chunk(pe, c0 + c)
            for i in range(per):
                j = c * per + i
                for tt in range(TT):
                    for h in range(cols // N):
                        mm = k.rows(pe, out(tt, h), (c0 + c) % NS, i * cols + h * N, N,
                                    k.xn_hi[:, j, tt * P:(tt + 1) * P], k.xn_lo[:, j, tt * P:(tt + 1) * P],
                                    False, j == KD - 1, start=(j == 0 and (wide or tt == 0)))
            mm.then_inc(k.chunk_done.sem, 1)

    @block.vector
    def _(dve):
        for c in range(n):
            k.lo_for(dve, c0 + c)
        dve.wait_ge(*k.chunk_done.at(c0 + n))
        for tt in range(TT):
            for h in range(cols // N):
                ins = dve.tensor_scalar(dst[:, tt, h * N:(h + 1) * N], out(tt, h), k.rcol[:, tt:tt + 1], None, ALU.mult)
        ins.then_inc(*up("product_read_dve"))
    if not wide:
        k.gu_read = list(k.gu_read)
        k.gu_read[b] = made("product_read_dve")
        k.bank = 1 - b
    k.used += n


def xn_parts(k):
    return dict(enumerate(k.xn_at))


def split_y(k):
    block, made, up = tools(k)
    xh, xl = k("xn_hi_ready"), k("xn_lo_ready")
    h0 = xh.n

    @block.scalar
    def _(act):
        act.wait_ge(*k.chunk_done.at(k.used))
        for j in range(KD // 2):
            act.wait_ge(*k.y_at[j])
            act.activation(k.xn_hi[:, 2 * j:2 * j + 2, :], k.xn[:, 2 * j:2 * j + 2, :], ACT.Copy).then_inc(*xh.up())

    @block.vector
    def _(dve):
        for j in range(KD // 2):
            dve.wait_ge(*xh.at(h0 + j + 1))
            dve.tensor_tensor(k.xn_lo[:, 2 * j:2 * j + 2, :], k.xn[:, 2 * j:2 * j + 2, :],
                              k.xn_hi[:, 2 * j:2 * j + 2, :], ALU.subtract).then_inc(*xl.up())
    k.xn_at = [xl.made(KD // 2 - 1 - m // 2) for m in range(KD)]


def project_out(k):
    block, made, up = tools(k)
    split_y(k)

    def add(m):
        return lambda dve, ps: dve.tensor_tensor(k.x[:, m, :], k.x[:, m, :], ps[:, 0:S], ALU.add)

    k.x_at = project(k, [("dve", False, P, add(m)) for m in range(KD)], k.xn_hi, k.xn_lo, first=xn_parts(k),
                     scaled=False)


class Attention:

    def __init__(self, k, n, q, kk, v, scale, bias, gate, y0, slopes=None, sink=None):
        self.k, self.q, self.kk, self.v, self.scale, self.bias = k, q, kk, v, scale, bias
        self.gate, self.y0, self.slopes, self.sink = gate, y0, slopes, sink
        A, H = k.arena, 4
        heads = lambda name, w: A(name, H * w).rearrange("p (h t) -> p h t", h=H)
        self.logit = [heads(f"logit{n % 2}_{tq}", P * (tq + 1)) for tq in range(2)]
        self.turn = [heads(f"turn_{tq}", P) for tq in range(2)]
        self.pt0, self.pt1 = heads("pt0", S), heads("pt1", P)
        small = A(f"att_columns{n % 2}", 6 * H)
        self.col = lambda what, tq: small[:, (2 * what + tq) * H:(2 * what + tq + 1) * H]
        self.ps = k.ps_acc[:, :, :].rearrange("p (q j) (h t) -> p q (j h) t", q=2, h=2)
        self.scores_at, self.exp_at = [None] * 2, [None] * 2

    def scores(self):
        block, made, up = tools(self.k)
        for tq in range(2):
            K = P * (tq + 1)

            @block.tensor
            def _(pe):
                if tq == 0:
                    pe.wait_ge(*made("att_operands"))
                    pe.wait_ge(*made("x_ready"))
                    pe.wait_ge(*made("acc_read"))
                    pe.wait_ge(*made("logits_ready"))
                for h in range(4):
                    mm = pe.matmul(self.ps[:, tq, h, 0:K], self.q(h, tq), self.kk(h, K), start=(h % 2 == 0), stop=True,
                                   skip_group_check=True)
                mm.then_inc(*up("scores_ready"))
            self.scores_at[tq] = made("scores_ready")

    def weights(self):
        block, made, up = tools(self.k)
        for tq in range(2):
            K = P * (tq + 1)
            L, ps = self.logit[tq], self.ps
            neg, total, es = (self.col(n, tq) for n in range(3))

            @block.vector
            def _(dve):
                dve.wait_ge(*self.scores_at[tq])
                dve.wait_ge(*made("transposed"))
                if self.slopes is None:
                    dve.scalar_tensor_tensor(out=L, in0=ps[:, tq, :, 0:K], scalar=self.scale, in1=self.bias(tq),
                                             op0=ALU.mult, op1=ALU.add).then_inc(*up("logits_ready"))
                else:
                    for h in range(4):
                        ins = dve.scalar_tensor_tensor(out=L[:, h, :], in0=self.bias(tq), scalar=self.slopes[h],
                                                       in1=ps[:, tq, h, 0:K], op0=ALU.mult, op1=ALU.add)
                    ins.then_inc(*up("logits_ready"))
                dve.wait_ge(*made("logits_ready"))
                dve.tensor_reduce(neg, L, AX.X, ALU.max).then_inc(*up("row_max_ready"))
                dve.wait_ge(*made("row_max_ready"))
                if self.sink is not None:
                    dve.tensor_tensor(neg, neg, self.sink, ALU.max).then_inc(*up("row_max_ready"))
                    dve.wait_ge(*made("row_max_ready"))
                    dve.tensor_tensor(es, self.sink, neg, ALU.subtract).then_inc(*up("row_max_ready"))
                    dve.wait_ge(*made("row_max_ready"))
                dve.tensor_scalar(neg, neg, -1.0, None, ALU.mult).then_inc(*up("row_max_ready"))

            @block.scalar
            def _(act):
                act.wait_ge(*made("row_max_ready"))
                if self.sink is not None:
                    act.activation(es, es, ACT.Exp)
                for h in range(4):
                    ins = act.activation(L[:, h, :], L[:, h, :], ACT.Exp, bias=neg[:, h:h + 1],
                                         accum_out=total[:, h:h + 1])
                ins.then_inc(*up("exp_ready"))
            self.exp_at[tq] = made("exp_ready")

    def values(self, fill=((), ())):
        k = self.k
        block, made, up = tools(k)
        H = 4
        pt0, pt1 = self.pt0, self.pt1
        for tq in range(2):
            L, turn = self.logit[tq], self.turn[tq]
            neg, total, es = (self.col(n, tq) for n in range(3))

            @block.vector
            def _(dve):
                dve.wait_ge(*self.exp_at[tq])
                if self.sink is not None:
                    dve.tensor_tensor(total, total, es, ALU.add).then_inc(*up("row_sum_ready"))
                    dve.wait_ge(*made("row_sum_ready"))
                dve.reciprocal(total, total).then_inc(*up("row_sum_ready"))
                dve.wait_ge(*made("row_sum_ready"))
                dve.wait_ge(*made("transposed"))
                dve.tensor_tensor(turn, con(k, "ident").unsqueeze(1).to_broadcast([P, H, P]),
                                  total.unsqueeze(2).to_broadcast([P, H, P]), ALU.mult).then_inc(*up("turn_ready"))

            if fill[tq]:
                project(k, fill[tq], k.xn_hi, k.xn_lo, side=True)

            @block.tensor
            def _(pe):
                if tq == 0:
                    pe.wait_ge(*k.gu_read[0])
                    pe.wait_ge(*k.gu_read[1])
                    pe.wait_ge(*made("misc_free"))
                else:
                    for r in k.side_read:
                        pe.wait_ge(*r)
                pe.wait_ge(*made("turn_ready"))
                for h in range(H):
                    for kt in range(tq + 1):
                        if kt == 0:
                            c = (h % 2) * S + tq * P
                            out = k.ps_gu[h // 2][:, c:c + P]
                        else:
                            out = k.ps_misc[:, h * P:(h + 1) * P]
                        mm = pe.matmul(out, L[:, h, kt * P:(kt + 1) * P], turn[:, h, :], start=True, stop=True,
                                       skip_group_check=True)
                mm.then_inc(*up("transposed"))

        @block.scalar
        def _(act):
            act.wait_ge(*made("transposed"))
            for j in range(2):
                act.activation(pt0[:, 2 * j:2 * j + 2, :], k.ps_gu[j][:, :].rearrange("p (h t) -> p h t", h=2), ACT.Copy)\
                   .then_inc(*up("pt_ready"))
                k.gu_read[j] = made("pt_ready")

        @block.vector
        def _(dve):
            dve.wait_ge(*made("transposed"))
            dve.tensor_copy(pt1, k.ps_misc[:, :].rearrange("p (h t) -> p h t", h=H)).then_inc(*up("misc_free"))

        @block.tensor
        def _(pe):
            pe.wait_ge(*made("y_ready"))
            pe.wait_ge(*made("pt_ready"))
            pe.wait_ge(*made("misc_free"))
            for h in range(H):
                b = 64 * (h % 2)
                out = k.ps_sum[b:b + 64, (h // 2) * S:(h // 2 + 1) * S]
                pe.matmul(out, self.v(0, h), pt0[:, h, :], start=(h < 2), stop=True, skip_group_check=True)
                mm = pe.matmul(out[:, P:S], self.v(1, h), pt1[:, h, :], start=False, stop=True, skip_group_check=True)
            mm.then_inc(*up("heads_ready"))

        @block.vector
        def _(dve):
            dve.wait_ge(*made("heads_ready"))
            heads = k.ps_sum[:, :].rearrange("p (m t) -> p m t", m=2)
            y = k.xn[:, self.y0:self.y0 + 2, :]
            if self.gate is None:
                dve.tensor_copy(y, heads).then_inc(*up("y_ready"))
            else:
                dve.wait_ge(*made("gate_ready"))
                dve.tensor_tensor(y, heads, self.gate, ALU.mult).then_inc(*up("y_ready"))
        k.y_at[self.y0 // 2] = made("y_ready")


def mla(k, vec, others, meanwhile=None):
    block, made, up = tools(k)
    A = k.arena
    H = 4
    cq = A("cq", 3 * S).rearrange("p (m t) -> p m t", m=3)
    sq = A("sq", 3 * S).rearrange("p (m t) -> p m t", m=3)
    rs = A("rs", 2 * S)
    kh = A("kh", H * S).rearrange("p (h t) -> p h t", h=H)
    qh = A("qh", H * S).rearrange("p (h t) -> p h t", h=H)
    t1 = A("t1", H * S).rearrange("p (h t) -> p h t", h=H)
    v = A("v", 2 * S).rearrange("p (k c) -> p k c", k=2)
    gate = A("gate", 2 * S).rearrange("p (m t) -> p m t", m=2)
    cos, sin = con(k, "rope")[64:96, :], con(k, "rope")[96:128, :]

    project(k, [("mul", False, P, cq[:, m, :]) for m in range(3)], k.xn_hi, k.xn_lo, first=xn_parts(k), with_rstd=True)
    if meanwhile is not None:
        meanwhile()
    c0 = k.used

    @block.tensor
    def _(pe):
        s = c0 % NS
        k.wait_chunk(pe, c0)
        pe.wait_ge(*made("acc_read"))
        pe.wait_ge(*made("x_ready"))
        for j in range(KD):
            k.products(pe, k.ps_acc[:, 0, 0:S], s, j * P, P, k.xn_hi[:, j, :], k.xn_lo[:, j, :], j == 0, j == KD - 1)
        for j in range(KD):
            for tt in range(2):
                mm = k.rows(pe, k.ps_acc[:, 1, tt * 8:tt * 8 + 8], s, j * P, 8, k.xn_hi[:, j, tt * P:(tt + 1) * P],
                            k.xn_lo[:, j, tt * P:(tt + 1) * P], False, j == KD - 1, start=(j == 0 and tt == 0))
        mm.then_inc(k.chunk_done.sem, 1)
    k.used += 1

    @block.scalar
    def _(act):
        k.hi_for(act, c0)
        act.wait_ge(*made("product_read_dve"))
        act.activation(sq, cq, ACT.Square).then_inc(*up("square_ready"))

    @block.vector
    def _(dve):
        k.lo_for(dve, c0)
        dve.wait_ge(*k.chunk_done.at(c0 + 1))
        dve.tensor_tensor(k.ps_acc[64:128, 0, 0:S], k.ps_acc[64:128, 0, 0:S], k.rstd[64:128, :], ALU.mult)\
           .then_inc(*up("rope_scaled"))
        dve.tensor_tensor(k.ba[:, :].rearrange("p (t c) -> p t c", t=TT), k.ps_acc[:, 1, 0:16].rearrange("p (t c) -> p t c", t=TT),
                          k.rcol[:, :].unsqueeze(2).to_broadcast([P, TT, 8]), ALU.mult).then_inc(*up("ba_ready"))
        dve.wait_ge(*made("rope_scaled"))
        dve.tensor_tensor(t1[64:96, 0, :], k.ps_acc[64:96, 0, 0:S], cos, ALU.mult)
        dve.tensor_tensor(t1[64:96, 1, :], k.ps_acc[96:128, 0, 0:S], sin, ALU.mult).then_inc(*up("acc_read"))
        dve.wait_ge(*made("acc_read"))
        for h in range(H):
            ins = dve.tensor_tensor(kh[64:96, h, :], t1[64:96, 0, :], t1[64:96, 1, :], ALU.add)
        ins.then_inc(*up("rope_keys"))

    @block.tensor
    def _(pe):
        pe.wait_ge(*made("square_ready"))
        pe.wait_ge(*made("misc_free"))
        pe.wait_ge(*made("sum_read"))
        for m in range(3):
            mm = pe.matmul(k.ps_sum[:, (m // 2) * S:(m // 2 + 1) * S], k.ones[:, :], sq[:, m, :],
                           start=(m == 0), stop=(m >= 1), skip_group_check=True)
        mm.then_inc(*up("sum_sq_ready"))

    @block.vector
    def _(dve):
        dve.wait_ge(*made("sum_sq_ready"))
        dve.tensor_scalar(rs[:, 0:S], k.ps_sum[:, 0:S], 1.0 / 256, EPS, ALU.mult, ALU.add)
        dve.tensor_scalar(rs[:, S:2 * S], k.ps_sum[:, S:2 * S], 1.0 / 128, EPS, ALU.mult, ALU.add)\
           .then_inc(*up("sum_read"))
        dve.wait_ge(*made("sum_read"))
        dve.reciprocal(rs, rs).then_inc(*up("latent_rstd"))

    @block.scalar
    def _(act):
        act.wait_ge(*made("latent_rstd"))
        act.activation(rs, rs, ACT.Sqrt).then_inc(*up("latent_rstd"))

    @block.vector
    def _(dve):
        dve.wait_ge(*made("latent_rstd"))
        for m in range(3):
            ins = dve.scalar_tensor_tensor(out=sq[:, m, :], in0=cq[:, m, :], scalar=vec[:, m:m + 1],
                                           in1=rs[:, (m // 2) * S:(m // 2 + 1) * S], op0=ALU.mult, op1=ALU.mult)
        ins.then_inc(*up("latent_ready"))

    @block.scalar
    def _(act):
        act.wait_ge(*made("latent_ready"))
        act.activation(k.lat_hi[:, :, :], sq, ACT.Copy).then_inc(*up("latent_hi_ready"))

    @block.vector
    def _(dve):
        dve.wait_ge(*made("latent_hi_ready"))
        dve.tensor_tensor(k.lat_lo[:, :, :], sq, k.lat_hi[:, :, :], ALU.subtract).then_inc(*up("latent_lo_ready"))

    project(k, [("mul", False, P, gate[:, m, :]) for m in range(2)], k.xn_hi, k.xn_lo)
    project(k, others[0:1], k.xn_hi, k.xn_lo, side=True)
    c1 = k.used
    psq = k.ps_acc[:, 0:2, :].rearrange("p j (h t) -> p (j h) t", h=2)
    psk = k.ps_acc[:, 2:4, :].rearrange("p j (h t) -> p (j h) t", h=2)

    @block.tensor
    def _(pe):
        pe.wait_ge(*made("latent_lo_ready"))
        pe.wait_ge(*made("acc_read"))
        k.wait_chunk(pe, c1)
        for h in range(H):
            for j in range(2):
                mm = k.products(pe, psq[:, h, :], c1 % NS, j * 512 + h * P, P, k.lat_hi[:, j, :], k.lat_lo[:, j, :],
                                False, j == 1, start=(j == 0 and h % 2 == 0))
        mm.then_inc(k.chunk_done.sem, 1)
        k.wait_chunk(pe, c1 + 1)
        pe.wait_ge(*k.gu_read[0])
        for h in range(H):
            k.products(pe, psk[:, h, :], (c1 + 1) % NS, h * P, P, k.lat_hi[:, 2, :], k.lat_lo[:, 2, :],
                       False, True, start=(h % 2 == 0))
        s = (c1 + 1) % NS
        for tt in range(2):
            out = k.ps_gu[0][:, tt * S:(tt + 1) * S].rearrange("p (h c) -> p h c", h=H)
            wh, wl = (w[:, s, 0:512].rearrange("p (h c) -> p h c", h=H)[:, :, 64:128] for w in (k.w_hi, k.w_lo))
            lh, ll = (x[:, 2, tt * P:(tt + 1) * P] for x in (k.lat_hi, k.lat_lo))
            pe.matmul(out, lh, wh, start=(tt == 0), stop=False, skip_group_check=True)
            pe.matmul(out, lh, wl, start=False, stop=False, skip_group_check=True)
            mm = pe.matmul(out, ll, wh, start=False, stop=True, skip_group_check=True)
        mm.then_inc(k.chunk_done.sem, 1)
    k.used += 2

    @block.scalar
    def _(act):
        k.hi_for(act, c1)
        k.hi_for(act, c1 + 1)
        act.wait_ge(*k.chunk_done.at(c1 + 2))
        act.activation(kh[0:64, :, :], psk[0:64, :, :], ACT.Copy)
        act.activation(v, k.ps_gu[0][:, :].rearrange("p (k c) -> p k c", k=2), ACT.Copy).then_inc(*up("keys_ready"))
        k.gu_read[0] = made("keys_ready")

    @block.vector
    def _(dve):
        k.lo_for(dve, c1)
        k.lo_for(dve, c1 + 1)
        dve.wait_ge(*k.chunk_done.at(c1 + 1))
        dve.wait_ge(*made("rope_keys"))
        dve.tensor_copy(qh[0:64, :, :], psq[0:64, :, :])
        dve.tensor_tensor(qh[64:96, :, :], psq[64:96, :, :], cos.unsqueeze(1).to_broadcast([32, H, S]), ALU.mult)
        dve.tensor_tensor(t1[64:96, :, :], psq[96:128, :, :], sin.unsqueeze(1).to_broadcast([32, H, S]), ALU.mult)\
           .then_inc(*up("acc_read"))
        dve.wait_ge(*made("acc_read"))
        dve.tensor_tensor(qh[64:96, :, :], qh[64:96, :, :], t1[64:96, :, :], ALU.add).then_inc(*up("att_operands"))

    @block.scalar
    def _(act):
        act.wait_ge(*made("product_read_dve"))
        act.activation(gate, gate, ACT.Silu).then_inc(*up("gate_ready"))

    @block.tensor
    def _(pe):
        pe.wait_ge(*made("keys_ready"))
    att = Attention(k, 0, lambda h, tq: qh[0:96, h, tq * P:(tq + 1) * P], lambda h, K: kh[0:96, h, 0:K],
                    lambda kt, h: v[:, kt, h * 64:(h + 1) * 64], 96.0 ** -0.5,
                    lambda tq: con(k, "causal", P if tq == 0 else 0).unsqueeze(1).to_broadcast([P, H, P * (tq + 1)]),
                    gate, 0)
    att.scores()
    att.weights()

    @block.scalar
    def _(act):
        act.wait_ge(*made("kz_zero"))
    att.values(fill=(others[1:3], others[3:5]))


def t5_bias(k, io):
    block, made, up = tools(k)
    rep = k.arena("t5_rep", 4 * P).rearrange("p (h c) -> p h c", h=4)
    row = k.arena("t5_row", 4 * 2 * S).rearrange("p (h c) -> p h c", h=4)
    scratch = io["scratch"]

    @block.vector
    def _(dve):
        dve.memset(k.t5[32:33, :], 1.0).then_inc(*up("t5_one"))
        dve.wait_ge(*made("t5_one"))
        dve.wait_ge(*made("t5_table_loaded"))
        dve.tensor_copy(rep[0:33, :, :], k.t5[0:33, :].unsqueeze(2).to_broadcast([33, 4, P])).then_inc(*up("t5_rep"))

    @block.tensor
    def _(pe):
        pe.wait_ge(*made("t5_rep"))
        for h in range(4):
            mm = pe.matmul(k.ps_acc[:, h, :], rep[0:33, h, :], con(k, "t5_hot")[0:33, :], start=True, stop=True)
        mm.then_inc(*up("t5_rows"))

    @block.vector
    def _(dve):
        dve.wait_ge(*made("t5_rows"))
        dve.tensor_copy(row, k.ps_acc[:, :, :]).then_inc(*up("acc_read"))

    @block.gpsimd
    def _(pool):
        pool.wait_ge(*made("acc_read"))
        pool.dma_start(scratch.rearrange("h p c -> p h c"), row).then_inc(*k("t5_stored").up_dma())
        pool.wait_ge(*made("t5_stored"))
        for tq in range(2):
            src = bass.AP(scratch.tensor, (S - 1) - P * tq, [[2 * S - 1, P], [2 * S * P, 4], [1, S]])
            pool.dma_start(k.t5b[:, tq, :, :], src).then_inc(*k("t5_loaded").up_dma())


def moba_buffers(k):
    A = k.arena
    kz = A("moba_kz", 4 * S).rearrange("p (h t) -> p h t", h=4)

    @k.block.gpsimd
    def _(pool):
        pool.wait_ge(*k("heads_ready").made())
        pool.wait_ge(*k("y_ready").made())
        pool.memset(kz, 0.0).then_inc(*k("kz_zero").up())
    two = lambda name: A(name, 2 * S).rearrange("p (m t) -> p m t", m=2)
    return two("moba_q"), kz, two("moba_v"), two("moba_gate")


def moba_keys(kz, m):
    def work(act, ps):
        act.activation(kz[0:64, 2 * m, :], ps[0:64, 0:S], ACT.Copy)
        return act.activation(kz[64:128, 2 * m + 1, :], ps[64:128, 0:S], ACT.Copy)
    return work


def moba(k, buffers, others):
    block, made, up = tools(k)
    H = 4
    q, kz, v, gate = buffers

    project_rows(k, v, S, False)
    project(k, [("mul", False, P, gate[:, 1, :])], k.xn_hi, k.xn_lo)

    @block.scalar
    def _(act):
        act.wait_ge(*made("product_read_dve"))
        act.activation(gate, gate, ACT.Silu).then_inc(*up("gate_ready"))

    @block.tensor
    def _(pe):
        pe.wait_ge(*made("product_read_act"))
        pe.wait_ge(*made("product_read_dve"))

    @block.vector
    def _(dve):
        dve.wait_ge(*made("t5_loaded"))
    att = Attention(k, 0, lambda h, tq: q[:, h // 2, tq * P:(tq + 1) * P], lambda h, K: kz[:, h, 0:K],
                    lambda kt, h: v[:, kt, h * 64:(h + 1) * 64], 64.0 ** -0.5,
                    lambda tq: k.t5b[:, tq, :, 0:P * (tq + 1)], gate, 6)
    att.scores()
    att.weights()
    att.values(fill=(others[0:2], others[2:4]))


def delta_gate(k):
    return k.arena("z", 4 * S).rearrange("p (m t) -> p m t", m=4)


def gdn(k, vec):
    block, made, up = tools(k)
    A = k.arena
    H, TAPS, G = 4, 4, 8
    z = delta_gate(k)
    qkv = A("qkv", 12 * S).rearrange("p (m t) -> p m t", m=12)
    raw = A("raw", 2 * (S + 4)).rearrange("p (b t) -> p b t", b=2)
    acc = A("acc", 2 * S).rearrange("p (b t) -> p b t", b=2)
    sq = A("sq", 8 * S)
    rs = A("rs", 8 * S)
    acc_flat = k.s[:, :, :].rearrange("p b t -> p (b t)")
    conv_w, gain, a_log, dt_bias = vec[:, 0:48], vec[:, 48:49], vec[:, 49:53], vec[:, 53:57]
    c0 = k.used
    b0 = k.bank
    z_read = made("product_read_dve")
    cr, cd, cs = k("conv_raw_ready"), k("conv_ready"), k("conv_silu_ready")
    tap = k("first_tap_ready")
    cs0, cd0, cr0, tap0 = cs.n, cd.n, cr.n, tap.n

    @block.gpsimd
    def _(pool):
        pool.wait_ge(*made("y_ready"))
        pool.wait_ge(*made("heads_ready"))
        pool.memset(raw[:, :, 0:3], 0.0).then_inc(*up("conv_pad_ready"))

    def conv(first, end):
        @block.scalar
        def _(act):
            def finish(t):
                act.wait_ge(*cd.at(cd0 + (TAPS - 1) * (t + 1)))
                act.activation(qkv[:, t, :], acc[:, t % 2, :], ACT.Silu).then_inc(*cs.up())
            for t in range(first, end):
                k.hi_for(act, c0 + t)
                act.wait_ge(*cr.at(cr0 + t + 1))
                if t >= 2:
                    act.wait_ge(*cs.at(cs0 + t - 1))
                act.activation(acc[:, t % 2, :], raw[:, t % 2, 0:S], ACT.Copy, scale=conv_w[:, TAPS * t:TAPS * t + 1])\
                   .then_inc(*tap.up())
                if t > first:
                    finish(t - 1)
            finish(end - 1)

        @block.vector
        def _(dve):
            if first == 0:
                dve.wait_ge(*made("conv_pad_ready"))
            for t in range(first, end):
                dve.wait_ge(*k.chunk_done.at(c0 + t + 1))
                if t >= 2:
                    dve.wait_ge(*cd.made(TAPS - 1))
                dve.tensor_tensor(raw[:, t % 2, 3:3 + S], k.ps_gu[(b0 + t) % 2][:, 0:S], k.rstd[:, :], ALU.mult)\
                   .then_inc(*cr.up())
                k.lo_for(dve, c0 + t)
                w = lambda j: conv_w[:, TAPS * t + j:TAPS * t + j + 1]
                dst, src = acc[:, t % 2, :], raw[:, t % 2, :]
                dve.wait_ge(*tap.at(tap0 + t + 1))
                for j in range(1, TAPS):
                    if j > 1:
                        dve.wait_ge(*cd.made())
                    dve.scalar_tensor_tensor(out=dst, in0=src[:, j:j + S], scalar=w(j), in1=dst,
                                             op0=ALU.mult, op1=ALU.add).then_inc(*cd.up())

        @block.tensor
        def _(pe):
            for t in range(first, end):
                c = c0 + t
                k.wait_chunk(pe, c)
                pe.wait_ge(*(cr.at(cr0 + t - 1) if t >= 2 else k.gu_read[(b0 + t) % 2]))
                for j in range(KD):
                    mm = k.products(pe, k.ps_gu[(b0 + t) % 2][:, 0:S], c % NS, j * P, P, k.xn_hi[:, j, :],
                                    k.xn_lo[:, j, :], j == 0, j == KD - 1)
                mm.then_inc(k.chunk_done.sem, 1)
        k.used += end - first

    @block.scalar
    def _(act):
        act.wait_ge(*z_read)
        act.activation(z, z, ACT.Silu).then_inc(*up("gate_ready"))

    g8 = A("g8", 96).rearrange("p (n c) -> p n c", n=12)
    (beta, aa, low, g, gc, kb_s, ke_s, ew) = (g8[:, n, :] for n in range(8))
    view = lambda t: t.rearrange("p (t h) -> p t h", t=2)
    ba = k.ba[:, :].rearrange("p (t c) -> p t c", t=2)

    @block.vector
    def _(dve):
        dve.wait_ge(*made("ba_ready"))
        dve.tensor_tensor(view(aa), ba[:, :, 4:8], dt_bias.unsqueeze(1).to_broadcast([P, 2, 4]), ALU.add)\
           .then_inc(*up("gate_step"))
        dve.wait_ge(*made("gate_step"))
        dve.tensor_scalar(low, aa, -1.0, None, ALU.mult).then_inc(*up("gate_step"))
        dve.wait_ge(*made("gate_step"))
        dve.tensor_tensor(low, aa, low, ALU.min).then_inc(*up("gate_step"))

    @block.scalar
    def _(act):
        act.wait_ge(*made("gate_step"))
        act.activation(view(beta), ba[:, :, 0:4], ACT.Sigmoid)
        act.activation(low, low, ACT.Exp).then_inc(*up("gate_exp"))
        act.activation(g8[:, 8, 0:4], a_log, ACT.Exp)
        act.wait_ge(*made("gate_exp"))
        act.activation(low, low, ACT.Ln, bias=1.0).then_inc(*up("gate_exp"))

    @block.vector
    def _(dve):
        dve.wait_ge(*made("gate_exp"))
        dve.scalar_tensor_tensor(out=g, in0=aa, scalar=0.0, in1=low, op0=ALU.max, op1=ALU.add).then_inc(*up("gate_step"))
        dve.wait_ge(*made("gate_step"))
        dve.scalar_tensor_tensor(out=view(g), in0=view(g), scalar=-1.0, in1=g8[:, 8, 0:4].unsqueeze(1).to_broadcast([P, 2, 4]),
                                 op0=ALU.mult, op1=ALU.mult).then_inc(*up("gate_step"))

    big = lambda name: A(name, G * P)
    four = lambda ap: ap.rearrange("p (n c) -> p n c", n=G)
    ET, LT, AT, T, U, Y = (big(n) for n in ("ET", "LT", "AT", "T", "U", "Y"))
    Lm = [big("Lm0"), big("Lm1")]
    grow = k.ps_acc[:, 0:2, :].rearrange("p j c -> p (j c)")
    brow = k.ps_acc[:, 2:4, :].rearrange("p j c -> p (j c)")
    bank = lambda ps0, n: ps0[:, n // 4, (n % 4) * P:(n % 4 + 1) * P]
    acc01, acc23 = k.ps_acc[:, 0:2, :], k.ps_acc[:, 2:4, :]
    grep, brep = Y, Lm[0]

    @block.vector
    def _(dve):
        dve.wait_ge(*made("gate_step"))
        dve.tensor_copy(four(grep), g.unsqueeze(2).to_broadcast([P, G, P]))
        dve.tensor_copy(four(brep), beta.unsqueeze(2).to_broadcast([P, G, P])).then_inc(*up("gates_spread"))

    @block.gpsimd
    def _(pool):
        ident = con(k, "ident").unsqueeze(1).to_broadcast([P, G, P])
        pool.tensor_copy(four(T), ident)
        pool.tensor_copy(four(U), ident).then_inc(*up("inv_start"))
    conv(0, 4)

    @block.tensor
    def _(pe):
        pe.wait_ge(*made("gates_spread"))
        pe.wait_ge(*made("acc_read"))
        pe.wait_ge(*made("misc_free"))
        for w in k.side_read:
            pe.wait_ge(*w)
        for n in range(G):
            pe.matmul(bank(acc01, n), four(grep)[:, n, :], con(k, "upper"), start=(n % 4 == 0), stop=True, skip_group_check=True)
        for n in range(G):
            pe.matmul(bank(acc23, n), four(brep)[:, n, :], con(k, "ident"), start=(n % 4 == 0), stop=True, skip_group_check=True)
        pe.matmul(k.ps_misc[:, 0:G], con(k, "upper"), g, start=True, stop=True).then_inc(*up("gate_rows_ready"))

    @block.vector
    def _(dve):
        dve.wait_ge(*made("gate_rows_ready"))
        dve.tensor_copy(gc, k.ps_misc[:, 0:G]).then_inc(*up("misc_free"))
        dve.wait_ge(*made("misc_free"))
        for n in range(G):
            ins = dve.tensor_scalar(four(ET)[:, n, :], bank(acc01, n), gc[:, n:n + 1], 0.0, ALU.subtract, ALU.min)
        dve.tensor_tensor(ke_s, grow.rearrange("p (n c) -> p n c", c=P)[:, :, P - 1], gc, ALU.subtract)
        dve.tensor_copy(acc_flat, grow[:, 4 * P:8 * P]).then_inc(*up("decay_args"))

    @block.scalar
    def _(act):
        act.wait_ge(*made("decay_args"))
        act.activation(ET, ET, ACT.Exp)
        act.activation(ke_s, ke_s, ACT.Exp)
        act.activation(kb_s, gc, ACT.Exp)
        act.activation(acc_flat, acc_flat, ACT.Exp).then_inc(*up("decay_exp"))

    @block.vector
    def _(dve):
        dve.wait_ge(*made("decay_exp"))
        dve.tensor_tensor(four(ET), four(ET), con(k, "upper").unsqueeze(1).to_broadcast([P, G, P]), ALU.mult)
        dve.tensor_tensor(kb_s, kb_s, beta, ALU.mult).then_inc(*up("decay_ready"))
        dve.tensor_copy(LT, brow).then_inc(*up("acc_read"))

    conv(4, 8)

    @block.scalar
    def _(act):
        act.wait_ge(*made("conv_silu_ready"))
        act.activation(sq, qkv[:, 0:8, :].rearrange("p m t -> p (m t)"), ACT.Square).then_inc(*up("square_ready"))

    conv(8, 9)

    for half in range(2):
        @block.tensor
        def _(pe):
            pe.wait_ge(*made("square_ready"))
            pe.wait_ge(*made("acc_read"))
            for m in range(4 * half, 4 * half + 4):
                mm = pe.matmul(k.ps_acc[:, m // 2, (m % 2) * S:(m % 2 + 1) * S], k.ones[:, :], sq[:, m * S:(m + 1) * S],
                               start=(m % 2 == 0), stop=True, skip_group_check=True)
            mm.then_inc(*up("sum_sq_ready"))

    @block.vector
    def _(dve):
        dve.wait_ge(*made("sum_sq_ready"))
        dve.tensor_scalar(rs, k.ps_acc[:, :, :].rearrange("p j c -> p (j c)"), 1e-6, None, ALU.add).then_inc(*up("acc_read"))
    conv(9, 10)

    @block.scalar
    def _(act):
        act.wait_ge(*made("acc_read"))
        act.activation(rs, rs, ACT.Ln).then_inc(*up("rs_step"))
        act.wait_ge(*made("rs_step"))
        act.activation(rs, rs, ACT.Exp, scale=-0.5).then_inc(*up("rs_step"))
    conv(10, 11)

    @block.vector
    def _(dve):
        dve.wait_ge(*made("rs_step"))
        rows = lambda m: qkv[:, m:m + 4, :].rearrange("p m t -> p (m t)")
        dve.tensor_tensor(rows(4), rows(4), rs[:, 4 * S:8 * S], ALU.mult).then_inc(*up("k_ready"))
        dve.scalar_tensor_tensor(out=rows(0), in0=rows(0), scalar=128.0 ** -0.5, in1=rs[:, 0:4 * S],
                                 op0=ALU.mult, op1=ALU.mult).then_inc(*up("q_ready"))

    conv(11, 12)
    for t in (10, 11):
        k.gu_read[(b0 + t) % 2] = cr.at(cr0 + t + 1)

    tile = lambda m, n: qkv[:, m + n % 4, (n // 4) * P:(n // 4 + 1) * P]
    gu = [k.ps_gu[0][:, :], k.ps_gu[1][:, :]]
    gub = lambda n: gu[n // 4][:, (n % 4) * P:(n % 4 + 1) * P]

    @block.tensor
    def _(pe):
        pe.wait_ge(*made("k_ready"))
        pe.wait_ge(*made("acc_read"))
        for n in range(G):
            mm = pe.matmul(bank(acc01, n), tile(4, n), tile(4, n), start=(n % 4 == 0), stop=True, skip_group_check=True)
        mm.then_inc(*up("kk_ready"))
        pe.wait_ge(*made("q_ready"))
        for n in range(G):
            mm = pe.matmul(bank(acc23, n), tile(4, n), tile(0, n), start=(n % 4 == 0), stop=True, skip_group_check=True)
        mm.then_inc(*up("qk_ready"))
        pe.wait_ge(*k.gu_read[0])
        pe.wait_ge(*k.gu_read[1])
        for n in range(G):
            mm = pe.transpose(gub(n), tile(4, n), con(k, "ident"))
        mm.then_inc(*up("k_turned"))

    kN, vN = sq[:, 0:G * P], sq[:, G * P:2 * G * P]
    Kb, ke, Vb = rs[:, 0:H * P], rs[:, H * P:2 * H * P], rs[:, 2 * H * P:4 * H * P]

    @block.vector
    def _(dve):
        dve.wait_ge(*made("decay_ready"))
        dve.wait_ge(*made("kk_ready"))
        dve.tensor_tensor(LT, LT, ET, ALU.mult).then_inc(*up("L_step"))
        dve.wait_ge(*made("L_step"))
        dve.tensor_tensor(LT, LT, acc01.rearrange("p j c -> p (j c)"), ALU.mult).then_inc(*up("L_ready"))
        dve.wait_ge(*made("qk_ready"))
        dve.tensor_tensor(AT, ET, acc23.rearrange("p j c -> p (j c)"), ALU.mult).then_inc(*up("A_ready"))

    @block.scalar
    def _(act):
        act.wait_ge(*made("k_turned"))
        for j in range(2):
            act.activation(kN[:, j * 4 * P:(j + 1) * 4 * P], gu[j], ACT.Copy).then_inc(*up("kN_ready"))

    @block.tensor
    def _(pe):
        pe.wait_ge(*made("conv_silu_ready"))
        pe.wait_ge(*made("kN_ready"))
        for n in range(G):
            mm = pe.transpose(gub(n), tile(8, n), con(k, "ident"))
        mm.then_inc(*up("v_turned"))

    @block.scalar
    def _(act):
        act.wait_ge(*made("v_turned"))
        for j in range(2):
            act.activation(vN[:, j * 4 * P:(j + 1) * 4 * P], gu[j], ACT.Copy).then_inc(*up("vN_ready"))
            k.gu_read[j] = made("vN_ready")

    lm_first, lm = k("Lm_first_ready"), k("Lm_ready")
    yr, ys, ty, uy, tr, ur = ([k(f"{name}{g}") for g in range(2)] for name in
                              ("Y_ready", "Y_copied", "TY_ready", "YU_ready", "T_ready", "U_ready"))
    yr0, ur0, lm0 = yr[1].n, ur[1].n, lm.n
    group = lambda g: range(4 * g, 4 * g + 4)
    part = lambda t, g: t[:, 4 * g * P:(4 * g + 4) * P]
    for lv in range(LEVELS):
        last = lv == LEVELS - 1

        @(block.gpsimd if lv else block.vector)
        def _(pool):
            if lv == 0:
                pool.wait_ge(*made("L_ready"))
                pool.wait_ge(*made("gate_rows_ready"))
            if lv == 1:
                pool.wait_ge(*made("L_ready"))
            if lv >= 2:
                pool.wait_ge(*yr[1].at(yr0 + lv - 1))
            if lv == 2:
                pool.wait_ge(*ur[1].at(ur0 + 1))
            m = con(k, "levels", lv * P, (lv + 1) * P).unsqueeze(1).to_broadcast([P, G, P])
            pool.tensor_tensor(four(Lm[lv % 2]), four(LT), m, ALU.mult).then_inc(*(lm if lv else lm_first).up())

        @block.tensor
        def _(pe):
            if lv == 0:
                pe.wait_ge(*made("inv_start"))
                pe.wait_ge(*made("A_ready"))
            pe.wait_ge(*(lm.at(lm0 + lv) if lv else lm_first.made()))
            for g in range(2):
                if lv:
                    pe.wait_ge(*tr[g].made())
                for n in group(g):
                    mm = pe.matmul(bank(acc01, n), four(Lm[lv % 2])[:, n, :], four(T)[:, n, :],
                                   start=(n % 4 == 0), stop=True, skip_group_check=True)
                mm.then_inc(*yr[g].up())

        if lv == 0:

            @block.vector
            def _(dve):
                dve.wait_ge(*lm_first.made())
                for g in range(2):
                    dve.wait_ge(*yr[g].made())
                    dve.tensor_tensor(part(T, g), part(T, g), acc01[:, g, :], ALU.subtract).then_inc(*tr[g].up())
                    dve.tensor_tensor(part(U, g), part(U, g), part(Lm[0], g), ALU.subtract).then_inc(*ur[g].up())
            continue

        @block.scalar
        def _(act):
            for g in range(2):
                act.wait_ge(*yr[g].made())
                act.activation(part(Y, g), acc01[:, g, :], ACT.Copy).then_inc(*ys[g].up())

        @block.tensor
        def _(pe):
            if lv == 1:
                pe.wait_ge(*made("vN_ready"))
            for g in range(2):
                pe.wait_ge(*ys[g].made())
                pe.wait_ge(*ur[g].made())
                if not last:
                    for n in group(g):
                        mm = pe.matmul(gub(n), four(U)[:, n, :], four(Y)[:, n, :],
                                       start=(n % 4 == 0), stop=True, skip_group_check=True)
                    mm.then_inc(*ty[g].up())
                for n in group(g):
                    mm = pe.matmul(bank(acc23, n), four(Y)[:, n, :], four(U)[:, n, :],
                                   start=(n % 4 == 0), stop=True, skip_group_check=True)
                mm.then_inc(*uy[g].up())

        @block.vector
        def _(dve):
            for g in range(2):
                if not last:
                    dve.wait_ge(*ty[g].made())
                    dve.tensor_tensor(part(T, g), part(T, g), gu[g], ALU.subtract).then_inc(*tr[g].up())
                dve.wait_ge(*uy[g].made())
                dve.tensor_tensor(part(U, g), part(U, g), acc23[:, g, :], ALU.subtract).then_inc(*ur[g].up())
    k.gu_read = [tr[g].made() for g in range(2)]

    cols = lambda s, w: s.unsqueeze(2).to_broadcast([P, w, P])

    @block.vector
    def _(dve):
        dve.wait_ge(*made("vN_ready"))
        dve.wait_ge(*made("decay_ready"))
        dve.tensor_tensor(four(Vb), four(vN), cols(beta, G), ALU.mult)
        dve.tensor_tensor(Kb.rearrange("p (h c) -> p h c", h=H), four(kN)[:, 4:8, :], cols(kb_s[:, 4:8], H), ALU.mult)
        dve.tensor_tensor(ke.rearrange("p (h c) -> p h c", h=H), four(kN)[:, 0:4, :], cols(ke_s[:, 0:4], H), ALU.mult)
        dve.tensor_tensor(acc_flat.rearrange("p (h c) -> p h c", h=H), acc_flat.rearrange("p (h c) -> p h c", h=H),
                          qkv[:, 0:4, P:S], ALU.mult).then_inc(*up("rhs_ready"))
    qg = acc_flat
    U0, WT, ST = T, Lm[0][:, 0:H * P], Lm[0][:, H * P:2 * H * P]
    UN = Lm[1][:, 0:H * P]
    h4 = lambda t, h: t[:, h * P:(h + 1) * P]

    @block.tensor
    def _(pe):
        pe.wait_ge(*ur[0].made())
        pe.wait_ge(*ur[1].made())
        pe.wait_ge(*made("rhs_ready"))
        for n in range(G):
            mm = pe.matmul(gub(n), four(U)[:, n, :], four(Vb)[:, n, :], start=(n % 4 == 0), stop=True, skip_group_check=True)
        mm.then_inc(*up("U0_ready"))
        for h in range(H):
            mm = pe.matmul(bank(acc01, h), h4(Kb, h), four(U)[:, 4 + h, :], start=(h == 0), stop=True, skip_group_check=True)
        mm.then_inc(*up("W_ready"))

    @block.scalar
    def _(act):
        act.wait_ge(*made("U0_ready"))
        for j in range(2):
            act.activation(U0[:, j * 4 * P:(j + 1) * 4 * P], gu[j], ACT.Copy).then_inc(*up("U0_copied"))
        k.gu_read = [made("U0_copied")] * 2

    @block.vector
    def _(dve):
        dve.wait_ge(*made("W_ready"))
        dve.tensor_copy(WT, acc01[:, 0, :]).then_inc(*up("W_copied"))

    @block.tensor
    def _(pe):
        pe.wait_ge(*made("U0_copied"))
        for h in range(H):
            mm = pe.matmul(bank(acc01, 4 + h), h4(ke, h), four(U0)[:, h, :], start=(h == 0), stop=True, skip_group_check=True)
        mm.then_inc(*up("S_ready"))

    @block.scalar
    def _(act):
        act.wait_ge(*made("S_ready"))
        act.activation(ST, acc01[:, 1, :], ACT.Copy).then_inc(*up("S_copied"))

    @block.tensor
    def _(pe):
        pe.wait_ge(*made("S_copied"))
        pe.wait_ge(*made("W_copied"))
        for h in range(H):
            mm = pe.matmul(bank(acc01, h), h4(WT, h), h4(ST, h), start=(h == 0), stop=True, skip_group_check=True)
        mm.then_inc(*up("WS_ready"))

    @block.vector
    def _(dve):
        dve.wait_ge(*made("WS_ready"))
        dve.tensor_tensor(UN, U0[:, 4 * P:8 * P], acc01[:, 0, :], ALU.subtract).then_inc(*up("U_ready"))

    @block.tensor
    def _(pe):
        for h in range(H):
            out = acc23[:, h // 2, (h % 2) * S:(h % 2 + 1) * S]
            pe.matmul(out[:, 0:P], four(U0)[:, h, :], four(AT)[:, h, :], start=(h % 2 == 0), stop=True, skip_group_check=True)
            pe.matmul(out[:, P:S], h4(ST, h), h4(qg, h), start=False, stop=False, skip_group_check=True)
        pe.wait_ge(*made("U_ready"))
        for h in range(H):
            out = acc23[:, h // 2, (h % 2) * S:(h % 2 + 1) * S]
            mm = pe.matmul(out[:, P:S], h4(UN, h), four(AT)[:, 4 + h, :], start=False, stop=True, skip_group_check=True)
        mm.then_inc(*up("heads_ready"))
    bank_of = lambda t: lambda j: t[:, j * 2 * S:(j + 1) * 2 * S]
    head_norm(k, [acc23[:, 0, :], acc23[:, 1, :]], [made("heads_ready")] * 2, [acc01[:, 0, :], acc01[:, 1, :]],
              bank_of(Y), bank_of(Lm[1]), gain, bank_of(z.rearrange("p m t -> p (m t)")), 2, P)

    @block.vector
    def _(dve):
        dve.wait_ge(*made("y_ready"))
        dve.tensor_copy(k.tiny[:, 0:1], k.xn[:, 2, 0:1]).then_inc(*up("acc_read"))


def head_norm(k, outs, outs_at, sums, sq, rs, gain, gate, y0, width, meanwhile=None):
    block, made, up = tools(k)
    n = len(outs)
    sqs, sm, rd, rt, nm, y = (k(name) for name in ("square_ready", "sum_sq_ready", "head_sums_read", "rs_step",
                                                   "norm_step", "y_ready"))
    sq0, sm0, rd0, rt0, nm0 = sqs.n, sm.n, rd.n, rt.n, nm.n

    @block.scalar
    def _(act):
        for j in range(n):
            act.wait_ge(*outs_at[j])
            act.activation(sq(j), outs[j], ACT.Square).then_inc(*sqs.up())

    @block.tensor
    def _(pe):
        for j in range(n):
            pe.wait_ge(*sqs.at(sq0 + j + 1))
            pe.wait_ge(*rd.at(rd0 + j - 1 if j >= 2 else rd0))
            for m in range(2):
                mm = pe.matmul(sums[j % 2][:, m * S:(m + 1) * S], k.ones[:, :], sq(j)[:, m * S:(m + 1) * S],
                               start=(m == 0), stop=True, skip_group_check=True)
            mm.then_inc(*sm.up())

    @block.vector
    def _(dve):
        for j in range(n):
            dve.wait_ge(*sm.at(sm0 + j + 1))
            dve.tensor_scalar(rs(j), sums[j % 2], 1.0 / width, EPS, ALU.mult, ALU.add).then_inc(*rd.up())

    @block.scalar
    def _(act):
        for j in range(n):
            act.wait_ge(*rd.at(rd0 + j + 1))
            act.activation(rs(j), rs(j), ACT.Ln).then_inc(*rt.up())
        for j in range(n):
            act.wait_ge(*rt.at(rt0 + j + 1))
            act.activation(rs(j), rs(j), ACT.Exp, scale=-0.5).then_inc(*rt.up())
    if meanwhile is not None:
        meanwhile()

    @block.vector
    def _(dve):
        for j in range(n):
            dve.wait_ge(*rt.at(rt0 + n + j + 1))
            dve.tensor_tensor(rs(j), rs(j), outs[j], ALU.mult).then_inc(*nm.up())
            dve.wait_ge(*nm.at(nm0 + j + 1))
            if j == (n // 2 if meanwhile else 0):
                dve.wait_ge(*made("gate_ready"))
            pair = k.xn[:, y0 + 2 * j:y0 + 2 * j + 2, :].rearrange("p m t -> p (m t)")
            dve.scalar_tensor_tensor(out=pair, in0=rs(j), scalar=gain, in1=gate(j), op0=ALU.mult, op1=ALU.mult)\
               .then_inc(*y.up())
            k.y_at[y0 // 2 + j] = y.made()


def widths(w, *parts):
    return np.concatenate([w[:, a:b] for a, b in parts], 1)


def as_columns(w):
    K, N = w.shape
    return w.reshape(K // P, P, N // P, P).transpose(2, 1, 0, 3).reshape(N // P, P, -1)


def as_rows(w):
    return w.reshape(-1, P, w.shape[1])


def as_wide(w):
    N = w.shape[1]
    per = CH // N
    return w.reshape(-1, per, P, N).transpose(0, 2, 1, 3).reshape(-1, P, CH)


def filled(chunks):
    n, p, c = chunks.shape
    return chunks if c == CH else np.concatenate([chunks, np.zeros((n, p, CH - c), chunks.dtype)], 2)


def first_chunks(w_in, w_uq, w_ukv, w_out):
    at = np.cumsum([0, 256, 128, 32, 256, 512, 512, 512, 512, 4, 4, 256, 256, 256, 256])
    part = lambda n: w_in[:, at[n]:at[n + 1]]
    kr = part(2)
    misc = np.concatenate([part(8), part(9), np.zeros((D, 56), w_in.dtype), kr, kr[:, 16:], kr[:, :16]], 1)
    q = w_uq.reshape(256, 4, 96)
    uq = np.concatenate([q, q[:, :, 80:96], q[:, :, 64:80]], 2).reshape(256, 512)
    uq = uq.reshape(2, P, 512).transpose(1, 0, 2).reshape(1, P, CH)
    cols = lambda n: as_columns(part(n))
    mg, (mq, mk, mgate), z = cols(3), (cols(n) for n in (10, 11, 13)), cols(7)
    return [cols(0), cols(1), as_columns(misc), mg, mq[0:1], uq, filled(w_ukv.reshape(1, P, 512)),
            mq[1:2], mgate[0:1], mk, as_wide(part(12)), mgate[1:2], z, as_columns(w_in[:, at[4]:at[7]]), as_columns(w_out)]


def first_layer(k, v, meanwhile=None):
    norm(k, v[:, 0:8])
    if meanwhile is not None:
        first_splits(k)
    k.arena.clear()
    z = delta_gate(k)
    buffers = moba_buffers(k)
    q, kz, val, gate = buffers
    mla(k, v[:, 8:11], [("mul", False, P, q[:, 0, :]), ("mul", False, P, q[:, 1, :]), ("mul", False, P, gate[:, 0, :]),
                        ("act", False, P, moba_keys(kz, 0)), ("act", False, P, moba_keys(kz, 1))], meanwhile)
    moba(k, buffers, [("mul", False, P, z[:, m, :]) for m in range(4)])
    k.arena.clear()
    gdn(k, v[:, 11:68])
    project_out(k)


def columns(v):
    return v.reshape(-1, P).T


def spread(v):
    return np.broadcast_to(v.reshape(1, -1), (P, v.size))


def first_vectors(norm_w, q_norm, kv_norm, conv_w, a_log, dt_bias, gdn_norm):
    conv = conv_w.reshape(4, 12, P).transpose(2, 1, 0).reshape(P, 48)
    return [columns(norm_w), columns(q_norm), columns(kv_norm), conv, columns(gdn_norm), spread(a_log), spread(dt_bias)]


I32 = mybir.dt.int32


def lower_bounds(k, raw):
    block, made, up = tools(k)
    L = k.lbw
    part = lambda n: L[:, n * KD:(n + 1) * KD]
    layer = lambda n: raw[:, n * KD:(n + 1) * KD]
    e4 = L[:, 0:4 * KD]

    @block.vector
    def _(dve):
        dve.tensor_reduce(part(4), raw.rearrange("p (l m) -> p m l", l=4), AX.X, ALU.max).then_inc(*up("bounds_step"))
        dve.wait_ge(*made("bounds_step"))
        dve.tensor_tensor(e4.rearrange("p (l m) -> p l m", l=4), raw.rearrange("p (l m) -> p l m", l=4),
                          part(4).unsqueeze(1).to_broadcast([P, 4, KD]), ALU.subtract).then_inc(*up("bounds_step"))

    @block.scalar
    def _(act):
        act.wait_ge(*made("bounds_step"))
        act.activation(e4, e4, ACT.Exp).then_inc(*up("bounds_exp"))

    @block.vector
    def _(dve):
        dve.wait_ge(*made("bounds_exp"))
        dve.tensor_reduce(part(5), e4.rearrange("p (l m) -> p m l", l=4), AX.X, ALU.add)
        dve.tensor_tensor(part(6), part(1), part(2), ALU.add).then_inc(*up("bounds_step"))
        dve.wait_ge(*made("bounds_step"))
        dve.tensor_tensor(part(6), part(6), part(3), ALU.add)
        dve.reciprocal(part(5), part(5)).then_inc(*up("bounds_step"))
        dve.wait_ge(*made("bounds_step"))
        dve.tensor_tensor(part(6), part(6), part(5), ALU.mult)
        dve.tensor_tensor(part(7), part(0), part(5), ALU.mult).then_inc(*up("bounds_ready"))
    k.lb = (part(6), part(7))


def hgrn(k, g_norm, lb):
    block, made, up = tools(k)
    A = k.arena
    H = 8
    q, kk, f = A("q", H * S), A("k", H * S), A("f", H * S)
    f2 = A("f2", H * S)
    v = A("v", 2 * H * P).rearrange("p (k c) -> p k c", k=2)
    gate = A("gate", H * S)
    at0 = A("at0", H * S).rearrange("p (h t) -> p h t", h=H)
    at1 = A("at1", H * P).rearrange("p (h t) -> p h t", h=H)
    m = lambda t, h: t[:, h * S:(h + 1) * S]
    sil = lambda h: lambda act, ps: act.activation(m(q, h), ps[:, 0:S], ACT.Silu)

    def forget(h):
        def work(act, ps):
            act.activation(m(f, h), ps[:, 0:S], ACT.Sigmoid)
            return act.activation(m(kk, h), ps[:, 0:S], ACT.Sigmoid, scale=-1.0)
        return work

    @block.scalar
    def _(act):
        act.wait_ge(*made("y_ready"))
        act.wait_ge(*made("acc_read"))
    project(k, [("act", False, P, sil(h)) for h in range(H)], k.xn_hi, k.xn_lo, first=xn_parts(k), with_rstd=True)
    project(k, [("act", False, P, forget(h)) for h in range(H)], k.xn_hi, k.xn_lo)

    @block.vector
    def _(dve):
        dve.wait_ge(*made("product_read_act"))
        if lb is not None:
            for h in range(H):
                dve.tensor_scalar(m(f, h), m(f, h), lb[1][:, h:h + 1], lb[0][:, h:h + 1], ALU.mult, ALU.add)
                ins = dve.tensor_scalar(m(kk, h), m(kk, h), lb[1][:, h:h + 1], None, ALU.mult)
            ins.then_inc(*up("forget_ready"))
    project_rows(k, v, D, True)
    project(k, [("act", False, P, (lambda h: lambda act, ps: act.activation(m(gate, h), ps[:, 0:S], ACT.Silu))(h))
                for h in range(H - 4)], k.xn_hi, k.xn_lo)

    def last_gates():
        project(k, [("mul", False, P, m(gate, h)) for h in range(H - 4, H)], k.xn_hi, k.xn_lo, side=True)

        @block.scalar
        def _(act):
            act.wait_ge(*made("product_read_dve"))
            last = gate[:, (H - 4) * S:H * S]
            act.activation(last, last, ACT.Silu).then_inc(*up("gate_ready"))

    sc, cp, dq, dk = k("level_scores"), k("level_copied"), k("q_decayed"), k("k_decayed")
    HG = 4
    copied, q_done, k_done = ([None, None] for _ in range(3))
    ident = con(k, "ident").unsqueeze(1).to_broadcast([P, HG, P])
    tot = [(f, 0)]
    at = 0
    for s in (2 << n for n in range(LEVELS)):
        tot.append((f2, at))
        at += H * S // s
    for lv in range(-1, LEVELS + 1):
        s = 0 if lv < 0 else 1 << lv
        for g in range(2):
            h0 = HG * g
            bank = lambda tt: k.ps_acc[:, 2 * g + tt, :]

            @block.tensor
            def _(pe):
                if lv < 0:
                    pe.wait_ge(*made("forget_ready"))
                    pe.wait_ge(*made("product_read_act"))
                    pe.wait_ge(*made("product_read_dve"))
                    pe.wait_ge(*made("x_ready"))
                    pe.wait_ge(*made("acc_read"))
                else:
                    pe.wait_ge(*q_done[g])
                    pe.wait_ge(*k_done[g])
                    pe.wait_ge(*copied[g])
                for h in range(HG):
                    for tt in range(2 if lv < LEVELS else 1):
                        a = (h0 + h) * S + tt * P
                        b = a if lv < LEVELS else a + P
                        mm = pe.matmul(bank(tt)[:, h * P:(h + 1) * P], kk[:, a:a + P], q[:, b:b + P],
                                       start=(h == 0), stop=True, skip_group_check=True)
                mm.then_inc(*sc.up())

            @block.vector
            def _(dve):
                dve.wait_ge(*sc.made())
                for tt in range(2):
                    src = bank(tt).rearrange("p (h t) -> p h t", h=HG)
                    dst = at0[:, h0:h0 + HG, 0:P] if tt == 0 else at1[:, h0:h0 + HG, :]
                    if lv < 0:
                        ins = dve.tensor_tensor(dst, src, ident, ALU.mult)
                    elif lv < LEVELS:
                        mask = con(k, "levels", lv * P, (lv + 1) * P).bitcast(I32).unsqueeze(1).to_broadcast([P, HG, P])
                        if tt == 0:
                            dve.wait_ge(*copied[g])
                        ins = dve.copy_predicated(dst, mask, src)
                    elif tt == 0:
                        ins = dve.tensor_copy(at0[:, h0:h0 + HG, P:S], src)
                ins.then_inc(*cp.up())
            copied[g] = cp.made()

            n = slice(h0 * S, (h0 + HG) * S)
            if lv == -1:
                @block.vector
                def _(dve):
                    dve.tensor_tensor(q[:, n], q[:, n], f[:, n], ALU.mult).then_inc(*dq.up())
                @block.gpsimd
                def _(pool):
                    pool.wait_ge(*sc.made())
                    pool.memset(k.tiny[:, g:g + 1], 0.0).then_inc(*dk.up())
            elif lv < LEVELS:
                src, a = tot[lv]
                w = H * S // s
                t2 = src[:, a + g * w // 2:a + (g + 1) * w // 2].rearrange("p (n two) -> p n two", two=2)
                blocks = lambda t: t[:, n].rearrange("p (n two s) -> p n two s", two=2, s=s)
                N = HG * S // (2 * s)
                first = t2[:, :, 0].unsqueeze(2).to_broadcast([P, N, s])
                second = t2[:, :, 1].unsqueeze(2).to_broadcast([P, N, s])

                q_before = q_done[g]

                @block.vector
                def _(dve):
                    dve.wait_ge(*q_done[g])
                    dve.tensor_tensor(blocks(q)[:, :, 1, :], blocks(q)[:, :, 1, :], first, ALU.mult)
                    dst, b = tot[lv + 1]
                    dve.tensor_tensor(dst[:, b + g * w // 4:b + (g + 1) * w // 4], t2[:, :, 0], t2[:, :, 1], ALU.mult)\
                       .then_inc(*dq.up())

                @block.gpsimd
                def _(pool):
                    pool.wait_ge(*sc.made())
                    if lv >= 1:
                        pool.wait_ge(*q_before)
                    pool.wait_ge(*k_done[g])
                    pool.tensor_tensor(blocks(kk)[:, :, 0, :], blocks(kk)[:, :, 0, :], second, ALU.mult).then_inc(*dk.up())
            q_done[g], k_done[g] = dq.made(), dk.made()

    @block.tensor
    def _(pe):
        pe.wait_ge(*cp.made())
        for h in range(H):
            out = k.ps_acc[:, h // 2, (h % 2) * S:(h % 2 + 1) * S]
            pe.matmul(out, v[:, 0, h * P:(h + 1) * P], at0[:, h, :], start=(h % 2 == 0), stop=True, skip_group_check=True)
            mm = pe.matmul(out[:, P:S], v[:, 1, h * P:(h + 1) * P], at1[:, h, :], start=False, stop=True,
                           skip_group_check=True)
            if h % 2:
                mm.then_inc(*up("heads_ready"))
        pe.wait_ge(*k.gu_read[0])
        pe.wait_ge(*k.gu_read[1])
    bank_of = lambda t: lambda j: t[:, j * 2 * S:(j + 1) * 2 * S]
    head_norm(k, [k.ps_acc[:, j, :] for j in range(4)], [k("heads_ready").made(3 - j) for j in range(4)],
              [k.ps_gu[0][:, :], k.ps_gu[1][:, :]], bank_of(q), bank_of(kk), g_norm, bank_of(gate), 0, P,
              meanwhile=last_gates)
    k.gu_read = [made("head_sums_read")] * 2
    end_mixer(k)


def end_mixer(k):
    block, made, up = tools(k)

    @block.vector
    def _(dve):
        dve.wait_ge(*made("y_ready"))
        dve.wait_ge(*made("end_of_mixer"))
        dve.tensor_copy(k.tiny[:, 15:16], k.xn[:, 7, 0:1]).then_inc(*up("end_of_mixer"))
        dve.wait_ge(*made("end_of_mixer"))
        dve.tensor_copy(k.tiny[:, 14:15], k.xn[:, 7, 0:1]).then_inc(*up("acc_read"))


def mlstm(k, b_if, norm_g):
    block, made, up = tools(k)
    A = k.arena
    H, G = 4, 8
    CAP = 15.0
    q, kt = A("q", H * S), A("k", H * S)
    v = A("v", 2 * D).rearrange("p (k c) -> p k c", k=2)
    gate = A("gate", KD * S)
    rows = A("rows", 2 * G * P)
    r, mrow, em, den = (A(n, H * S) for n in ("r", "mrow", "em", "den"))
    w0, s0 = A("w0", H * S), A("s0", H * S)
    w1, s1 = A("w1", H * P), A("s1", H * P)
    m = lambda t, h: t[:, h * S:(h + 1) * S]
    mp = lambda t, h: t[:, h * P:(h + 1) * P]
    copy = lambda t, h: lambda act, ps: act.activation(m(t, h), ps[:, 0:S], ACT.Copy)

    @block.scalar
    def _(act):
        act.wait_ge(*made("y_ready"))
        act.wait_ge(*made("acc_read"))
    gates = A("gates", 112).rearrange("p (n c) -> p n c", c=8)
    raw = gates[:, 0:2, :].rearrange("p t c -> p (t c)")
    project(k, [("mul", True, 8, gates[:, 0:2, :])] + [("mul", False, P, m(q, h)) for h in range(H)],
            k.xn_hi, k.xn_lo, first=xn_parts(k), with_rstd=True)

    c8 = lambda n: gates[:, n, :]
    view = lambda t: t.rearrange("p (t h) -> p t h", t=2)
    fg, low, lsm, nlf, ig, rc, nb = (c8(n) for n in range(3, 10))

    @block.vector
    def _(dve):
        dve.wait_ge(*made("product_read_dve"))
        dve.tensor_tensor(gates[:, 0:2, :], gates[:, 0:2, :], b_if.unsqueeze(1).to_broadcast([P, 2, 8]), ALU.add)\
           .then_inc(*up("gate_step"))

    @block.scalar
    def _(act):
        act.wait_ge(*made("gate_step"))
        act.activation(raw, raw, ACT.Tanh, scale=1.0 / CAP).then_inc(*up("gate_exp"))

    @block.vector
    def _(dve):
        dve.wait_ge(*made("gate_exp"))
        dve.tensor_scalar(view(ig), gates[:, 0:2, 0:4], CAP, None, ALU.mult)
        dve.tensor_scalar(view(fg), gates[:, 0:2, 4:8], CAP, None, ALU.mult)
        dve.tensor_scalar(view(low), gates[:, 0:2, 4:8], -CAP, None, ALU.mult).then_inc(*up("gate_step"))
        dve.wait_ge(*made("gate_step"))
        dve.tensor_tensor(low, fg, low, ALU.min).then_inc(*up("gate_step"))

    @block.scalar
    def _(act):
        act.wait_ge(*made("gate_step"))
        act.activation(lsm, low, ACT.Exp).then_inc(*up("gate_exp"))
        act.wait_ge(*made("gate_exp"))
        act.activation(lsm, lsm, ACT.Ln, bias=1.0).then_inc(*up("gate_exp"))

    @block.vector
    def _(dve):
        dve.wait_ge(*made("gate_exp"))
        dve.tensor_scalar(low, fg, 0.0, None, ALU.min).then_inc(*up("gate_step"))
        dve.wait_ge(*made("gate_step"))
        dve.tensor_tensor(nlf, lsm, low, ALU.subtract).then_inc(*up("gate_step"))
        dve.wait_ge(*made("gate_step"))
        four = lambda t: t.rearrange("p (n c) -> p n c", n=G)
        dve.tensor_copy(four(rows[:, 0:G * P]), ig.unsqueeze(2).to_broadcast([P, G, P]))
        dve.tensor_copy(four(rows[:, G * P:2 * G * P]), nlf.unsqueeze(2).to_broadcast([P, G, P]))\
           .then_inc(*up("gates_spread"))
    project(k, [("mul", False, P, m(kt, h)) for h in range(H)], k.xn_hi, k.xn_lo)
    rows_i, rows_f = rows[:, 0:G * P], rows[:, G * P:2 * G * P]
    upper, ident = con(k, "upper"), con(k, "ident")

    @block.tensor
    def _(pe):
        pe.wait_ge(*made("gates_spread"))
        pe.wait_ge(*made("x_ready"))
        pe.wait_ge(*made("acc_read"))
        pe.wait_ge(*made("misc_free"))
        for h in range(H):
            for base, with_i in ((2, False), (0, True)):
                out = k.ps_acc[:, base + h // 2, (h % 2) * S:(h % 2 + 1) * S]
                pe.matmul(out[:, 0:P], mp(rows_f, h), upper, start=(h % 2 == 0), stop=True, skip_group_check=True)
                pe.matmul(out[:, P:S], mp(rows_f, 4 + h), upper, start=False, stop=True, skip_group_check=True)
                pe.matmul(out[:, P:S], mp(rows_f, h), k.ones[:, :], start=False, stop=True, skip_group_check=True)
                if with_i:
                    for tt in range(2):
                        pe.matmul(out[:, tt * P:(tt + 1) * P], mp(rows_i, 4 * tt + h), ident, start=False, stop=True,
                                  skip_group_check=True)
        pe.matmul(k.ps_misc[:, 0:8], upper, nlf, start=True, stop=True, skip_group_check=True)
        pe.matmul(k.ps_misc[:, 4:8], k.ones[:, :], nlf[:, 0:4], start=False, stop=True, skip_group_check=True)\
          .then_inc(*up("gate_rows_ready"))

    @block.scalar
    def _(act):
        act.wait_ge(*made("gate_rows_ready"))
        act.activation(r, k.ps_acc[:, 0:2, :].rearrange("p j c -> p (j c)"), ACT.Copy).then_inc(*up("r_ready"))

    @block.vector
    def _(dve):
        dve.wait_ge(*made("gate_rows_ready"))
        dve.tensor_tensor(rc, k.ps_misc[:, 0:8], ig, ALU.add).then_inc(*up("misc_free"))
        dve.wait_ge(*made("r_ready"))
        for h in range(H):
            ins = dve.tensor_tensor_scan(m(mrow, h), m(r, h), m(r, h), 0.0, ALU.max, ALU.max)
        ins.then_inc(*up("M_ready"))
        dve.wait_ge(*made("M_ready"))
        dve.wait_ge(*made("misc_free"))
        dve.tensor_tensor(em, k.ps_acc[:, 2:4, :].rearrange("p j c -> p (j c)"), mrow, ALU.subtract).then_inc(*up("acc_read"))
        for h in range(H):
            dve.tensor_scalar(m(w0, h), m(mrow, h), rc[:, h:h + 1], 0.0, ALU.subtract, ALU.max)
            ins = dve.tensor_scalar(mp(w1, h), m(mrow, h)[:, P:S], rc[:, 4 + h:5 + h], 0.0, ALU.subtract, ALU.max)
        ins.then_inc(*up("decay_args"))

    @block.scalar
    def _(act):
        act.wait_ge(*made("decay_args"))
        act.activation(w0, w0, ACT.Exp, scale=-1.0)
        act.activation(w1, w1, ACT.Exp, scale=-1.0)
        act.activation(em, em, ACT.Exp).then_inc(*up("decay_exp"))

    @block.vector
    def _(dve):
        dve.wait_ge(*made("decay_exp"))
        diag0 = w0.rearrange("p (h t) -> p h t", h=H)[:, :, 0:P]
        diag1 = w1.rearrange("p (h t) -> p h t", h=H)
        for d in (diag0, diag1):
            ins = dve.tensor_tensor(d, d, upper.unsqueeze(1).to_broadcast([P, H, P]), ALU.mult)
        ins.then_inc(*up("decay_ready"))
    project_rows(k, v, D, True)
    project(k, [("act", False, P, (lambda h: lambda act, ps: act.activation(m(gate, h), ps[:, 0:S], ACT.Sigmoid))(h))
                for h in range(KD - 4)], k.xn_hi, k.xn_lo)

    @block.tensor
    def _(pe):
        pe.wait_ge(*made("acc_read"))
        pe.wait_ge(*made("product_read_dve"))
        for h in range(H):
            pe.matmul(k.ps_acc[:, h // 2, (h % 2) * S:(h % 2 + 1) * S], m(kt, h)[:, 0:P], m(q, h),
                      start=(h % 2 == 0), stop=True, skip_group_check=True)
        for h in range(H):
            mm = pe.matmul(k.ps_acc[:, 2, h * P:(h + 1) * P], m(kt, h)[:, P:S], m(q, h)[:, P:S],
                           start=(h == 0), stop=True, skip_group_check=True)
        mm.then_inc(*up("scores_ready"))

    @block.vector
    def _(dve):
        dve.wait_ge(*made("scores_ready"))
        dve.wait_ge(*made("decay_ready"))
        dve.scalar_tensor_tensor(out=s0, in0=k.ps_acc[:, 0:2, :].rearrange("p j c -> p (j c)"), scalar=128.0 ** -0.5,
                                 in1=w0, op0=ALU.mult, op1=ALU.mult)
        dve.scalar_tensor_tensor(out=s1, in0=k.ps_acc[:, 2, :], scalar=128.0 ** -0.5, in1=w1, op0=ALU.mult, op1=ALU.mult)\
           .then_inc(*up("weights_ready"))

    @block.tensor
    def _(pe):
        pe.wait_ge(*made("weights_ready"))
        pe.wait_ge(*k.gu_read[0])
        pe.wait_ge(*k.gu_read[1])
        for h in range(H):
            out = k.ps_gu[h // 2][:, (h % 2) * S:(h % 2 + 1) * S]
            pe.matmul(out, k.ones[:, :], m(s0, h), start=(h % 2 == 0), stop=True, skip_group_check=True)
            mm = pe.matmul(out[:, P:S], k.ones[:, :], mp(s1, h), start=False, stop=True, skip_group_check=True)
        mm.then_inc(*up("den_ready"))
        for j in range(KD):
            out = k.ps_acc[:, j // 2, (j % 2) * S:(j % 2 + 1) * S]
            pe.matmul(out, v[:, 0, j * P:(j + 1) * P], m(s0, j // 2), start=(j % 2 == 0), stop=True, skip_group_check=True)
            mm = pe.matmul(out[:, P:S], v[:, 1, j * P:(j + 1) * P], mp(s1, j // 2), start=False, stop=True,
                           skip_group_check=True)
        mm.then_inc(*up("heads_ready"))

    @block.scalar
    def _(act):
        act.wait_ge(*made("den_ready"))
        for j in range(2):
            act.activation(den[:, j * 2 * S:(j + 1) * 2 * S], k.ps_gu[j][:, :], ACT.Abs).then_inc(*up("den_abs"))
        act.wait_ge(*made("heads_ready"))
        act.activation(rows, k.ps_acc[:, :, :].rearrange("p j c -> p (j c)"), ACT.Square).then_inc(*up("square_ready"))

    @block.vector
    def _(dve):
        dve.wait_ge(*made("den_abs"))
        dve.tensor_tensor(den, den, em, ALU.max).then_inc(*up("den_step"))
        dve.wait_ge(*made("den_step"))
        dve.scalar_tensor_tensor(out=den, in0=den, scalar=EPS, in1=den, op0=ALU.mult, op1=ALU.mult).then_inc(*up("den_step"))

    @block.tensor
    def _(pe):
        pe.wait_ge(*made("square_ready"))
        pe.wait_ge(*made("den_abs"))
        for h in range(H):
            for j in range(2):
                mm = pe.matmul(k.ps_gu[h // 2][:, (h % 2) * S:(h % 2 + 1) * S], k.ones[:, :], m(rows, 2 * h + j),
                               start=(h % 2 == 0 and j == 0), stop=(j == 1), skip_group_check=True)
        mm.then_inc(*up("sum_sq_ready"))

    @block.vector
    def _(dve):
        dve.wait_ge(*made("sum_sq_ready"))
        dve.wait_ge(*made("den_step"))
        for j in range(2):
            dve.scalar_tensor_tensor(out=den[:, j * 2 * S:(j + 1) * 2 * S], in0=k.ps_gu[j][:, :], scalar=1.0 / 256,
                                     in1=den[:, j * 2 * S:(j + 1) * 2 * S], op0=ALU.mult, op1=ALU.add)\
               .then_inc(*up("head_sums_read"))
    k.gu_read = [made("head_sums_read")] * 2

    @block.scalar
    def _(act):
        act.wait_ge(*made("head_sums_read"))
        act.activation(den, den, ACT.Ln).then_inc(*up("rs_step"))
        act.wait_ge(*made("rs_step"))
        act.activation(den, den, ACT.Exp, scale=-0.5).then_inc(*up("rs_step"))
    normed = made("rs_step")

    project(k, [("mul", False, P, m(gate, h)) for h in range(KD - 4, KD)], k.xn_hi, k.xn_lo, side=True)

    @block.scalar
    def _(act):
        act.wait_ge(*made("product_read_dve"))
        last = gate[:, (KD - 4) * S:KD * S]
        act.activation(last, last, ACT.Sigmoid).then_inc(*up("gate_ready"))

    @block.vector
    def _(dve):
        dve.wait_ge(*made("rs_step"))
        for j in range(KD):
            dve.scalar_tensor_tensor(out=k.xn[:, j, :], in0=k.ps_acc[:, j // 2, (j % 2) * S:(j % 2 + 1) * S],
                                     scalar=norm_g[:, j:j + 1], in1=m(den, j // 2), op0=ALU.mult, op1=ALU.mult)\
               .then_inc(*up("norm_step"))
            if j % 2:
                dve.wait_ge(*made("norm_step"))
                if j == 5:
                    dve.wait_ge(*made("gate_ready"))
                pair = k.xn[:, j - 1:j + 1, :].rearrange("p m t -> p (m t)")
                dve.tensor_tensor(pair, pair, gate[:, (j - 1) * S:(j + 1) * S], ALU.mult).then_inc(*up("y_ready"))
                k.y_at[j // 2] = made("y_ready")
    end_mixer(k)


def swa(k, gains, sinks):
    block, made, up = tools(k)
    A = k.arena
    q = A("q", 10 * S).rearrange("p (m t) -> p m t", m=10)
    sq = A("sq", 10 * S).rearrange("p (m t) -> p m t", m=10)
    rs = A("rs", 10 * S).rearrange("p (m t) -> p m t", m=10)
    kz = A("kz", 4 * S).rearrange("p (h t) -> p h t", h=4)
    v = A("v", 2 * S).rearrange("p (k c) -> p k c", k=2)

    @block.gpsimd
    def _(pool):
        pool.wait_ge(*made("y_ready"))
        pool.wait_ge(*made("acc_read"))
        pool.memset(kz, 0.0).then_inc(*up("kz_zero"))

    @block.scalar
    def _(act):
        act.wait_ge(*made("y_ready"))
        act.wait_ge(*made("acc_read"))
    project(k, [("mul", False, P, q[:, m, :]) for m in range(10)], k.xn_hi, k.xn_lo, first=xn_parts(k), with_rstd=True)

    @block.scalar
    def _(act):
        act.wait_ge(*made("product_read_dve"))
        act.activation(sq, q, ACT.Square).then_inc(*up("square_ready"))
    sums = lambda m: (k.ps_acc[:, m // 2, :] if m < 8 else k.ps_misc[:, :])[:, (m % 2) * S:(m % 2 + 1) * S]

    @block.tensor
    def _(pe):
        pe.wait_ge(*made("square_ready"))
        pe.wait_ge(*made("acc_read"))
        pe.wait_ge(*made("x_ready"))
        pe.wait_ge(*made("misc_free"))
        for m in range(10):
            mm = pe.matmul(sums(m), con(k, "halves"), sq[:, m, :], start=(m % 2 == 0), stop=True, skip_group_check=True)
        mm.then_inc(*up("sum_sq_ready"))

    @block.vector
    def _(dve):
        dve.wait_ge(*made("sum_sq_ready"))
        dve.tensor_scalar(rs[:, 0:8, :].rearrange("p m t -> p (m t)"), k.ps_acc[:, :, :].rearrange("p j c -> p (j c)"),
                          1.0 / 64, EPS, ALU.mult, ALU.add).then_inc(*up("acc_read"))
        dve.tensor_scalar(rs[:, 8:10, :].rearrange("p m t -> p (m t)"), k.ps_misc[:, :], 64 * EPS, None, ALU.add)\
           .then_inc(*up("misc_free"))

    @block.scalar
    def _(act):
        act.wait_ge(*made("misc_free"))
        act.activation(rs, rs, ACT.Ln).then_inc(*up("rs_step"))
        act.wait_ge(*made("rs_step"))
        act.activation(rs, rs, ACT.Exp, scale=-0.5).then_inc(*up("rs_step"))
    project_rows(k, v, S, False)

    @block.vector
    def _(dve):
        dve.wait_ge(*made("rs_step"))
        dve.wait_ge(*made("kz_zero"))
        for h in range(4):
            b = slice(64 * (h % 2), 64 * (h % 2) + 64)
            dve.scalar_tensor_tensor(out=kz[b, h, :], in0=q[b, 8 + h // 2, :], scalar=gains[b, 1:2],
                                     in1=rs[b, 8 + h // 2, :], op0=ALU.mult, op1=ALU.mult)
        dve.scalar_tensor_tensor(out=q[:, 0:8, :], in0=q[:, 0:8, :], scalar=gains[:, 0:1], in1=rs[:, 0:8, :],
                                 op0=ALU.mult, op1=ALU.mult).then_inc(*up("att_operands"))

    def group(g):
        key = lambda h: 2 * (g // 2) + h % 2
        name = [HEADS_SWA[4 * g + h] for h in range(4)]
        return Attention(k, g, lambda h, tq: q[:, 2 * g + h // 2, tq * P:(tq + 1) * P], lambda h, K: kz[:, key(h), 0:K],
                         lambda kt, h: v[:, kt, key(h) * 64:(key(h) + 1) * 64], 1.0,
                         lambda tq: con(k, "distance", P if tq == 0 else 0), None, 2 * g,
                         slopes=[-2.0 ** (-8.0 * (n + 1) / 16) for n in name], sink=sinks[:, 4 * g:4 * g + 4])

    groups = [group(g) for g in range(4)]
    groups[0].scores()
    groups[0].weights()
    for g in range(4):
        if g < 3:
            groups[g + 1].scores()
            groups[g + 1].weights()
        groups[g].values()
    end_mixer(k)


HEADS_SWA = [4 * (2 * (j // 4) + half) + j % 4 for j in range(8) for half in range(2)]


def ffn_chunks(w_gu, w_down):
    g, u, d = as_columns(w_gu[:, :FF]), as_columns(w_gu[:, FF:]), as_rows(w_down)
    out = []
    for t in range(FT):
        out += [g[t], u[t]] + ([d[t - 1]] if t else [])
    return [np.stack(out + [d[FT - 1]])]


def ple_chunks(w_gate, w_proj):
    gate = as_columns(w_gate)
    return [gate[0:2], as_rows(w_proj), gate[2:]]


def hgrn_chunks(w_in, w_out):
    return [as_columns(w_in[:, :2 * D]), as_wide(w_in[:, 2 * D:3 * D]), as_columns(w_in[:, 3 * D:]), as_columns(w_out)]


def mlstm_chunks(w_qkvo, w_if, w_out):
    gates = np.concatenate([w_if, np.zeros((D, P - w_if.shape[1]), w_if.dtype)], 1)
    return [as_columns(gates), as_columns(w_qkvo[:, :D]), as_wide(w_qkvo[:, D:2 * D]), as_columns(w_qkvo[:, 2 * D:]),
            as_columns(w_out)]


def swa_chunks(w_qkv, w_o):
    q = w_qkv[:, :1024].reshape(D, 16, 64)[:, HEADS_SWA, :].reshape(D, 1024)
    o = w_o.reshape(16, 64, D)[HEADS_SWA, :, :].reshape(1024, D)
    return [as_columns(np.concatenate([q, w_qkv[:, 1024:1280]], 1)), as_wide(w_qkv[:, 1280:]), as_columns(o)]


def last_output(k, out):
    @k.block.sync
    def _(sp):
        sp.wait_ge(*k("x_ready").made())
        sp.dma_start(out, k.x[:, :, :]).then_inc(*k("stored").up_dma())
        sp.wait_ge(*k("stored").made())


VEC_FIRST, VEC_SECOND = 68, 4 * KD
N_VEC = 2 * VEC_FIRST + KD + 4 * VEC_SECOND + 4 * KD + 2 + (8 + KD) + (2 + 16)


def build(nc, io, out, n_chunks):
    with ExitStack() as ctx:
        k = setup(nc, ctx, io, n_chunks, N_VEC, N_CONST_1)
        k.ident = con(k, "ident")
        start(k, io)
        at = [0]

        def vec(n):
            at[0] += n
            return k.vec[:, at[0] - n:at[0]]

        first_layer(k, vec(VEC_FIRST), lambda: t5_bias(k, io))
        first_layer(k, vec(VEC_FIRST))
        norm_to_x(k, vec(KD))
        load_p(k, io)
        gains = [vec(VEC_SECOND) for _ in range(4)]
        bounds, hg_norm, ml, sw = vec(4 * KD), vec(2), vec(8 + KD), vec(18)
        lower_bounds(k, bounds)
        for layer in range(4):
            gain = lambda n: gains[layer][:, n * KD:(n + 1) * KD]
            norm(k, gain(0))
            ffn(k)
            norm(k, gain(1))
            k.arena.clear()
            if layer % 3 == 0:
                j = layer // 3
                hgrn(k, hg_norm[:, j:j + 1], k.lb if layer else None)
            elif layer == 1:
                mlstm(k, ml[:, 0:8], ml[:, 8:8 + KD])
            else:
                swa(k, sw[:, 0:2], sw[:, 2:18])
            project_out(k)
            norm(k, gain(2))
            ffn(k)
            norm(k, gain(3))
            ple(k, layer)
        assert k.used == n_chunks
        last_output(k, out)


def kernel(x, norm_w, w_in, mla_q_norm, mla_w_uq, mla_kv_norm, mla_w_ukv, gdn_conv_w, gdn_A_log, gdn_dt_bias,
           gdn_norm_w, w_out, t5_table, final_norm_w, p_2, norm_gains_2, w_ffn_gu_2, w_ffn_down_2, w_ple_gate_2,
           w_ple_proj_2, hg_lower_bounds_2, hg_w_in_2, hg_g_norm_2, hg_w_out_2, ml_w_qkvo_2, ml_w_if_2, ml_b_if_2,
           ml_norm_2, ml_w_out_2, sw_w_qkv_2, sw_q_norm_2, sw_k_norm_2, sw_sinks_2, sw_w_o_2):
    import concourse.bacc as _bacc
    from concourse.bass_utils import run_bass_kernel_spmd as _run

    (x, norm_w, w_in, mla_q_norm, mla_w_uq, mla_kv_norm, mla_w_ukv, gdn_conv_w, gdn_A_log, gdn_dt_bias,
     gdn_norm_w, w_out, t5_table, final_norm_w, p_2, norm_gains_2, w_ffn_gu_2, w_ffn_down_2, w_ple_gate_2,
     w_ple_proj_2, hg_lower_bounds_2, hg_w_in_2, hg_g_norm_2, hg_w_out_2, ml_w_qkvo_2, ml_w_if_2, ml_b_if_2,
     ml_norm_2, ml_w_out_2, sw_w_qkv_2, sw_q_norm_2, sw_k_norm_2, sw_sinks_2, sw_w_o_2) = (np.asarray(a) for a in (
         x, norm_w, w_in, mla_q_norm, mla_w_uq, mla_kv_norm, mla_w_ukv, gdn_conv_w, gdn_A_log, gdn_dt_bias,
         gdn_norm_w, w_out, t5_table, final_norm_w, p_2, norm_gains_2, w_ffn_gu_2, w_ffn_down_2, w_ple_gate_2,
         w_ple_proj_2, hg_lower_bounds_2, hg_w_in_2, hg_g_norm_2, hg_w_out_2, ml_w_qkvo_2, ml_w_if_2, ml_b_if_2,
         ml_norm_2, ml_w_out_2, sw_w_qkv_2, sw_q_norm_2, sw_k_norm_2, sw_sinks_2, sw_w_o_2))

    chunks, vecs = [], []
    for n in range(2):
        chunks += first_chunks(w_in[n], mla_w_uq[n], mla_w_ukv[n], w_out[n])
        vecs += first_vectors(norm_w[n], mla_q_norm[n], mla_kv_norm[n], gdn_conv_w[n], gdn_A_log[n], gdn_dt_bias[n],
                              gdn_norm_w[n])
    vecs += [columns(final_norm_w)]
    for n in range(4):
        chunks += ffn_chunks(w_ffn_gu_2[n, 0], w_ffn_down_2[n, 0])
        chunks += (hgrn_chunks(hg_w_in_2[n // 3], hg_w_out_2[n // 3]) if n % 3 == 0 else
                   mlstm_chunks(ml_w_qkvo_2[0], ml_w_if_2[0], ml_w_out_2[0]) if n == 1 else
                   swa_chunks(sw_w_qkv_2[0], sw_w_o_2[0]))
        chunks += ffn_chunks(w_ffn_gu_2[n, 1], w_ffn_down_2[n, 1])
        chunks += ple_chunks(w_ple_gate_2[n], w_ple_proj_2[n])
        vecs += [columns(norm_gains_2[n, i]) for i in range(4)]
    twice = lambda v: np.concatenate([v, v]).reshape(P, 1)
    vecs += [columns(hg_lower_bounds_2[n]) for n in range(4)] + [columns(hg_g_norm_2[n]) for n in range(2)]
    vecs += [spread(ml_b_if_2[0]), columns(ml_norm_2[0])]
    vecs += [twice(sw_q_norm_2[0]), twice(sw_k_norm_2[0]), spread(sw_sinks_2[0][HEADS_SWA])]

    arrays = {
        "w": np.concatenate(chunks),
        "x": np.ascontiguousarray(x[0].T.reshape(KD, P, S).transpose(1, 0, 2)),
        "vec": np.ascontiguousarray(np.concatenate(vecs, 1)),
        "p": np.ascontiguousarray(p_2[:, 0].transpose(0, 2, 1).reshape(4, 2, P, S).transpose(2, 0, 1, 3)),
        "const": constants(),
        "t5": np.ascontiguousarray(t5_table),
    }
    nc = _bacc.Bacc("TRN2", target_bir_lowering=False, num_devices=1)
    io = {n: nc.dram_tensor(f"in_{n}_dram", a.shape, mybir.dt.from_np(a.dtype), kind="ExternalInput").ap()
          for n, a in arrays.items()}
    io["scratch"] = nc.dram_tensor("distance_rows", [4, P, 2 * S], F32, kind="Internal").ap()
    out = nc.dram_tensor("out_0_dram", [P, KD, S], F32, kind="ExternalOutput").ap()
    build(nc, io, out, arrays["w"].shape[0])
    r = _run(nc, [{f"in_{n}_dram": a for n, a in arrays.items()}], core_ids=[0])
    y = r.results[0]["out_0_dram"]
    return np.ascontiguousarray(y.transpose(2, 1, 0)).reshape(1, S, D)
```
